# Optimizing a Trainium2 kernel written in Bass

```python
import jax, jax.numpy as jnp
from jax import lax
import numpy as np
import jax
import jax.numpy as jnp

D_MODEL = 1024
BATCH = 1
SEQ = 256
DEPTH = 1

ATTN_HEADS = 8
ATTN_HD = 64
ATTN_WIDTH = ATTN_HEADS * ATTN_HD
DILATED_PATTERNS = ((128, 1), (512, 4), (2048, 16))
ATTN_BLOCK = 128
DN_HEADS = 4
DN_KD = 128
DN_VD = 128
DN_QK_WIDTH = DN_HEADS * DN_KD
DN_V_WIDTH = DN_HEADS * DN_VD
DN_CONV_DIM = 2 * DN_QK_WIDTH + DN_V_WIDTH
CONV_K = 4
DN_CHUNK = 64
D_MIX = ATTN_WIDTH + DN_V_WIDTH
IN_SPLITS = (ATTN_WIDTH, 2 * ATTN_WIDTH, 3 * ATTN_WIDTH,
             3 * ATTN_WIDTH + DN_CONV_DIM,
             3 * ATTN_WIDTH + DN_CONV_DIM + DN_V_WIDTH,
             3 * ATTN_WIDTH + DN_CONV_DIM + DN_V_WIDTH + DN_HEADS)
IN_COLS = 3 * ATTN_WIDTH + DN_CONV_DIM + DN_V_WIDTH + 2 * DN_HEADS
N_EXPERTS = 32
TOP_K = 4
D_EXPERT = 1024
SWIGLU_LIMIT = 7.0
SWIGLU_ALPHA = 1.702
MOE_BLOCK = 128
NORM_EPS = 1e-6


def rms_norm(x, w):
    xf = x.astype(jnp.float32)
    y = xf * lax.rsqrt(jnp.mean(xf * xf, axis=-1, keepdims=True) + NORM_EPS)
    return (y * w.astype(jnp.float32)).astype(x.dtype)

def l2_norm(x):
    return x * lax.rsqrt(jnp.sum(x * x, axis=-1, keepdims=True) + NORM_EPS)

def modulate(x, w, shift, scale):
    return rms_norm(x, w) * (1 + scale[:, None, :]) + shift[:, None, :]

def dilated_branch(q, k, v, window, dilation):
    B, S, H, Dh = q.shape
    L = S // dilation
    span = window // dilation
    nb = -(-L // ATTN_BLOCK)
    Lp = nb * ATTN_BLOCK

    def to_sub(t):
        t = t.astype(jnp.float32).reshape(B, L, dilation, H, Dh).transpose(0, 2, 3, 1, 4)
        return jnp.pad(t, ((0, 0), (0, 0), (0, 0), (0, Lp - L), (0, 0)))

    def window_blocks(t):
        t = jnp.pad(t, ((0, 0), (0, 0), (0, 0), (ATTN_BLOCK, 0), (0, 0)))
        t = t.reshape(B, dilation, H, nb + 1, ATTN_BLOCK, Dh)
        return jnp.concatenate([t[:, :, :, :-1], t[:, :, :, 1:]], axis=-2)

    qb = to_sub(q).reshape(B, dilation, H, nb, ATTN_BLOCK, Dh)
    kw = window_blocks(to_sub(k))
    vw = window_blocks(to_sub(v))
    s = jnp.einsum('bdhnqe,bdhnke->bdhnqk', qb, kw) * (ATTN_HD ** -0.5)
    dist = (jnp.arange(ATTN_BLOCK)[:, None] + ATTN_BLOCK) - jnp.arange(2 * ATTN_BLOCK)[None, :]
    band = (dist >= 0) & (dist <= span)
    kpos = jnp.arange(nb)[:, None] * ATTN_BLOCK - ATTN_BLOCK + jnp.arange(2 * ATTN_BLOCK)[None, :]
    mask = band[None, :, :] & (kpos >= 0)[:, None, :]
    s = jnp.where(mask, s, -jnp.inf)
    m = jnp.max(s, axis=-1, keepdims=True)
    p = jnp.exp(s - m)
    den = jnp.sum(p, axis=-1)
    o = jnp.einsum('bdhnqk,bdhnke->bdhnqe', p, vw) / den[..., None]
    lse = m[..., 0] + jnp.log(den)
    o = o.reshape(B, dilation, H, Lp, Dh)[:, :, :, :L].transpose(0, 3, 1, 2, 4).reshape(B, S, H, Dh)
    lse = lse.reshape(B, dilation, H, Lp)[:, :, :, :L].transpose(0, 3, 1, 2).reshape(B, S, H)
    return o, lse

def dilated_attention(q, k, v):
    outs, lses = [], []
    for window, dilation in DILATED_PATTERNS:
        o, lse = dilated_branch(q, k, v, window, dilation)
        outs.append(o)
        lses.append(lse)
    wts = jax.nn.softmax(jnp.stack(lses, axis=0), axis=0)
    return jnp.einsum('gbsh,gbshe->bshe', wts, jnp.stack(outs, axis=0))

def causal_short_conv(x, w):
    S = x.shape[1]
    xp = jnp.pad(x, ((0, 0), (CONV_K - 1, 0), (0, 0)))
    y = w[CONV_K - 1] * x
    for j in range(CONV_K - 1):
        y = y + w[j] * xp[:, j:j + S]
    return y

def gated_delta_rule(q, k, v, g, beta):
    B, S, H, Dk = q.shape
    Dv = v.shape[-1]
    C = DN_CHUNK
    N = S // C
    q = l2_norm(q) * (Dk ** -0.5)
    k = l2_norm(k)

    def chunk(t):
        return jnp.swapaxes(t.reshape((B, N, C, H) + t.shape[3:]), 2, 3)

    qc, kc, vc, gc, bc = chunk(q), chunk(k), chunk(v), chunk(g), chunk(beta)
    gc = jnp.cumsum(gc, axis=-1)
    tril = jnp.tril(jnp.ones((C, C), dtype=bool))
    strict = jnp.tril(jnp.ones((C, C), dtype=bool), -1)
    decay = jnp.exp(jnp.where(tril, gc[..., :, None] - gc[..., None, :], -jnp.inf))
    kb = kc * bc[..., None]
    vb = vc * bc[..., None]
    a_low = jnp.where(strict, jnp.einsum('bnhie,bnhje->bnhij', kb, kc) * decay, 0.0)
    lhs = a_low + jnp.eye(C, dtype=jnp.float32)
    u = lax.linalg.triangular_solve(lhs, vb, left_side=True, lower=True)
    w = lax.linalg.triangular_solve(lhs, kb * jnp.exp(gc)[..., None], left_side=True, lower=True)
    intra = jnp.einsum('bnhie,bnhje->bnhij', qc, kc) * decay
    q_dec = qc * jnp.exp(gc)[..., None]
    k_dec = kc * jnp.exp(gc[..., -1:] - gc)[..., None]
    g_last = jnp.exp(gc[..., -1])

    def step(state, xs):
        qd, kd, u_i, w_i, intra_i, gl = xs
        v_new = u_i - jnp.einsum('bhce,bhef->bhcf', w_i, state)
        o = jnp.einsum('bhce,bhef->bhcf', qd, state) + jnp.einsum('bhij,bhjf->bhif', intra_i, v_new)
        state = state * gl[..., None, None] + jnp.einsum('bhce,bhcf->bhef', kd, v_new)
        return state, o

    xs = tuple(jnp.moveaxis(t, 1, 0) for t in (q_dec, k_dec, u, w, intra, g_last))
    state0 = jnp.zeros((B, H, Dk, Dv), jnp.float32)
    _, o = lax.scan(step, state0, xs)
    return o.transpose(1, 0, 3, 2, 4).reshape(B, S, H, Dv)

def hybrid_mixer(h, w_in, conv_w, A_log, dt_bias, dn_norm_w, w_out):
    B, S, _ = h.shape
    proj = h @ w_in
    aq, ak, av, dqkv, dz, db, da = jnp.split(proj, IN_SPLITS, axis=-1)
    shp_a = (B, S, ATTN_HEADS, ATTN_HD)
    attn_out = dilated_attention(aq.reshape(shp_a), ak.reshape(shp_a), av.reshape(shp_a))
    attn_out = attn_out.reshape(B, S, ATTN_WIDTH).astype(h.dtype)
    dqkv = jax.nn.silu(causal_short_conv(dqkv, conv_w)).astype(jnp.float32)
    dq, dk, dv = jnp.split(dqkv, (DN_QK_WIDTH, 2 * DN_QK_WIDTH), axis=-1)
    g = -jnp.exp(A_log.astype(jnp.float32)) * jax.nn.softplus(da.astype(jnp.float32) + dt_bias.astype(jnp.float32))
    beta = jax.nn.sigmoid(db.astype(jnp.float32))
    o = gated_delta_rule(dq.reshape(B, S, DN_HEADS, DN_KD), dk.reshape(B, S, DN_HEADS, DN_KD),
                         dv.reshape(B, S, DN_HEADS, DN_VD), g, beta)
    o = rms_norm(o, dn_norm_w) * jax.nn.silu(dz.astype(jnp.float32).reshape(B, S, DN_HEADS, DN_VD))
    dn_out = o.reshape(B, S, DN_V_WIDTH).astype(h.dtype)
    return jnp.concatenate([attn_out, dn_out], axis=-1) @ w_out

def clamped_swiglu(hgu):
    gate, up = jnp.split(hgu, 2, axis=-1)
    gate = jnp.minimum(gate, SWIGLU_LIMIT)
    up = jnp.clip(up, -SWIGLU_LIMIT, SWIGLU_LIMIT)
    return gate * jax.nn.sigmoid(SWIGLU_ALPHA * gate) * (up + 1)

def routed_moe(h, w_router, b_router, w1, b1, w2, b2):
    B, S, D = h.shape
    T = B * S
    xt = h.reshape(T, D)
    logits = (xt @ w_router + b_router).astype(jnp.float32)
    top_v, top_e = lax.top_k(logits, TOP_K)
    gates = jax.nn.softmax(top_v, axis=-1)
    A = T * TOP_K
    e_flat = top_e.reshape(A)
    tok_flat = jnp.repeat(jnp.arange(T, dtype=jnp.int32), TOP_K)
    g_flat = gates.reshape(A)
    order = jnp.argsort(e_flat)
    se, stok, sg = e_flat[order], tok_flat[order], g_flat[order]
    counts = jnp.zeros((N_EXPERTS,), jnp.int32).at[e_flat].add(1)
    padded = (counts + MOE_BLOCK - 1) // MOE_BLOCK * MOE_BLOCK
    pend = jnp.cumsum(padded)
    pstart = pend - padded
    cstart = jnp.cumsum(counts) - counts
    dest = pstart[se] + (jnp.arange(A, dtype=jnp.int32) - cstart[se])
    P = A + N_EXPERTS * MOE_BLOCK
    NB = P // MOE_BLOCK
    row_tok = jnp.zeros((P,), jnp.int32).at[dest].set(stok)
    row_gate = jnp.zeros((P,), jnp.float32).at[dest].set(sg)
    block_exp = jnp.minimum(jnp.searchsorted(pend, jnp.arange(NB) * MOE_BLOCK, side='right'),
                            N_EXPERTS - 1).astype(jnp.int32)
    xs = xt[row_tok].reshape(NB, MOE_BLOCK, D)

    def expert_block(args):
        xb, e = args
        return clamped_swiglu(xb @ w1[e] + b1[e]) @ w2[e] + b2[e]

    yb = lax.map(expert_block, (xs, block_exp)).reshape(P, D)
    y = jnp.zeros((T, D), h.dtype).at[row_tok].add(yb * row_gate[:, None].astype(yb.dtype))
    return y.reshape(B, S, D)

def first_inputs(seed: int = 0) -> dict:
    key = jax.random.key(seed)
    ks = jax.random.split(key, 20)
    D, L, E, F = D_MODEL, DEPTH, N_EXPERTS, D_EXPERT
    nrm = jax.random.normal
    return {
        'x': nrm(ks[0], (BATCH, SEQ, D), jnp.float32),
        'c': nrm(ks[1], (BATCH, D), jnp.float32),
        'w_ada': nrm(ks[2], (L, D, 6 * D), jnp.float32) * (0.5 * D ** -0.5),
        'b_ada': nrm(ks[3], (L, 6 * D), jnp.float32) * 0.02,
        'norm1_w': 1.0 + 0.05 * nrm(ks[4], (L, D), jnp.float32),
        'w_in': nrm(ks[5], (L, D, IN_COLS), jnp.float32) * (D ** -0.5),
        'conv_w': nrm(ks[6], (L, CONV_K, DN_CONV_DIM), jnp.float32) * 0.5,
        'A_log': jnp.log(jax.random.uniform(ks[7], (L, DN_HEADS), jnp.float32, 1.0, 16.0)),
        'dt_bias': jax.random.uniform(ks[8], (L, DN_HEADS), jnp.float32, -4.5, -2.5),
        'dn_norm_w': 1.0 + 0.05 * nrm(ks[9], (L, DN_VD), jnp.float32),
        'w_out': nrm(ks[10], (L, D_MIX, D), jnp.float32) * (D_MIX ** -0.5),
        'norm2_w': 1.0 + 0.05 * nrm(ks[11], (L, D), jnp.float32),
        'w_router': nrm(ks[12], (L, D, E), jnp.float32) * (D ** -0.5),
        'b_router': nrm(ks[13], (L, E), jnp.float32) * 0.01,
        'w1': nrm(ks[14], (L, E, D, 2 * F), jnp.float32) * (D ** -0.5),
        'b1': nrm(ks[15], (L, E, 2 * F), jnp.float32) * 0.01,
        'w2': nrm(ks[16], (L, E, F, D), jnp.float32) * (F ** -0.5),
        'b2': nrm(ks[17], (L, E, D), jnp.float32) * 0.01,
        'final_norm_w': 1.0 + 0.05 * nrm(ks[18], (D,), jnp.float32),
    }

def first_block(x, c, w_ada, b_ada, norm1_w, w_in, conv_w, A_log, dt_bias, dn_norm_w, w_out,
              norm2_w, w_router, b_router, w1, b1, w2, b2, final_norm_w):
    cond = jax.nn.silu(c)
    for l in range(DEPTH):
        mod = cond @ w_ada[l] + b_ada[l]
        shift1, scale1, gate1, shift2, scale2, gate2 = jnp.split(mod, 6, axis=-1)
        h = modulate(x, norm1_w[l], shift1, scale1)
        x = x + gate1[:, None, :] * hybrid_mixer(h, w_in[l], conv_w[l], A_log[l], dt_bias[l],
                                                 dn_norm_w[l], w_out[l])
        h = modulate(x, norm2_w[l], shift2, scale2)
        x = x + gate2[:, None, :] * routed_moe(h, w_router[l], b_router[l], w1[l], b1[l], w2[l], b2[l])
    return rms_norm(x, final_norm_w)


DEPTH_2 = 2

GRID_W = 64
CTX_LEN = 256
N_MIXERS = 2
RET_HEADS = 4
RET_QK_DIM = D_MODEL // RET_HEADS
RET_V_DIM = 2 * D_MODEL // RET_HEADS
RET_CHUNK = 128
NAT_HEAD_DIM = 32
NAT_HEADS = D_MODEL // NAT_HEAD_DIM
NAT_WIN_ROWS = 8
NAT_WIN_COLS = 16
MLP_HIDDEN = 4 * D_MODEL
ROPE_BASE = 10000.0
LN_EPS = 1e-5
DN_ALPHA = (2.0 * DEPTH_2) ** 0.25
DN_BETA = (8.0 * DEPTH_2) ** -0.25
N_RET_LAYERS = (DEPTH_2 + 1) // 2
N_NAT_LAYERS = DEPTH_2 // 2


def layer_norm(x, g, b):
    xf = x.astype(jnp.float32)
    mu = jnp.mean(xf, axis=-1, keepdims=True)
    var = jnp.mean(jnp.square(xf - mu), axis=-1, keepdims=True)
    return ((xf - mu) * lax.rsqrt(var + LN_EPS) * g + b).astype(x.dtype)

def axial_rope_angles(n, axis_dim):
    t = jnp.arange(n)
    row = (t // GRID_W).astype(jnp.float32)
    col = (t % GRID_W).astype(jnp.float32)
    inv = 1.0 / (ROPE_BASE ** (jnp.arange(0, axis_dim, 2, dtype=jnp.float32) / axis_dim))
    return row[:, None] * inv, col[:, None] * inv

def rope_rotate(x, ang):
    cos = jnp.cos(ang).astype(x.dtype)
    sin = jnp.sin(ang).astype(x.dtype)
    x1, x2 = jnp.split(x, 2, axis=-1)
    return jnp.concatenate([x1 * cos - x2 * sin, x2 * cos + x1 * sin], axis=-1)

def axial_rope(x, ang_row, ang_col):
    xr, xc = jnp.split(x, 2, axis=-1)
    return jnp.concatenate([rope_rotate(xr, ang_row), rope_rotate(xc, ang_col)], axis=-1)

def retention_chunk_scan(q, k, v, log_gamma, state0, with_out):
    b, h, n, dk = q.shape
    dv = v.shape[-1]
    cs = RET_CHUNK
    nc = n // cs
    dt = v.dtype
    pos = jnp.arange(cs, dtype=jnp.float32)
    lg = log_gamma.astype(jnp.float32)[:, None]
    rel = pos[:, None] - pos[None, :]
    intra = jnp.where(rel >= 0, jnp.exp(lg[:, :, None] * jnp.maximum(rel, 0.0)), 0.0).astype(dt)
    q_dec = jnp.exp(lg * (pos + 1.0))[..., None].astype(dt)
    k_dec = jnp.exp(lg * (cs - 1.0 - pos))[..., None].astype(dt)
    chunk_dec = jnp.exp(lg * cs)[..., None].astype(dt)

    def to_chunks(t):
        return jnp.moveaxis(t.reshape(b, h, nc, cs, t.shape[-1]), 2, 0)

    def step(state, qkv):
        qc, kc, vc = qkv
        new_state = state * chunk_dec + jnp.einsum('bhsd,bhse->bhde', kc * k_dec, vc)
        if with_out:
            scores = jnp.einsum('bhcd,bhsd->bhcs', qc, kc) * intra
            out = (jnp.einsum('bhcs,bhse->bhce', scores, vc)
                   + jnp.einsum('bhcd,bhde->bhce', qc * q_dec, state))
            return new_state, out
        return new_state, None

    state, outs = lax.scan(step, state0, (to_chunks(q), to_chunks(k), to_chunks(v)))
    if with_out:
        outs = jnp.moveaxis(outs, 0, 2).reshape(b, h, n, dv)
    return state, outs

def retention_mixer(h_lat, h_ctx, w_in, w_o, decay_param, ang_row, ang_col, ctx_out):
    b = h_lat.shape[0]
    qk_w = RET_HEADS * RET_QK_DIM
    v_w = RET_HEADS * RET_V_DIM

    def heads(t, hd):
        return t.reshape(b, t.shape[1], RET_HEADS, hd).transpose(0, 2, 1, 3)

    def project(h, w):
        p = h @ w
        q = heads(p[..., :qk_w], RET_QK_DIM)
        k = heads(p[..., qk_w:2 * qk_w], RET_QK_DIM) * (RET_QK_DIM ** -0.5)
        v = heads(p[..., 2 * qk_w:2 * qk_w + v_w], RET_V_DIM)
        return q, k, v, p[..., 2 * qk_w + v_w:]

    def flip(t):
        return t[:, :, ::-1]

    def finish(o, g):
        of = o.astype(jnp.float32)
        mu = jnp.mean(of, axis=-1, keepdims=True)
        var = jnp.mean(jnp.square(of - mu), axis=-1, keepdims=True)
        on = ((of - mu) * lax.rsqrt(var + LN_EPS)).astype(o.dtype)
        on = on.transpose(0, 2, 1, 3).reshape(b, o.shape[2], v_w)
        return (on * jax.nn.silu(g)) @ w_o

    log_gamma = -jnp.exp(decay_param.astype(jnp.float32))
    w_ctx = w_in if ctx_out else w_in[:, :2 * qk_w + v_w]
    q_c, k_c, v_c, g_c = project(h_ctx, w_ctx)
    zeros = jnp.zeros((b, RET_HEADS, RET_QK_DIM, RET_V_DIM), v_c.dtype)
    s_f, o_cf = retention_chunk_scan(q_c, k_c, v_c, log_gamma[0], zeros, ctx_out)
    s_b, o_cb = retention_chunk_scan(flip(q_c), flip(k_c), flip(v_c), log_gamma[1], zeros, ctx_out)

    q_l, k_l, v_l, g_l = project(h_lat, w_in)
    q_l = axial_rope(q_l, ang_row, ang_col)
    k_l = axial_rope(k_l, ang_row, ang_col)
    _, o_lf = retention_chunk_scan(q_l, k_l, v_l, log_gamma[0], s_f, True)
    _, o_lb = retention_chunk_scan(flip(q_l), flip(k_l), flip(v_l), log_gamma[1], s_b, True)
    y_lat = finish(o_lf + flip(o_lb), g_l)
    y_ctx = finish(o_cf + flip(o_cb), g_c) if ctx_out else None
    return y_lat, y_ctx

def neighbourhood_mixer(h_lat, h_ctx, w_in, w_o, rpb, ctx_out):
    b, n, d = h_lat.shape
    rows = n // GRID_W
    kh = min(NAT_WIN_ROWS, rows)
    kw = NAT_WIN_COLS
    nh, hd = NAT_HEADS, NAT_HEAD_DIM
    scale = hd ** -0.5

    p = h_lat @ w_in
    q = p[..., :d].reshape(b, rows, GRID_W, nh, hd) * scale
    k = p[..., d:2 * d].reshape(b, rows, GRID_W, nh, hd)
    v = p[..., 2 * d:].reshape(b, rows, GRID_W, nh, hd)

    pc = h_ctx @ (w_in if ctx_out else w_in[:, d:])
    pc = pc[..., d:] if ctx_out else pc
    L = h_ctx.shape[1]
    k_c = pc[..., :d].reshape(b, L, nh, hd)
    v_c = pc[..., d:].reshape(b, L, nh, hd)

    row_start = jnp.clip(jnp.arange(rows) - kh // 2, 0, rows - kh)
    cols = jnp.arange(GRID_W)
    col_start = jnp.clip(cols - kw // 2, 0, GRID_W - kw)
    col_in = (cols[None, :] >= col_start[:, None]) & (cols[None, :] < col_start[:, None] + kw)
    dc_idx = jnp.clip(cols[None, :] - cols[:, None] + NAT_WIN_COLS - 1, 0, 2 * NAT_WIN_COLS - 2)
    rpb_f = rpb.astype(jnp.float32)
    band = kh * GRID_W

    def row_block(args):
        q_r, r = args
        start = row_start[r]
        k_band = lax.dynamic_slice_in_dim(k, start, kh, axis=1)
        v_band = lax.dynamic_slice_in_dim(v, start, kh, axis=1)
        dr_idx = start + jnp.arange(kh) - r + NAT_WIN_ROWS - 1
        bias = rpb_f[:, dr_idx[None, :, None], dc_idx[:, None, :]]
        bias = jnp.where(col_in[:, None, :], bias, -jnp.inf)
        s_loc = jnp.einsum('bqhd,bikhd->bhqik', q_r, k_band).astype(jnp.float32) + bias
        s_ctx = jnp.einsum('bqhd,blhd->bhql', q_r, k_c).astype(jnp.float32)
        s = jnp.concatenate([s_loc.reshape(b, nh, GRID_W, band), s_ctx], axis=-1)
        prob = jax.nn.softmax(s, axis=-1).astype(v.dtype)
        p_loc = prob[..., :band].reshape(b, nh, GRID_W, kh, GRID_W)
        return (jnp.einsum('bhqik,bikhd->bqhd', p_loc, v_band)
                + jnp.einsum('bhql,blhd->bqhd', prob[..., band:], v_c))

    o = lax.map(row_block, (jnp.moveaxis(q, 1, 0), jnp.arange(rows)))
    y_lat = jnp.moveaxis(o, 0, 1).reshape(b, n, d) @ w_o

    y_ctx = None
    if ctx_out:
        q_c = pc_q = (h_ctx @ w_in[:, :d]).reshape(b, L, nh, hd) * scale
        s = jnp.einsum('blhd,bmhd->bhlm', q_c, k_c).astype(jnp.float32)
        prob = jax.nn.softmax(s, axis=-1).astype(v_c.dtype)
        y_ctx = jnp.einsum('bhlm,bmhd->blhd', prob, v_c).reshape(b, L, d) @ w_o
    return y_lat, y_ctx

def sq_relu_mlp(h, w1, w2):
    return jnp.square(jax.nn.relu(h @ w1)) @ w2

def second_inputs(seed: int = 0) -> dict:
    key = jax.random.key(seed)
    ks = jax.random.split(key, 17)
    f32 = jnp.float32

    def nrm(k, shape, scale):
        return jax.random.normal(k, shape, f32) * scale

    qk_w = RET_HEADS * RET_QK_DIM
    v_w = RET_HEADS * RET_V_DIM
    base_decay = jnp.log(-jnp.log(1.0 - 2.0 ** (-5.0 - jnp.arange(RET_HEADS, dtype=f32))))
    return {
        'x': nrm(ks[0], (BATCH, SEQ, D_MODEL), 1.0),
        'c': nrm(ks[1], (BATCH, D_MODEL), 1.0),
        'ctx': nrm(ks[2], (BATCH, CTX_LEN, D_MODEL), 1.0),
        'c_ctx': nrm(ks[3], (D_MODEL,), 1.0),
        'ada_w': nrm(ks[4], (DEPTH_2, D_MODEL, 6 * D_MODEL), 0.5 * D_MODEL ** -0.5),
        'ada_b': nrm(ks[5], (DEPTH_2, 6 * D_MODEL), 0.02),
        'ret_w_in': nrm(ks[6], (N_RET_LAYERS, D_MODEL, 2 * qk_w + 2 * v_w), D_MODEL ** -0.5),
        'ret_w_o': nrm(ks[7], (N_RET_LAYERS, v_w, D_MODEL), DN_BETA * v_w ** -0.5),
        'ret_decay': base_decay + nrm(ks[8], (N_RET_LAYERS, 2, RET_HEADS), 0.1),
        'nat_w_in': nrm(ks[9], (N_NAT_LAYERS, D_MODEL, 3 * D_MODEL), D_MODEL ** -0.5),
        'nat_w_o': nrm(ks[10], (N_NAT_LAYERS, D_MODEL, D_MODEL), DN_BETA * D_MODEL ** -0.5),
        'nat_rpb': nrm(ks[11], (N_NAT_LAYERS, NAT_HEADS, 2 * NAT_WIN_ROWS - 1, 2 * NAT_WIN_COLS - 1), 0.1),
        'mlp_w1': nrm(ks[12], (DEPTH_2, D_MODEL, MLP_HIDDEN), D_MODEL ** -0.5),
        'mlp_w2': nrm(ks[13], (DEPTH_2, MLP_HIDDEN, D_MODEL), DN_BETA * MLP_HIDDEN ** -0.5),
        'ln_g': 1.0 + nrm(ks[14], (DEPTH_2, 2, D_MODEL), 0.02),
        'ln_b': nrm(ks[15], (DEPTH_2, 2, D_MODEL), 0.02),
    }

def second_block(x, c, ctx, c_ctx, ada_w, ada_b, ret_w_in, ret_w_o, ret_decay,
              nat_w_in, nat_w_o, nat_rpb, mlp_w1, mlp_w2, ln_g, ln_b):
    n = x.shape[1]
    ang_row, ang_col = axial_rope_angles(n, RET_QK_DIM // 2)
    silu_c = jax.nn.silu(c)
    silu_cc = jax.nn.silu(c_ctx)
    for i in range(DEPTH_2):
        last = i == DEPTH_2 - 1
        j = i // N_MIXERS
        mod = (silu_c @ ada_w[i] + ada_b[i])[:, None, :]
        mod_c = silu_cc @ ada_w[i] + ada_b[i]
        sh1, sc1, g1, sh2, sc2, g2 = jnp.split(mod, 6, axis=-1)
        sh1c, sc1c, g1c, sh2c, sc2c, g2c = jnp.split(mod_c, 6, axis=-1)

        h = x * (1.0 + sc1) + sh1
        hc = ctx * (1.0 + sc1c) + sh1c
        if i % N_MIXERS == 0:
            y, yc = retention_mixer(h, hc, ret_w_in[j], ret_w_o[j], ret_decay[j],
                                    ang_row, ang_col, not last)
        else:
            y, yc = neighbourhood_mixer(h, hc, nat_w_in[j], nat_w_o[j], nat_rpb[j], not last)

        x = layer_norm(DN_ALPHA * x + g1 * y, ln_g[i, 0], ln_b[i, 0])
        h = x * (1.0 + sc2) + sh2
        x = layer_norm(DN_ALPHA * x + g2 * sq_relu_mlp(h, mlp_w1[i], mlp_w2[i]), ln_g[i, 1], ln_b[i, 1])

        if not last:
            ctx = layer_norm(DN_ALPHA * ctx + g1c * yc, ln_g[i, 0], ln_b[i, 0])
            hc = ctx * (1.0 + sc2c) + sh2c
            ctx = layer_norm(DN_ALPHA * ctx + g2c * sq_relu_mlp(hc, mlp_w1[i], mlp_w2[i]),
                             ln_g[i, 1], ln_b[i, 1])
    return x


def setup_inputs(seed=0):
    out = dict(first_inputs(seed))
    for name, value in second_inputs(seed + 1).items():
        if name != "x":
            out[name + "_2"] = value
    return out


def reference(
    x, c, w_ada, b_ada, norm1_w, w_in, conv_w, A_log, dt_bias, dn_norm_w, w_out, norm2_w,
    w_router, b_router, w1, b1, w2, b2, final_norm_w, c_2, ctx_2, c_ctx_2, ada_w_2, ada_b_2,
    ret_w_in_2, ret_w_o_2, ret_decay_2, nat_w_in_2, nat_w_o_2, nat_rpb_2, mlp_w1_2, mlp_w2_2,
    ln_g_2, ln_b_2,
):
    x = first_block(
        x, c, w_ada, b_ada, norm1_w, w_in, conv_w, A_log, dt_bias, dn_norm_w, w_out, norm2_w,
        w_router, b_router, w1, b1, w2, b2, final_norm_w,
    )
    return second_block(
        x, c_2, ctx_2, c_ctx_2, ada_w_2, ada_b_2, ret_w_in_2, ret_w_o_2, ret_decay_2,
        nat_w_in_2, nat_w_o_2, nat_rpb_2, mlp_w1_2, mlp_w2_2, ln_g_2, ln_b_2,
    )


_drawn_inputs = setup_inputs


def setup_inputs(seed=0):
    import zlib

    import numpy as np

    out = dict(_drawn_inputs(seed))
    spreads = {}
    factors = {'norm1_w': 3.615,
     'dn_norm_w': 4.258,
     'b_router': 30.459,
     'b1': 64.0,
     'b2': 64.0,
     'ada_b_2': 3.229,
     'nat_rpb_2': 64.0,
     'norm2_w': 5.298}
    for name, (base, spread) in spreads.items():
        noise = np.random.default_rng([zlib.crc32(name.encode()), seed]).standard_normal(out[name].shape)
        drawn = base * np.exp(spread * noise) if base else spread * noise
        out[name] = jnp.asarray(drawn.astype(out[name].dtype))
    for name, factor in factors.items():
        out[name] = (out[name] * factor).astype(out[name].dtype)
    return out
```

```python
from contextlib import ExitStack, contextmanager

import numpy as np

import concourse.bass as bass
from concourse import mybir

F32 = mybir.dt.float32
I32 = mybir.dt.int32
ALU = mybir.AluOpType
ACT = mybir.ActivationFunctionType
AX = mybir.AxisListType.X

P = 128
D = 1024
KT = D // P
SEQ = 256
XT = SEQ // P
AT_W = 512
DN_HEADS = 4
EXPERTS = 32
TOP_K = 4
F_EXP = 1024
RET_HEADS = 4
RET_V = 512
MLP_HID = 4096
NAT_HEADS = 32
NAT_HD = 32
NAT_GROUPS = NAT_HEADS * NAT_HD // P
GRID_W = 64
REACH = 2 * GRID_W
EPS_RMS = 1e-6
EPS_LN = 1e-5
ALPHA = (2.0 * 2) ** 0.25
RPB_W = 2 * GRID_W - 1
NEG = -1e30
LEVELS = 7


class Count:

    def __init__(self, start=0):
        self.n, self.turn, self.per, self.start = start, None, 0, 0
        self.name = ''

    def at(self, k=0):
        return self.n + k if self.turn is None else self.turn * self.per + (self.n + k)

    def dma(self):
        use = (self.n // 2 + 1) * 16
        return use if self.turn is None else self.turn * (self.per * 8) + use


@contextmanager
def turns(eng, number, per):
    with eng.Fori(0, number) as i:
        for c, step in per.items():
            c.turn, c.per, c.start = i, step, c.n
        yield i
        for c, step in per.items():
            assert c.n - c.start == step, ("a turn moves the count by", c.n - c.start, "not", step, c.name)
    for c, step in per.items():
        c.turn, c.n = None, c.start + number * step


class Pair:

    def __init__(self, banks, full, free):
        self.banks, self.full, self.free = banks, full, free


class Filler:
    def __init__(self, pe, pair):
        self.pe, self.pair, self.c = pe, pair, Count()

    def open(self):
        self.pe.wait_ge(self.pair.free, self.c.at(1))
        return self.pair.banks[self.c.n % 2]

    def close(self, last):
        last.then_inc(self.pair.full, 1)
        self.c.n += 1

    def read(self, ago=0):
        self.pe.wait_ge(self.pair.free, self.c.at(2 - ago))


class Reader:
    def __init__(self, eng, pair):
        self.eng, self.pair, self.c = eng, pair, Count()

    def take(self):
        self.eng.wait_ge(self.pair.full, self.c.at(1))
        return self.pair.banks[self.c.n % 2]

    def done(self, last):
        last.then_inc(self.pair.free, 1)
        self.c.n += 1

    def settle(self):
        self.eng.wait_ge(self.pair.free, self.c.at(2))


class GemmFiller(Filler):

    def __init__(self, pe, pair, ring, landed, half0_used, panel_done):
        super().__init__(pe, pair)
        self.others, self.panels = Count(), Count()
        self.ring, self.landed, self.half0_used, self.panel_done = ring, landed, half0_used, panel_done
        self.seen = set()

    def half(self, h):
        slot = self.panels.n % 2
        if h not in self.seen:
            self.pe.wait_ge(self.landed[slot][h], self.panels.dma())
            self.seen.add(h)
        return self.ring[:, slot, 4 * h:4 * h + 4, :]

    def close(self, last, ends_panel=False):
        last.then_inc(self.panel_done if ends_panel else self.pair.full, 1)
        self.c.n += 1
        if ends_panel:
            self.panels.n += 1
            self.seen = set()
        else:
            self.others.n += 1

    def product(self, lhs, rhs, ends_panel=False, depth=KT, dst=lambda b: b[:, :]):
        b = self.open()
        for k in range(depth):
            v = self.half(k // 4)[:, k % 4, :]
            m = self.pe.matmul(dst(b), lhs(k, v), rhs(k, v), start=(k == 0), stop=(k == depth - 1))
            if ends_panel and k == 3:
                m.then_inc(self.half0_used, 1)
        self.close(m, ends_panel)


class GemmReader:
    def __init__(self, eng, pair, panel_done):
        self.eng, self.pair, self.panel_done = eng, pair, panel_done
        self.c, self.others, self.panels = Count(), Count(), Count()

    def take(self, ends_panel=False):
        if ends_panel:
            self.eng.wait_ge(self.panel_done, self.panels.at(1))
            self.panels.n += 1
        else:
            self.eng.wait_ge(self.pair.full, self.others.at(1))
            self.others.n += 1
        return self.pair.banks[self.c.n % 2]

    def done(self, last):
        last.then_inc(self.pair.free, 1)
        self.c.n += 1

    def settle(self):
        self.eng.wait_ge(self.pair.free, self.c.at(2))


class Chain:

    def __init__(self, eng, sem):
        self.eng, self.sem, self.c = eng, sem, Count()

    def __call__(self, ins):
        ins.then_inc(self.sem, 1)
        self.c.n += 1
        self.eng.wait_ge(self.sem, self.c.at())


class Post:

    def __init__(self, eng, sem):
        self.eng, self.sem, self.c = eng, sem, Count()

    def send(self, ins):
        ins.then_inc(self.sem, 1)
        self.c.n += 1

    def get(self, k=1):
        self.c.n += k
        self.eng.wait_ge(self.sem, self.c.at())


CONSTS, CONST_COLS = {}, 0
for _name, _shape in (("ident", (P,)), ("upper", (P,)), ("strict", (P,)), ("lvl", (LEVELS, P)),
                      ("lcount", (3 * P,)), ("swap", (P,)), ("anti", (P,)), ("dist", (2, SEQ)),
                      ("rope", (2, 2, SEQ)), ("natmask", (GRID_W,)), ("iota", (2 * P,))):
    CONSTS[_name] = (CONST_COLS, _shape)
    CONST_COLS += int(np.prod(_shape))


def constants():
    c = {}
    r = np.arange(P)
    c["ident"] = r[:, None] == r[None, :]
    c["upper"] = r[:, None] <= r[None, :]
    c["strict"] = r[:, None] < r[None, :]
    c["lvl"] = np.stack([((r[None, :] >> (l + 1)) == (r[:, None] >> (l + 1)))
                         & ((r[None, :] >> l) % 2 == 1) & ((r[:, None] >> l) % 2 == 0)
                         for l in range(LEVELS)], axis=1)
    t, s = np.arange(SEQ)[:, None], np.arange(SEQ)[None, :]
    d = t - s
    seen = ((d >= 0) & (d <= 128)) * 1 + ((d >= 0) & (d % 4 == 0)) + ((d >= 0) & (d % 16 == 0))
    lc = np.where(seen > 0, np.log(np.maximum(seen, 1)), NEG)
    c["lcount"] = np.concatenate([lc[0:P, 0:P], lc[P:SEQ, :]], axis=1)
    c["swap"] = r[:, None] == (r[None, :] + 64) % P
    c["anti"] = (r[:, None] // 64 == r[None, :] // 64) & (r[:, None] % 64 == 63 - r[None, :] % 64)
    c["dist"] = np.stack([s[0][None, :] - (r[:, None] + P * n) for n in range(2)], axis=1)
    inv = (1.0 / (10000.0 ** (np.arange(0, P, 2, dtype=np.float32) / P))).astype(np.float32)
    pos = np.arange(SEQ)
    ang = [inv[r % 64][:, None] * x[None, :].astype(np.float32) for x in (pos // GRID_W, pos % GRID_W)]
    sign = np.where(r < 64, -1.0, 1.0)[:, None]
    c["rope"] = np.stack([np.stack([np.cos(x), np.sin(x) * sign], axis=1) for x in ang], axis=1)
    q, k = (r % GRID_W)[:, None], np.arange(GRID_W)[None, :]
    start = np.clip(q - 8, 0, GRID_W - 16)
    c["natmask"] = np.where((k >= start) & (k < start + 16), 0.0, NEG)
    c["iota"] = np.broadcast_to(np.arange(2 * P)[None, :], (P, 2 * P))
    return np.concatenate([c[n].reshape(P, -1).astype(np.float32) for n in CONSTS], axis=1)


def program(nc, a, out, dbg=None):
    ctx = ExitStack()
    with ctx:
        def sb(name, *shape, dt=F32):
            return ctx.enter_context(nc.sbuf_tensor(name, [P, *shape], dt))

        def sem(name):
            return ctx.enter_context(nc.semaphore(name))

        bank = [ctx.enter_context(nc.psum_tensor(f"bank{i}", [P, 512], F32)) for i in range(8)]

        ring = sb("ring", 2, KT, 512)
        tok = sb("tok", 4, D)
        xn = sb("xn", XT, D)
        hT = sb("hT", KT, 512)
        hid = sb("hid", KT, 512)
        yacc = sb("yacc", 4, D)
        gateb = sb("gateb", 2, D)
        lnrow = sb("lnrow", 2, D)
        cst = sb("cst", CONST_COLS)

        def const(name):
            first, shape = CONSTS[name]
            v = cst[:, first:first + int(np.prod(shape))]
            if len(shape) == 2:
                return v.rearrange("p (a b) -> p a b", a=shape[0])
            if len(shape) == 3:
                return v.rearrange("p (a b c) -> p a b c", a=shape[0], b=shape[1])
            return v

        ident, upper, strict, lvl = const("ident"), const("upper"), const("strict"), const("lvl")
        lcount, swap, anti, dist = const("lcount"), const("swap"), const("anti"), const("dist")
        rope, natmask, iota = const("rope"), const("natmask"), const("iota")
        ones = sb("ones", P)
        params = sb("params", 3, P)
        csil = sb("csil", KT, 3)
        biascol = sb("biascol", 144)
        parcol = sb("parcol", 64)
        convcol = sb("convcol", DN_HEADS, 12)
        modcol = sb("modcol", 144, 3)
        arow = sb("arow", 2, 512)
        scol = sb("scol", 4, KT)
        diag = sb("diag", KT, P)
        stats = sb("stats", 4, 2, 6)
        mv = sb("mv", 4, 2)
        std = sb("std", 4)
        rstd = sb("rstd", 4)
        hsel = sb("hsel", 10, 2)
        gmul = sb("gmul", 4, KT)
        headp = sb("headp", 2, 4)
        dnw = sb("dnw", P)
        smallw = sb("smallw", KT * 8 + KT * EXPERTS)
        wdba = smallw[:, 0:KT * 8].rearrange("p (k n) -> p k n", k=KT)
        wr = smallw[:, KT * 8:].rearrange("p (k n) -> p k n", k=KT)
        brow = sb("brow", EXPERTS)
        lgam = sb("lgam", 8)
        idle = sb("idle", 4)
        scratch = sb("scratch", 14 * 1024)
        cnt_i = sb("cnt_i", 1, dt=I32)

        def carve(start, *shape):
            n = int(np.prod(shape))
            v = scratch[:, start:start + n]
            if len(shape) == 2:
                return v.rearrange("p (a b) -> p a b", a=shape[0])
            if len(shape) == 3:
                return v.rearrange("p (a b c) -> p a b c", a=shape[0], b=shape[1])
            return v

        gemm = Pair(bank[0:2], sem("gemm_full"), sem("gemm_free"))
        side = Pair(bank[2:4], sem("side_full"), sem("side_free"))
        att = Pair(bank[4:6], sem("att_full"), sem("att_free"))
        mixp = Pair(bank[6:8], sem("mix_full"), sem("mix_free"))
        landed = [[sem(f"landed_{s}{h}") for h in range(2)] for s in range(2)]
        half0_used = sem("half0_used")
        panel_done = sem("panel_done")
        consts_in = sem("consts_in")
        params_in = sem("params_in")
        tok_in = sem("tok_in")
        small_in = sem("small_in")
        dve_step = sem("dve_step")
        act_step = sem("act_step")
        act_to_pe = sem("act_to_pe")
        b2_go = sem("b2_go")
        nat_go = sem("nat_go")
        to_act = sem("to_act")
        from_act = sem("from_act")
        to_pe = sem("to_pe")
        b2_in = sem("b2_in")
        b1_in = [sem("b1_in0"), sem("b1_in1")]
        b1_used = sem("b1_used")
        rows_in = sem("rows_in")
        rows_used = sem("rows_used")
        ones_ready = sem("ones_ready")
        count_ready = sem("count_ready")
        bias_in = [sem("bias_in0"), sem("bias_in1")]
        bias_used = sem("bias_used")
        out_ready = sem("out_ready")
        out_done = sem("out_done")
        o_gemm = Pair(bank[0:2], sem("o_gemm_full"), sem("o_gemm_free"))
        o_side = Pair(bank[2:4], sem("o_side_full"), sem("o_side_free"))
        o_att = Pair(bank[4:6], sem("o_att_full"), sem("o_att_free"))
        o_mix = Pair(bank[6:8], sem("o_mix_full"), sem("o_mix_free"))
        o_landed = [[sem(f"o_landed_{s}{h}") for h in range(2)] for s in range(2)]
        o_half0 = sem("o_half0_used")
        o_done = sem("o_panel_done")
        o_dve = sem("o_dve_step")
        o_to_act = sem("o_to_act")
        o_from_act = sem("o_from_act")
        o_to_pe = sem("o_to_pe")
        o_b1 = [sem("o_b1_in0"), sem("o_b1_in1")]
        o_b1_used = sem("o_b1_used")

        qkT = carve(0, 512)
        vtok = carve(512, 2, P)
        cin = carve(768, 3, 260)
        cy = carve(1552, 3, SEQ)
        cs = carve(2320, 3, SEQ)
        dz = carve(3088, 2, P)
        qkv = carve(3344, 6, P)
        qn = carve(4112, 2, P)
        kn = carve(4368, 2, P)
        kb = carve(4624, 2, P)
        vb = carve(4880, 2, P)
        kbg = carve(5136, P)
        qd = carve(5264, P)
        kd = carve(5392, P)
        featT = carve(5520, 7, P)
        decay = carve(6416, 2, P)
        LT = carve(6672, 2, P)
        IT = carve(6928, 2, P)
        LM = carve(7184, 2, P)
        TU = carve(7440, 4, P)
        P1 = carve(7952, 2, P)
        unew = carve(8208, 2, P)
        wT = carve(8464, P)
        state = carve(8592, P)
        osb = carve(8720, 2, P)
        gb = carve(8976, 2, P)
        cw = carve(9232, 12)
        gates = carve(9248, 10, 8)
        satt = carve(9344, 3 * P)
        pT = carve(9728, 3 * P)
        amax = carve(10112, 8)
        aden = carve(10120, 8)
        arec = carve(10128, 8)
        dss = carve(10136, 16)
        mix = hid[:, 0:4, :].rearrange("p a b -> p (a b)").rearrange("p (t n) -> p t n", t=2)
        lg = carve(0, 2, EXPERTS)
        m8 = carve(64, 2, 8)
        eq = carve(80, 2, EXPERTS)
        cum = carve(144, 2, 2, EXPERTS)
        sel = carve(272, 2, EXPERTS)
        eg = carve(336, 2, EXPERTS)
        gt = carve(400, 2, EXPERTS)
        rs = carve(464, 16)
        cntf = carve(480, EXPERTS)
        gate = carve(512, 2, EXPERTS + 1)
        pos = carve(578, 2, EXPERTS + 1)
        gT = carve(644, SEQ)
        b2sb = carve(900, D)
        E0 = 2048
        pg = carve(1924, 2, 2, 2)
        OH = carve(E0, 2, P)
        GD = carve(E0 + 256, 2, 2, P)
        xg = carve(E0 + 768, KT, P)
        act_h = carve(E0 + 1792, D)
        up_h = carve(E0 + 2816, D)
        sig = carve(E0 + 3840, D)
        aT = carve(E0 + 4864, KT, P)
        ysb = carve(E0 + 5888, D)
        comb = carve(E0 + 6912, 2, P)
        b1b = carve(E0 + 7168, 2, 2048)
        rqk = carve(0, 4, 512)
        rv = carve(2048, 4, 512)
        rg = carve(4096, 4, 512)
        dpos = carve(6144, 2, SEQ)
        dneg = carve(6656, 2, SEQ)
        Wd = carve(7168, 2, SEQ)
        Wc = carve(7680, 2, SEQ)
        We = carve(8192, 2, SEQ)
        rsT = carve(8704, 6, SEQ)
        ro = carve(10240, 4, 512)
        lgs = carve(12296, 4)
        rtmp = carve(12304, 2, SEQ)
        lgx = carve(12816, 4)
        roT = hid[:, 0:4, :]
        mtmp = carve(0, 512)
        nq = carve(0, SEQ)
        nk = carve(256, 512)
        nv = carve(768, 4, P)
        nbias = carve(1280, 2, 6, GRID_W)
        ns = carve(2048, 2, 512)
        nmax = carve(3072, 4)
        nneg = carve(3076, 4)
        nden = carve(3080, 4)
        nrec = carve(3084, 4)
        npT = carve(3088, 4, P)
        no = xn

        def param_row(src, t):
            n = src.shape[-1]
            return bass.AP(src.tensor, src.offset, [[0, P], [1, n]])

        block = ctx.enter_context(nc.Block())


        @block.sync
        def _(sp):
            panels = Count()

            def panel(src, width=512, start=False, sems=(landed, half0_used, panel_done)):
                arrived, half0, done = sems
                slot = panels.n % 2
                for h, used in enumerate((half0, done)):
                    if not start:
                        sp.wait_ge(used, panels.at(-1))
                    dst = ring[:, slot, 4 * h:4 * h + 4, 0:width]
                    part = 4 * width
                    sp.dma_start(dst, src[:, h * part:(h + 1) * part].rearrange("p (k n) -> p k n", k=4))\
                        .then_inc(arrived[slot][h], 16)
                panels.n += 1

            for j in range(2):
                panel(a["panels_a"][j], start=True)
            for name, row0 in (("x", 0), ("ctx_2", 2)):
                sp.dma_start(tok[:, row0:row0 + 2, :],
                             a[name][0].rearrange("(t p) n -> p t n", p=P)).then_inc(tok_in, 16)

            def stream(src, first, number, **kw):
                with turns(sp, (number - first) // 2, {panels: 2}) as i:
                    for j in range(2):
                        panel(at(src, i * 2 + (first + j)), **kw)

            def at(src, index):
                return src[bass.ds(index, 1)].rearrange("a p n -> (a p) n")

            stream(a["panels_a"], 2, a["panels_a"].shape[0])
            stream(a["panels_e"], 0, a["panels_e"].shape[0])
            sp.wait_ge(count_ready, 1)
            most = sp.value_load(cnt_i[0:1, 0:1], min_val=0, max_val=SEQ)
            kept = panels.n
            with sp.If(most > P):
                sp.wait_ge(panel_done, panels.at())
                panels.n = 0
                o = (o_landed, o_half0, o_done)
                for j in range(2):
                    panel(a["panels_e"][j], start=True, sems=o)
                stream(a["panels_e"], 2, a["panels_e"].shape[0], sems=o)
                sp.wait_ge(o_done, panels.at())
            panels.n = kept
            stream(a["panels_b"], 0, a["panels_b"].shape[0])
            stream(a["panels_n"], 0, a["panels_n"].shape[0], width=3 * P)
            stream(a["panels_c"], 0, a["panels_c"].shape[0])
            sp.wait_ge(out_ready, 1)
            sp.dma_start(out[0].rearrange("(t p) n -> p t n", p=P), tok[:, 0:2, :]).then_inc(out_done, 16)
            sp.wait_ge(out_done, 16)

        @block.gpsimd
        def _(pool):
            pool.dma_start(cst[:, :], a["consts"]).then_inc(consts_in, 16)
            pool.dma_start(params[:, :, :], a["params"].rearrange("(t p) n -> p t n", p=P)).then_inc(params_in, 16)
            pool.memset(ones[:, :], 1.0).then_inc(ones_ready, 1)
            pool.memset(cin[:, :, 0:4], 0.0).then_inc(ones_ready, 1)
            pool.dma_start(smallw[:, :], a["smallw"]).then_inc(small_in, 16)
            pool.dma_start(headp[:, 0, :], param_row(a["A_log"][0], 4)).then_inc(small_in, 16)
            pool.dma_start(headp[:, 1, :], param_row(a["dt_bias"][0], 4)).then_inc(small_in, 16)
            pool.dma_start(dnw[:, :], param_row(a["dn_norm_w"][0], P)).then_inc(small_in, 16)
            pool.dma_start(brow[:, :], param_row(a["b_router"][0], EXPERTS)).then_inc(small_in, 16)
            pool.dma_start(lgam[:, :], param_row(a["ret_decay"], 8)).then_inc(small_in, 16)
            pool.dma_start(lnrow[:, 0, :], param_row(a["final_norm_w"], D)).then_inc(rows_in, 16)
            pool.wait_ge(b2_go, 1)
            pool.dma_start(b2sb[0:EXPERTS, :], a["b2"][0]).then_inc(b2_in, 16)

            b1 = a["b1"]

            def load_b1(uses, e, parity, arrived, used, start=False):
                if not start:
                    pool.wait_ge(used, uses.at(-1))
                src = bass.AP(b1.tensor, e * (2 * F_EXP), [[0, P], [1, 2 * F_EXP]])
                pool.dma_start(b1b[:, parity, :], src).then_inc(arrived[parity], 16)
                uses.n += 1

            def all_b1(arrived, used):
                uses = Count()
                for p in range(2):
                    load_b1(uses, p, p, arrived, used, start=True)
                with turns(pool, EXPERTS // 2 - 1, {uses: 2}) as i:
                    for p in range(2):
                        load_b1(uses, i * 2 + (2 + p), p, arrived, used)
                pool.wait_ge(used, uses.at())

            all_b1(b1_in, b1_used)
            pool.wait_ge(count_ready, 1)
            most = pool.value_load(cnt_i[0:1, 0:1], min_val=0, max_val=SEQ)
            with pool.If(most > P):
                all_b1(o_b1, o_b1_used)
            for n in range(4):
                pool.wait_ge(rows_used, n + 1)
                for j, name in enumerate(("ln_g_2", "ln_b_2")):
                    pool.dma_start(lnrow[:, j, :], param_row(a[name][n // 2, n % 2], D)).then_inc(rows_in, 16)
                if n == 1:
                    uses = Count()
                    rp = a["rpb"]

                    def load_bias(uses, head, parity, start=False):
                        if not start:
                            pool.wait_ge(bias_used, uses.at(-1))
                        for b in range(2):
                            src = bass.AP(rp.tensor, head * (15 * RPB_W) + (5 - b) * RPB_W,
                                          [[1, GRID_W], [RPB_W, 6], [1, GRID_W]])
                            pool.dma_start(nbias[64 * b:64 * b + 64, parity, :, :], src)\
                                .then_inc(bias_in[parity], 16)
                        uses.n += 1

                    pool.wait_ge(nat_go, 1)
                    for p in range(2):
                        load_bias(uses, p, p, start=True)
                    with turns(pool, NAT_HEADS // 2 - 1, {uses: 2}) as i:
                        for p in range(2):
                            load_bias(uses, i * 2 + (2 + p), p)

        @block.scalar
        def _(act):
            step = Chain(act, act_step)
            asked = Post(act, to_act)
            to_dve = Post(act, from_act)
            to_tensor = Post(act, act_to_pe)

            act.wait_ge(params_in, 16)
            to_tensor.send(act.activation(params[:, 0, :], params[:, 0, :], ACT.Silu))

            def root(n, post=None):
                asked.get()
                to_dve.send(act.activation(std[:, 0:n], mv[:, 0:n, 1], ACT.Sqrt))

            root(XT)
            act.wait_ge(small_in, 96)
            asked.get()
            act.activation(gates[:, 0, :], gates[:, 0, :], ACT.Sigmoid)
            step(act.activation(gates[:, 2, :], gates[:, 2, :], ACT.Abs))
            step(act.activation(gates[:, 2, :], gates[:, 2, :], ACT.Exp, scale=-1.0))
            act.activation(headp[:, 0, :], headp[:, 0, :], ACT.Exp)
            to_dve.send(act.activation(gates[:, 3, :], gates[:, 2, :], ACT.Ln, bias=1.0))
            asked.get()
            act.activation(gates[:, 5, :], gates[:, 4, :], ACT.Exp)
            to_dve.send(act.activation(gates[:, 6, :], gates[:, 6, :], ACT.Exp))

            with turns(act, DN_HEADS, {asked.c: 6, to_dve.c: 3, to_tensor.c: 3}) as i:
                for h in range(2):
                    asked.get()
                    for t, cols in enumerate((slice(0, P), slice(P, 3 * P))):
                        m = act.activation(satt[:, cols], satt[:, cols], ACT.Exp, bias=amax[:, t:t + 1],
                                           accum_out=aden[:, t:t + 1])
                    to_tensor.send(m)
                asked.get()
                act.activation(dz[:, :, :], dz[:, :, :], ACT.Silu)
                to_tensor.send(act.activation(cs[:, :, :], cy[:, :, :], ACT.Silu))
                asked.get()
                to_dve.send(act.activation(dss[:, 4:8], dss[:, 0:4], ACT.Sqrt))
                asked.get()
                to_dve.send(act.activation(decay[:, :, :], decay[:, :, :], ACT.Exp))
                asked.get()
                to_dve.send(act.activation(dss[:, 12:14], dss[:, 8:10], ACT.Sqrt))

            root(XT)
            asked.get()
            for t in range(XT):
                m = act.activation(eg[:, t, :], lg[:, t, :], ACT.Exp, bias=rs[:, t:t + 1])
            to_dve.send(m)

            def experts(asked, to_dve):
                with turns(act, EXPERTS // 2, {asked.c: 4, to_dve.c: 4}) as i:
                    for _ in range(2):
                        for c in range(2):
                            asked.get()
                            to_dve.send(act.activation(sig[:, 512 * c:512 * c + 512],
                                                       act_h[:, 512 * c:512 * c + 512],
                                                       ACT.Sigmoid, scale=1.702))

            experts(asked, to_dve)
            act.wait_ge(count_ready, 1)
            most = act.value_load(cnt_i[0:1, 0:1], min_val=0, max_val=SEQ)
            with act.If(most > P):
                experts(Post(act, o_to_act), Post(act, o_from_act))
            root(XT)

            asked.get()
            to_dve.send(act.activation(lgam[:, :], lgam[:, :], ACT.Exp))
            with turns(act, RET_HEADS, {asked.c: 3, to_dve.c: 3}) as i:
                asked.get()
                act.activation(Wd[:, :, :], dpos[:, :, :], ACT.Exp, scale=lgs[:, 0:1])
                act.activation(We[:, :, :], dneg[:, :, :], ACT.Exp, scale=lgs[:, 1:2])
                act.activation(Wc[:, :, :], dist[:, :, :], ACT.Exp, scale=lgs[:, 0:1], bias=lgs[:, 2:3])
                to_dve.send(act.activation(rtmp[:, :, :], dist[:, :, :], ACT.Exp, scale=lgx[:, 0:1],
                                           bias=lgs[:, 3:4]))
                asked.get()
                to_dve.send(act.activation(rg[:, :, :], rg[:, :, :], ACT.Silu))
                root(4)
            root(4)
            root(4)
            with turns(act, NAT_GROUPS // 2, {asked.c: 16, to_tensor.c: 16}) as i:
                for n in range(16):
                    asked.get()
                    to_tensor.send(act.activation(ns[:, n % 2, :], ns[:, n % 2, :], ACT.Exp,
                                                  bias=nneg[:, n % 2:n % 2 + 1],
                                                  accum_out=nden[:, n % 2:n % 2 + 1]))
            root(XT)
            root(XT)

        @block.tensor
        def _(pe):
            G = GemmFiller(pe, gemm, ring, landed, half0_used, panel_done)
            S, A, M = Filler(pe, side), Filler(pe, att), Filler(pe, mixp)
            from_dve = Post(pe, to_pe)
            from_a = Post(pe, act_to_pe)
            per_gemm = lambda fills, panels: {G.c: fills, G.others: fills - panels, G.panels: panels}

            pe.wait_ge(consts_in, 16)
            pe.wait_ge(params_in, 16)
            pe.wait_ge(ones_ready, 2)
            from_a.get()
            b = S.open()
            for n in range(3):
                m = pe.transpose(b[:, n * P:n * P + P], params[:, n, :], ident)
            S.close(m)
            S.read()

            def ada_product(j):
                G.product(lambda k, v: csil[:, k, :], lambda k, v: v, ends_panel=True, dst=lambda b: b[0:3, :])

            def ada_turn(j, ago):
                G.read(ago)
                b = S.open()
                for c in range(4):
                    m = pe.matmul(b[:, 3 * c:3 * c + 3], arow[0:3, j % 2, c * P:c * P + P], ident[0:3, 0:3],
                                  start=True, stop=True)
                S.close(m)

            def ada_four():
                for j in range(4):
                    ada_product(j)
                    if j:
                        ada_turn(j - 1, 1)
                ada_turn(3, 0)

            ada_four()
            with turns(pe, 8, {**per_gemm(4, 4), S.c: 4}) as i:
                ada_four()

            def spread_gate(number):
                for _ in range(number):
                    from_dve.get()
                    for c in range(2):
                        b = S.open()
                        S.close(pe.matmul(b[:, :], ones[:, :], diag[:, 4 * c:4 * c + 4, :], start=True, stop=True))
                    S.read()

            def to_features(src, tiles):
                from_dve.get()
                for k in range(KT):
                    b = S.open()
                    for t in range(tiles):
                        m = pe.transpose(b[:, t * P:t * P + P], src(t, k), ident)
                    S.close(m)
                S.read()

            x_part = lambda t, k: xn[:, t, k * P:k * P + P]
            tok_part = lambda t, k: tok[:, t, k * P:k * P + P]
            mix_part = lambda t, k: mix[:, t, k * P:k * P + P]
            spread_gate(1)
            to_features(x_part, XT)

            pe.wait_ge(small_in, 96)
            b = S.open()
            for t in range(XT):
                for k in range(KT):
                    m = pe.matmul(b[:, 8 * t:8 * t + 8], hT[:, k, t * P:t * P + P], wdba[:, k, :],
                                  start=(k == 0), stop=(k == KT - 1))
            S.close(m)
            from_dve.get()
            b = S.open()
            pe.matmul(b[:, 0:8], upper, gates[:, 1, :], start=True, stop=True)
            S.close(pe.matmul(b[:, 8:16], ones[:, :], gates[:, 1, :], start=True, stop=True))

            def mixer_products():
                def features(b, dst, cols, mark):
                    for k in range(KT):
                        m = pe.matmul(b[:, dst:dst + SEQ], G.half(k // 4)[:, k % 4, cols:cols + P],
                                      hT[:, k, 0:SEQ], start=(k == 0), stop=(k == KT - 1))
                    return m

                def tokens(b, dst, cols, mark):
                    for t in range(XT):
                        for k in range(KT):
                            m = pe.matmul(b[:, dst + t * P:dst + t * P + P], hT[:, k, t * P:t * P + P],
                                          G.half(k // 4)[:, k % 4, cols:cols + P],
                                          start=(k == 0), stop=(k == KT - 1))
                            if mark and t == XT - 1 and k == 3:
                                m.then_inc(half0_used, 1)
                    return m

                b = G.open()
                features(b, 0, 0, False)
                G.close(features(b, SEQ, P, False))
                b = G.open()
                G.close(tokens(b, 0, 2 * P, True), ends_panel=True)
                b = G.open()
                features(b, 0, 0, False)
                G.close(features(b, SEQ, P, False))
                b = G.open()
                features(b, 0, 2 * P, False)
                G.close(tokens(b, SEQ, 3 * P, True), ends_panel=True)

            with turns(pe, DN_HEADS, {**per_gemm(4, 2), S.c: 24, A.c: 6, from_dve.c: 9, from_a.c: 3}) as i:
                mixer_products()
                G.read(2)
                for h in range(2):
                    r = slice(64 * h, 64 * h + 64)
                    b = A.open()
                    pe.matmul(b[:, 0:P], qkT[r, 0:P], qkT[r, SEQ:SEQ + P], start=True, stop=True)
                    A.close(pe.matmul(b[:, P:3 * P], qkT[r, P:SEQ], qkT[r, SEQ:2 * SEQ], start=True, stop=True))
                    from_a.get()
                    b = A.open()
                    for n in range(3):
                        m = pe.transpose(b[:, n * P:n * P + P], satt[:, n * P:n * P + P], ident)
                    A.close(m)
                    A.read()
                    b = A.open()
                    pe.matmul(b[:, 0:64], pT[:, 0:P], vtok[:, 0, r], start=True, stop=True)
                    pe.matmul(b[:, 64:128], pT[:, P:2 * P], vtok[:, 0, r], start=True, stop=False)
                    A.close(pe.matmul(b[:, 64:128], pT[:, 2 * P:3 * P], vtok[:, 1, r], start=False, stop=True))
                from_a.get()
                for ns_ in (range(4), range(4, 6)):
                    b = S.open()
                    for c, n in enumerate(ns_):
                        m = pe.transpose(b[:, c * P:c * P + P], cs[:, n // 2, (n % 2) * P:(n % 2) * P + P], ident)
                    S.close(m)
                from_dve.get()
                b = S.open()
                for n in range(2):
                    m = pe.matmul(b[:, n * P:n * P + P], gb[:, n, :], upper, start=True, stop=True)
                S.close(m)
                from_dve.get()
                for srcs in ((kn[:, 0, :], kn[:, 1, :], kb[:, 0, :], kb[:, 1, :]),
                             (qn[:, 0, :], qn[:, 1, :], qd[:, :])):
                    b = S.open()
                    for c, src in enumerate(srcs):
                        m = pe.transpose(b[:, c * P:c * P + P], src, ident)
                    S.close(m)
                S.read()
                b = S.open()
                for n in range(2):
                    pe.matmul(b[:, n * P:n * P + P], featT[:, n, :], featT[:, 2 + n, :], start=True, stop=True)
                    m = pe.matmul(b[:, (2 + n) * P:(3 + n) * P], featT[:, n, :], featT[:, 4 + n, :],
                                  start=True, stop=True)
                S.close(m)
                for l in range(LEVELS):
                    from_dve.get()
                    b = S.open()
                    for n in range(2):
                        m = pe.matmul(b[:, n * P:n * P + P], LM[:, n, :], TU[:, n, :], start=True, stop=True)
                    S.close(m)
                    S.read()
                    b = S.open()
                    for n in range(2):
                        pe.matmul(b[:, n * P:n * P + P], TU[:, 2 + n, :], P1[:, n, :], start=True, stop=True)
                        m = pe.matmul(b[:, (2 + n) * P:(3 + n) * P], P1[:, n, :], TU[:, 2 + n, :],
                                      start=True, stop=True)
                    S.close(m)
                S.read()
                b = S.open()
                for n in range(2):
                    pe.matmul(b[:, n * P:n * P + P], TU[:, 2 + n, :], vb[:, n, :], start=True, stop=True)
                S.close(pe.matmul(b[:, 2 * P:3 * P], kbg[:, :], TU[:, 3, :], start=True, stop=True))
                S.read()
                b = S.open()
                pe.matmul(b[:, 0:P], IT[:, 0, :], unew[:, 0, :], start=True, stop=True)
                S.close(pe.matmul(b[:, P:2 * P], kd[:, :], unew[:, 0, :], start=True, stop=True))
                S.read()
                b = S.open()
                S.close(pe.matmul(b[:, 0:P], wT[:, :], state[:, :], start=True, stop=True))
                S.read()
                b = S.open()
                pe.matmul(b[:, 0:P], featT[:, 6, :], state[:, :], start=True, stop=False)
                S.close(pe.matmul(b[:, 0:P], IT[:, 1, :], unew[:, 1, :], start=False, stop=True))

            to_features(mix_part, XT)

            def rows_product(tiles):
                for t in range(tiles):
                    G.product(lambda k, v: hT[:, k, t * P:t * P + P], lambda k, v: v, ends_panel=(t == tiles - 1))

            for c in range(2):
                rows_product(XT)

            to_features(x_part, XT)
            b = S.open()
            for t in range(XT):
                for k in range(KT):
                    m = pe.matmul(b[:, EXPERTS * t:EXPERTS * (t + 1)], hT[:, k, t * P:t * P + P], wr[:, k, :],
                                  start=(k == 0), stop=(k == KT - 1))
            S.close(m)
            from_dve.get()
            b = S.open()
            pe.matmul(b[:, 0:EXPERTS], strict, sel[:, 0, :], start=True, stop=True)
            pe.matmul(b[:, EXPERTS:2 * EXPERTS], strict, sel[:, 1, :], start=True, stop=False)
            pe.matmul(b[:, EXPERTS:2 * EXPERTS], ones[:, :], sel[:, 0, :], start=False, stop=True)
            pe.matmul(b[:, 2 * EXPERTS:3 * EXPERTS], ones[:, :], sel[:, 0, :], start=True, stop=False)
            S.close(pe.matmul(b[:, 2 * EXPERTS:3 * EXPERTS], ones[:, :], sel[:, 1, :], start=False, stop=True))
            from_dve.get()
            b = S.open()
            for t in range(XT):
                m = pe.transpose(b[0:EXPERTS, t * P:t * P + P], gate[:, t, 0:EXPERTS], ident)
            S.close(m)
            S.read()
            pe.wait_ge(b2_in, 16)
            for t in range(XT):
                for c in range(2):
                    b = S.open()
                    S.close(pe.matmul(b[:, :], gT[0:EXPERTS, t * P:t * P + P], b2sb[0:EXPERTS, 512 * c:512 * c + 512],
                                      start=True, stop=True))
            S.read()

            def experts(G, S, A, M, from_dve):
                def gather():
                    from_dve.get()
                    for half in range(2):
                        b = A.open()
                        for k in range(4):
                            for t in range(XT):
                                m = pe.matmul(b[:, k * P:k * P + P], xn[:, t, (4 * half + k) * P:(4 * half + k + 1) * P],
                                              OH[:, t, :], start=(t == 0), stop=(t == XT - 1))
                        A.close(m)

                def turn_act(c):
                    from_dve.get()
                    b = S.open()
                    for n in range(4):
                        m = pe.transpose(b[:, n * P:n * P + P], act_h[:, (4 * c + n) * P:(4 * c + n + 1) * P], ident)
                    S.close(m)

                def up(j):
                    G.product(lambda k, v: xg[:, k, :], lambda k, v: v, ends_panel=True)

                gather()
                with turns(pe, EXPERTS // 2, {G.c: 12, G.panels: 12, S.c: 4, A.c: 4, M.c: 10, from_dve.c: 6}) as i:
                    for e in range(2):
                        A.read()
                        up(0)
                        up(1)
                        up(2)
                        turn_act(0)
                        up(3)
                        gather()
                        b = M.open()
                        for t in range(XT):
                            m = pe.transpose(b[:, t * P:t * P + P], GD[:, e, t, :], ident)
                        M.close(m)
                        turn_act(1)
                        S.read()
                        for c in range(2):
                            G.product(lambda k, v: aT[:, k, :], lambda k, v: v, ends_panel=True)
                        for c in range(2):
                            G.read(1 - c)
                            for t in range(XT):
                                b = M.open()
                                M.close(pe.matmul(b[:, :], comb[:, t, :], ysb[:, 512 * c:512 * c + 512],
                                                  start=True, stop=True))
                for f in (G, S, A, M):
                    f.read()

            experts(G, S, A, M, from_dve)
            pe.wait_ge(count_ready, 1)
            most = pe.value_load(cnt_i[0:1, 0:1], min_val=0, max_val=SEQ)
            with pe.If(most > P):
                experts(GemmFiller(pe, o_gemm, ring, o_landed, o_half0, o_done), Filler(pe, o_side),
                        Filler(pe, o_att), Filler(pe, o_mix), Post(pe, o_to_pe))
            spread_gate(1)

            to_features(tok_part, 4)
            with turns(pe, RET_HEADS, {**per_gemm(20, 4), S.c: 6, A.c: 6, M.c: 4, from_dve.c: 2}) as i:
                for u in range(4):
                    G.product(lambda k, v: v[:, u * P:u * P + P], lambda k, v: hT[:, k, :], ends_panel=(u == 3))
                G.read()
                for n in range(2):
                    b = S.open()
                    for j in range(2):
                        m = pe.matmul(b[:, j * SEQ:(j + 1) * SEQ], swap, rqk[:, 2 * n + j, 0:SEQ], start=True, stop=True)
                    S.close(m)
                rows_product(4)
                rows_product(4)
                from_dve.get()
                for n in range(6):
                    keys, queries = (n, 0) if n < 4 else (n - 2, SEQ)
                    b = A.open()
                    for c in range(2):
                        m = pe.matmul(b[:, 0:SEQ], rqk[:, 2 + c, keys * P:keys * P + P], rqk[:, c, queries:queries + SEQ],
                                      start=(c == 0), stop=(c == 1))
                    A.close(m)
                A.read()
                for t in range(4):
                    b = M.open()
                    src = [(n, n) for n in range(4)] if t < 2 else [(4, 2), (5, 3)]
                    for n, key in src:
                        m = pe.matmul(b[:, :], rsT[:, n, (t % 2) * P:(t % 2) * P + P], rv[:, key, :],
                                      start=(n == src[0][0]), stop=(n == src[-1][0]))
                    M.close(m)
                from_dve.get()
                for k in range(4):
                    b = S.open()
                    for t in range(4):
                        m = pe.transpose(b[:, t * P:t * P + P], ro[:, t, k * P:k * P + P], ident)
                    S.close(m)
                S.read()
                for c in range(2):
                    for t in range(4):
                        b = G.open()
                        for k in range(4):
                            m = pe.matmul(b[:, :], roT[:, k, t * P:t * P + P], G.half(c)[:, k, :],
                                          start=(k == 0), stop=(k == 3))
                            if c == 1 and t == 0 and k == 0:
                                m.then_inc(half0_used, 1)
                        G.close(m, ends_panel=(c == 1 and t == 3))

            def mlp(tiles):
                width = tiles * P
                to_features(tok_part, tiles)
                with turns(pe, 4, {**per_gemm(8 + 2 * tiles, 4), from_dve.c: 1}) as i:
                    for j in range(2):
                        for u in range(4):
                            G.product(lambda k, v: v[:, u * P:u * P + P], lambda k, v: hT[:, k, 0:width],
                                      ends_panel=(u == 3), dst=lambda b: b[:, 0:width])
                    from_dve.get()
                    for c in range(2):
                        for t in range(tiles):
                            G.product(lambda k, v: hid[:, k, t * P:t * P + P], lambda k, v: v,
                                      ends_panel=(t == tiles - 1))

            spread_gate(2)
            mlp(4)
            spread_gate(2)

            to_features(tok_part, 4)
            heads = Count()
            with turns(pe, NAT_GROUPS // 2, {**per_gemm(6, 2), S.c: 16, A.c: 16, M.c: 16, from_a.c: 16, heads: 8}) as i:
                for g in range(2):
                    b = G.open()
                    for k in range(KT):
                        m = pe.matmul(b[:, 0:SEQ], G.half(k // 4)[:, k % 4, 0:P], hT[:, k, 0:SEQ],
                                      start=(k == 0), stop=(k == KT - 1))
                    G.close(m)
                    b = G.open()
                    for k in range(KT):
                        m = pe.matmul(b[:, :], G.half(k // 4)[:, k % 4, P:2 * P], hT[:, k, :],
                                      start=(k == 0), stop=(k == KT - 1))
                    G.close(m)
                    b = G.open()
                    for t in range(4):
                        for k in range(KT):
                            m = pe.matmul(b[:, t * P:t * P + P], hT[:, k, t * P:t * P + P],
                                          G.half(k // 4)[:, k % 4, 2 * P:3 * P], start=(k == 0), stop=(k == KT - 1))
                            if t == 3 and k == 3:
                                m.then_inc(half0_used, 1)
                    G.close(m, ends_panel=True)
                    G.read()

                    def scores(n):
                        h, t = n // 2, n % 2
                        r = slice(NAT_HD * h, NAT_HD * h + NAT_HD)
                        b = A.open()
                        if t == 0:
                            use = heads.n % 2
                            pe.wait_ge(bias_in[use], (heads.n // 2 + 1) * 32 + heads.turn * (heads.per * 16))
                        pe.matmul(b[:, :], nq[r, t * P:t * P + P], nk[r, :], start=True, stop=False)
                        A.close(pe.matmul(b[:, 0:SEQ], anti, nbias[:, heads.n % 2, 2 - 2 * t:6 - 2 * t, :],
                                          start=False, stop=True))
                        if t == 1:
                            heads.n += 1

                    scores(0)
                    for n in range(8):
                        if n < 7:
                            scores(n + 1)
                        h = n // 2
                        from_a.get()
                        b = M.open()
                        for k in range(4):
                            m = pe.transpose(b[:, k * P:k * P + P], ns[:, n % 2, k * P:k * P + P], ident)
                        M.close(m)
                        M.read()
                        b = S.open()
                        for k in range(4):
                            m = pe.matmul(b[:, 0:NAT_HD], npT[:, k, :], nv[:, k, NAT_HD * h:NAT_HD * (h + 1)],
                                          start=(k == 0), stop=(k == 3))
                        S.close(m)
            to_features(x_part, XT)
            for c in range(2):
                rows_product(XT)
            spread_gate(1)
            mlp(2)
            spread_gate(1)

        @block.vector
        def _(dve):
            step = Chain(dve, dve_step)
            G = GemmReader(dve, gemm, panel_done)
            S, A, M = Reader(dve, side), Reader(dve, att), Reader(dve, mixp)
            ask = Post(dve, to_act)
            from_a = Post(dve, from_act)
            to_tensor = Post(dve, to_pe)
            per_gemm = lambda fills, panels: {G.c: fills, G.others: fills - panels, G.panels: panels}
            tt, ts, stt, copy = dve.tensor_tensor, dve.tensor_scalar, dve.scalar_tensor_tensor, dve.tensor_copy

            def col(tile, *index):
                v = tile[(slice(None), *index[:-1], slice(index[-1], index[-1] + 1))]
                return v

            for pair in (gemm, side, att, mixp):
                dve.sem_inc(pair.free, 2)
            b = S.take()
            copy(csil[:, :, :], b[:, 0:3 * KT].rearrange("p (c k) -> p k c", c=3))
            copy(biascol[:, 0:48], b[:, 2 * P:2 * P + 48])
            copy(biascol[:, 48:144], b[:, P:P + 96])
            copy(parcol[:, 0:16], b[:, 2 * P + 48:2 * P + 64])
            S.done(copy(convcol[:, :, :], b[:, 2 * P + 64:2 * P + 112].rearrange("p (h n) -> p h n", h=4)))

            def ada_four(first):
                for j in range(5):
                    if j < 4:
                        b = G.take(ends_panel=True)
                        G.done(copy(arow[0:3, j % 2, :], b[0:3, :]))
                    if j:
                        b = S.take()
                        dst = modcol[:, 4 * (j - 1):4 * j, :] if first is None else \
                            modcol[:, bass.ds(first + 4 * (j - 1), 4), :]
                        S.done(copy(dst, b[:, 0:12].rearrange("p (n c) -> p n c", n=4)))

            ada_four(None)
            with turns(dve, 8, {**per_gemm(4, 4), S.c: 4}) as i:
                ada_four(i * 16 + 16)
            S.settle()
            step(tt(modcol[:, :, :], modcol[:, :, :], biascol[:, :].unsqueeze(2).to_broadcast([P, 144, 3]), ALU.add))

            def mod(layer, part, cond):
                j = 48 * layer + 8 * part
                return modcol[:, j:j + 8, cond]

            def scales(layer, part, norm, conds):
                for n, c in enumerate(conds):
                    step(ts(scol[:, 2 * n, :], mod(layer, part + 1, c), 1.0, None, ALU.add))
                    if norm is not None:
                        step(tt(scol[:, 2 * n, :], scol[:, 2 * n, :], parcol[:, norm:norm + 8], ALU.mult))
                    step(copy(scol[:, 2 * n + 1, :], mod(layer, part, c)))

            def spread_gate(cols, dst):
                for k in range(KT):
                    m = ts(diag[:, k, :], ident, cols[:, k:k + 1], None, ALU.mult)
                to_tensor.send(m)
                for c in range(2):
                    b = S.take()
                    S.done(copy(gateb[:, dst, 512 * c:512 * c + 512], b[:, :]))
                S.settle()

            def spread_gates(layer, part, conds):
                for n, c in enumerate(conds):
                    step(copy(gmul[:, n, :], mod(layer, part, c)))
                    spread_gate(gmul[:, n, :], n)

            def variance(tiles, src, center, eps, width=D):
                parts = width // 512
                for t in range(tiles):
                    for c in range(parts):
                        m = dve.bn_stats(stats[:, t, c, :], src(t)[:, 512 * c:512 * c + 512])
                step(m)
                dve.memset(idle[:, 0:1], 0.0)
                for t in range(tiles):
                    m = dve.bn_aggr(mv[:, t, :], stats[:, t, 0:parts, :])
                step(m)
                if not center:
                    for t in range(tiles):
                        m = stt(mv[:, t, 1:2], mv[:, t, 0:1], mv[:, t, 0:1], mv[:, t, 1:2], ALU.mult, ALU.add)
                    step(m)
                ask.send(ts(mv[:, 0:tiles, 1], mv[:, 0:tiles, 1], eps, None, ALU.add))
                from_a.get()
                step(dve.reciprocal(rstd[:, 0:tiles], std[:, 0:tiles]))

            def from_features(tiles, scaled):
                for k in range(KT):
                    b = S.take()
                    if not scaled:
                        m = copy(hT[:, k, 0:tiles * P], b[:, 0:tiles * P])
                    for n in range(tiles // 2 if scaled else 0):
                        m = ts(hT[:, k, SEQ * n:SEQ * (n + 1)], b[:, SEQ * n:SEQ * (n + 1)],
                               scol[:, 2 * n, k:k + 1], scol[:, 2 * n + 1, k:k + 1], ALU.mult, ALU.add)
                    S.done(m)

            def rms_rows():
                variance(XT, lambda t: tok[:, t, :], False, EPS_RMS)
                for t in range(XT):
                    m = ts(xn[:, t, :], tok[:, t, :], rstd[:, t:t + 1], None, ALU.mult)
                return m

            spread_gates(0, 2, (0,))
            scales(0, 0, 0, (0,))
            dve.wait_ge(tok_in, 32)
            to_tensor.send(rms_rows())
            from_features(XT, True)

            dve.wait_ge(small_in, 96)
            b = S.take()
            bv = b[:, 0:16].rearrange("p (t n) -> p t n", t=2)
            gr = lambda n: gates[:, n, :]
            g3 = lambda n: gates[:, n, :].rearrange("p (t h) -> p t h", t=2)
            copy(g3(0), bv[:, :, 0:4])
            S.done(tt(g3(1), bv[:, :, 4:8], headp[:, 1, :].unsqueeze(1).to_broadcast([P, 2, 4]), ALU.add))
            S.settle()
            ask.send(copy(gr(2), gr(1)))
            from_a.get()
            step(stt(gr(1), gr(1), 0.0, gr(3), ALU.max, ALU.add))
            to_tensor.send(stt(g3(1), g3(1), -1.0, headp[:, 0, :].unsqueeze(1).to_broadcast([P, 2, 4]),
                               ALU.mult, ALU.mult))
            b = S.take()
            copy(gr(4), b[:, 0:8])
            S.done(copy(gr(6), b[:, 8:16]))
            S.settle()
            ask.send(tt(gr(6), gr(6), gr(4), ALU.subtract))
            from_a.get()
            for n in range(4):
                m = copy(TU[:, n, :], ident)
            step(m)

            def attention_head(i, h):
                r = slice(64 * h, 64 * h + 64)
                b = A.take()
                A.done(stt(satt[:, :], b[:, 0:3 * P], 0.125, lcount, ALU.mult, ALU.add))
                A.settle()
                dve.tensor_reduce(amax[:, 0:1], satt[:, 0:P], AX, ALU.max)
                step(dve.tensor_reduce(amax[:, 1:2], satt[:, P:3 * P], AX, ALU.max))
                ask.send(ts(amax[:, 0:2], amax[:, 0:2], -1.0, None, ALU.mult))
                b = A.take()
                A.done(copy(pT[:, :], b[:, 0:3 * P]))
                step(dve.reciprocal(arec[:, 0:2], aden[:, 0:2]))
                b = A.take()
                for t in range(2):
                    m = ts(mix[:, t, bass.ds(i * P + 64 * h, 64)], b[:, 64 * t:64 * t + 64],
                           arec[:, t:t + 1], None, ALU.mult)
                A.done(m)

            with turns(dve, DN_HEADS, {**per_gemm(4, 2), S.c: 24, A.c: 6, ask.c: 6, from_a.c: 3, to_tensor.c: 9,
                                       step.c: 21}) as i:
                b = G.take()
                G.done(copy(qkT[:, :], b[:, :]))
                b = G.take(True)
                G.done(copy(vtok[:, :, :].rearrange("p a b -> p (a b)"), b[:, 0:SEQ]))
                b = G.take()
                G.done(copy(cin[:, 0:2, 4:260], b[:, :].rearrange("p (a b) -> p a b", a=2)))
                b = G.take(True)
                copy(cin[:, 2, 4:260], b[:, 0:SEQ])
                G.done(copy(dz[:, :, :].rearrange("p a b -> p (a b)"), b[:, SEQ:2 * SEQ]))
                for h in range(2):
                    attention_head(i, h)
                for n in range(7):
                    copy(hsel[:, n, :], g3(n)[:, :, bass.ds(i, 1)].rearrange("p t a -> p (t a)"))
                step(copy(cw[:, :], convcol[:, bass.ds(i, 1), :].rearrange("p a n -> p (a n)")))
                G.settle()
                for p in range(3):
                    m = ts(cy[:, p, :], cin[:, p, 4:260], cw[:, 9 + p:10 + p], None, ALU.mult)
                step(m)
                for j in range(3):
                    for p in range(3):
                        m = stt(cy[:, p, :], cin[:, p, 1 + j:257 + j], cw[:, 3 * j + p:3 * j + p + 1], cy[:, p, :],
                                ALU.mult, ALU.add)
                    if j < 2:
                        step(m)
                ask.send(m)
                for n in range(2):
                    m = ts(gb[:, n, :], ones[:, :], hsel[:, 1, n:n + 1], None, ALU.mult)
                to_tensor.send(m)
                for first, number in ((0, 4), (4, 2)):
                    b = S.take()
                    S.done(copy(qkv[:, first:first + number, :].rearrange("p a b -> p (a b)"), b[:, 0:number * P]))
                S.settle()
                for n in range(4):
                    m = dve.tensor_tensor_reduce(osb[:, n % 2, :], qkv[:, n, :], qkv[:, n, :], 1.0, 0.0,
                                                 ALU.mult, ALU.add, dss[:, n:n + 1])
                    step(m)
                ask.send(ts(dss[:, 0:4], dss[:, 0:4], EPS_RMS, None, ALU.add))
                b = S.take()
                for n in range(2):
                    m = ts(decay[:, n, :], b[:, n * P:n * P + P], hsel[:, 4, n:n + 1], 0.0, ALU.subtract, ALU.min)
                S.done(m)
                S.settle()
                from_a.get()
                ask.send(dve.reciprocal(dss[:, 4:8], dss[:, 4:8]))
                dve.wait_ge(to_act, ask.c.at())
                for n in range(2):
                    ts(qn[:, n, :], qkv[:, n, :], dss[:, 4 + n:5 + n], P ** -0.5, ALU.mult, ALU.mult)
                    ts(kn[:, n, :], qkv[:, 2 + n, :], dss[:, 6 + n:7 + n], None, ALU.mult)
                    m = ts(vb[:, n, :], qkv[:, 4 + n, :], hsel[:, 0, n:n + 1], None, ALU.mult)
                step(m)
                for n in range(2):
                    m = ts(kb[:, n, :], kn[:, n, :], hsel[:, 0, n:n + 1], None, ALU.mult)
                step(m)
                ts(kbg[:, :], kb[:, 1, :], hsel[:, 5, 1:2], None, ALU.mult)
                ts(qd[:, :], qn[:, 1, :], hsel[:, 5, 1:2], None, ALU.mult)
                to_tensor.send(ts(kd[:, :], kn[:, 0, :], hsel[:, 6, 0:1], None, ALU.mult))
                from_a.get()
                step(tt(decay[:, :, :], decay[:, :, :], upper.unsqueeze(1).to_broadcast([P, 2, P]), ALU.mult))
                for first, number in ((0, 4), (4, 3)):
                    b = S.take()
                    S.done(copy(featT[:, first:first + number, :].rearrange("p a b -> p (a b)"), b[:, 0:number * P]))
                b = S.take()
                bb = b[:, :].rearrange("p (a n) -> p a n", a=4)
                tt(LT[:, :, :], bb[:, 0:2, :], decay[:, :, :], ALU.mult)
                S.done(tt(IT[:, :, :], bb[:, 2:4, :], decay[:, :, :], ALU.mult))
                for n in range(4):
                    m = copy(TU[:, n, :], ident)
                step(m)
                S.settle()
                for l in range(LEVELS):
                    to_tensor.send(tt(LM[:, :, :], LT[:, :, :], lvl[:, l, :].unsqueeze(1).to_broadcast([P, 2, P]),
                                      ALU.mult))
                    b = S.take()
                    S.done(copy(P1[:, :, :].rearrange("p a b -> p (a b)"), b[:, 0:SEQ]))
                    b = S.take()
                    S.done(tt(TU[:, :, :].rearrange("p a b -> p (a b)"), TU[:, :, :].rearrange("p a b -> p (a b)"),
                              b[:, :], ALU.subtract))
                    S.settle()
                b = S.take()
                copy(unew[:, :, :].rearrange("p a b -> p (a b)"), b[:, 0:SEQ])
                S.done(copy(wT[:, :], b[:, 2 * P:3 * P]))
                b = S.take()
                copy(osb[:, 0, :], b[:, 0:P])
                S.done(copy(state[:, :], b[:, P:2 * P]))
                b = S.take()
                S.done(tt(unew[:, 1, :], unew[:, 1, :], b[:, 0:P], ALU.subtract))
                b = S.take()
                S.done(copy(osb[:, 1, :], b[:, 0:P]))
                S.settle()
                for n in range(2):
                    step(dve.tensor_tensor_reduce(qn[:, n, :], osb[:, n, :], osb[:, n, :], 1.0, 0.0,
                                                  ALU.mult, ALU.add, dss[:, 8 + n:9 + n]))
                ask.send(ts(dss[:, 8:10], dss[:, 8:10], 1.0 / P, EPS_RMS, ALU.mult, ALU.add))
                from_a.get()
                step(dve.reciprocal(dss[:, 14:16], dss[:, 12:14]))
                for n in range(2):
                    m = stt(osb[:, n, :], osb[:, n, :], dss[:, 14 + n:15 + n], dnw[:, :], ALU.mult, ALU.mult)
                step(m)
                step(tt(mix[:, :, bass.ds(i * P + AT_W, P)], osb[:, :, :], dz[:, :, :], ALU.mult))

            to_tensor.send(ts(mix[:, 0, 0:1], mix[:, 0, 0:1], 1.0, None, ALU.mult))
            from_features(XT, False)

            def gated_rows(c, t):
                cols = slice(512 * c, 512 * c + 512)
                b = G.take(t == XT - 1)
                G.done(tt(xn[:, t, cols], b[:, :], gateb[:, 0, cols], ALU.mult))
                G.settle()
                step(tt(tok[:, t, cols], tok[:, t, cols], xn[:, t, cols], ALU.add))

            for c in range(2):
                for t in range(XT):
                    gated_rows(c, t)

            scales(0, 3, 8, (0,))
            to_tensor.send(rms_rows())
            from_features(XT, True)
            b = S.take()
            S.done(tt(lg[:, :, :], b[:, 0:2 * EXPERTS].rearrange("p (t n) -> p t n", t=2),
                      brow[:, :].unsqueeze(1).to_broadcast([P, 2, EXPERTS]), ALU.add))
            S.settle()
            dve.memset(m8[:, :, :], 0.0)
            dve.memset(gate[:, :, EXPERTS:EXPERTS + 1], 0.0)
            step(dve.memset(pos[:, :, EXPERTS:EXPERTS + 1], -1.0))
            for t in range(XT):
                m = dve.max(m8[:, t, :], lg[:, t, :])
            step(m)
            ask.send(ts(rs[:, 0:2], m8[:, :, 0], -1.0, None, ALU.mult))
            fourth = lambda t: m8[:, t, TOP_K - 1:TOP_K]
            for t in range(XT):
                ts(eq[:, t, :], lg[:, t, :], fourth(t), None, ALU.is_equal)
                m = ts(sel[:, t, :], lg[:, t, :], fourth(t), None, ALU.is_gt)
            step(m)
            dve.tensor_reduce(rs[:, 2:4], sel[:, :, :], AX, ALU.add)
            step(copy(cum[:, 0, :, :], eq[:, :, :]))
            for l in range(5):
                s, d, w = cum[:, l % 2, :, :], cum[:, (l + 1) % 2, :, :], 1 << l
                copy(d[:, :, 0:w], s[:, :, 0:w])
                step(tt(d[:, :, w:EXPERTS], s[:, :, w:EXPERTS], s[:, :, 0:EXPERTS - w], ALU.add))
            step(ts(rs[:, 2:4], rs[:, 2:4], -1.0, float(TOP_K), ALU.mult, ALU.add))
            for t in range(XT):
                m = stt(eq[:, t, :], cum[:, 1, t, :], rs[:, 2 + t:3 + t], eq[:, t, :], ALU.is_le, ALU.mult)
            step(m)
            to_tensor.send(tt(sel[:, :, :], sel[:, :, :], eq[:, :, :], ALU.add))
            dve.wait_ge(to_pe, to_tensor.c.at())
            from_a.get()
            step(tt(eg[:, :, :], eg[:, :, :], sel[:, :, :], ALU.mult))
            step(dve.tensor_reduce(rs[:, 4:6], eg[:, :, :], AX, ALU.add))
            step(dve.reciprocal(rs[:, 6:8], rs[:, 4:6]))
            for t in range(XT):
                m = ts(gate[:, t, 0:EXPERTS], eg[:, t, :], rs[:, 6 + t:7 + t], None, ALU.mult)
            step(m)
            b = S.take()
            copy(cntf[:, :], b[:, 2 * EXPERTS:3 * EXPERTS])
            bp = b[:, 0:2 * EXPERTS].rearrange("p (t n) -> p t n", t=2)
            S.done(stt(pos[:, :, 0:EXPERTS], bp, 1.0, sel[:, :, :], ALU.add, ALU.mult))
            S.settle()
            step(ts(pos[:, :, 0:EXPERTS], pos[:, :, 0:EXPERTS], -1.0, None, ALU.add))
            step(dve.tensor_reduce(rs[:, 8:9], cntf[:, :], AX, ALU.max))
            copy(cnt_i[:, :], rs[:, 8:9]).then_inc(count_ready, 1)
            to_tensor.send(ts(gate[:, 0, EXPERTS:EXPERTS + 1], gate[:, 0, EXPERTS:EXPERTS + 1], 0.0, None, ALU.mult))
            dve.memset(rs[:, 9:10], 0.0).then_inc(b2_go, 1)
            b = S.take()
            S.done(copy(gT[0:EXPERTS, :], b[0:EXPERTS, 0:SEQ]))
            for t in range(XT):
                for c in range(2):
                    b = S.take()
                    S.done(copy(yacc[:, t, 512 * c:512 * c + 512], b[:, :]))
            S.settle()

            def experts(G, S, A, M, ask, from_a, to_tensor, step, slot0, arrived, b1_done):
                uses = Count()
                freed = Post(dve, b1_done)

                def prepare(e, parity):
                    copy(pg[:, 0, parity, :], pos[:, :, bass.ds(e, 1)].rearrange("p t a -> p (t a)"))
                    step(copy(pg[:, 1, parity, :], gate[:, :, bass.ds(e, 1)].rearrange("p t a -> p (t a)")))
                    for t in range(XT):
                        ts(OH[:, t, :], iota[:, slot0:slot0 + P], pg[:, 0, parity, t:t + 1], None, ALU.is_equal)
                        m = ts(GD[:, parity, t, :], iota[:, slot0:slot0 + P], pg[:, 0, parity, t:t + 1],
                               pg[:, 1, parity, t:t + 1], ALU.is_equal, ALU.mult)
                    to_tensor.send(m)

                def gathered():
                    for half in range(2):
                        b = A.take()
                        for n in range(4):
                            k = 4 * half + n
                            m = ts(xg[:, k, :], b[:, n * P:n * P + P], scol[:, 0, k:k + 1], scol[:, 1, k:k + 1],
                                   ALU.mult, ALU.add)
                        A.done(m)

                def biased(c, e):
                    for n, dst in enumerate((act_h, up_h)):
                        b = G.take(True)
                        G.done(tt(dst[:, 512 * c:512 * c + 512], b[:, :],
                                  b1b[:, e, F_EXP * n + 512 * c:F_EXP * n + 512 * c + 512], ALU.add))
                        yield n

                def swiglu(c):
                    s = slice(512 * c, 512 * c + 512)
                    G.settle()
                    ask.send(ts(act_h[:, s], act_h[:, s], 7.0, None, ALU.min))
                    m = ts(up_h[:, s], up_h[:, s], 7.0, -7.0, ALU.min, ALU.max)
                    if c == 0:
                        step(m)
                    else:
                        freed.send(m)
                        dve.wait_ge(b1_done, freed.c.at())
                    dve.wait_ge(ask.sem, ask.c.at())
                    step(stt(up_h[:, s], up_h[:, s], 1.0, act_h[:, s], ALU.add, ALU.mult))
                    from_a.get()
                    to_tensor.send(tt(act_h[:, s], up_h[:, s], sig[:, s], ALU.mult))

                def turned(c):
                    b = S.take()
                    S.done(copy(aT[:, 4 * c:4 * c + 4, :].rearrange("p a b -> p (a b)"), b[:, :]))

                prepare(0, 0)
                gathered()
                with turns(dve, EXPERTS // 2, {G.c: 12, G.panels: 12, S.c: 4, A.c: 4, M.c: 10, to_tensor.c: 6,
                                               ask.c: 4, from_a.c: 4, uses: 2, freed.c: 2, step.c: 8}) as i:
                    for e in range(2):
                        dve.wait_ge(arrived[uses.n % 2], uses.dma())
                        uses.n += 1
                        for _ in biased(0, e):
                            pass
                        swiglu(0)
                        prepare(i * 2 + (e + 1), 1 - e)
                        for n in biased(1, e):
                            if n == 0:
                                turned(0)
                        swiglu(1)
                        gathered()
                        b = M.take()
                        M.done(copy(comb[:, :, :].rearrange("p a b -> p (a b)"), b[:, 0:SEQ]))
                        turned(1)
                        for c in range(2):
                            b = G.take(True)
                            G.done(copy(ysb[:, 512 * c:512 * c + 512], b[:, :]))
                        for c in range(2):
                            for t in range(XT):
                                b = M.take()
                                s = slice(512 * c, 512 * c + 512)
                                M.done(tt(yacc[:, t, s], yacc[:, t, s], b[:, :], ALU.add))
                    M.settle()

            experts(G, S, A, M, ask, from_a, to_tensor, step, 0, b1_in, b1_used)
            dve.wait_ge(count_ready, 1)
            most = dve.value_load(cnt_i[0:1, 0:1], min_val=0, max_val=SEQ)
            with dve.If(most > P):
                for pair in (o_gemm, o_side, o_att, o_mix):
                    dve.sem_inc(pair.free, 2)
                experts(GemmReader(dve, o_gemm, o_done), Reader(dve, o_side), Reader(dve, o_att),
                        Reader(dve, o_mix), Post(dve, o_to_act), Post(dve, o_from_act), Post(dve, o_to_pe),
                        Chain(dve, o_dve), P, o_b1, o_b1_used)

            spread_gates(0, 5, (0,))
            for t in range(XT):
                m = tt(yacc[:, t, :], yacc[:, t, :], gateb[:, 0, :], ALU.mult)
            step(m)
            for t in range(XT):
                m = tt(tok[:, t, :], tok[:, t, :], yacc[:, t, :], ALU.add)
            step(m)
            variance(XT, lambda t: tok[:, t, :], False, EPS_RMS)
            dve.wait_ge(rows_in, 16)
            for t in range(XT):
                m = stt(tok[:, t, :], tok[:, t, :], rstd[:, t:t + 1], lnrow[:, 0, :], ALU.mult, ALU.mult)
            m.then_inc(rows_used, 1)
            dve.wait_ge(rows_used, 1)

            norms = [0]

            def layer_norm(tiles, last=False):
                for t in range(tiles):
                    m = tt(yacc[:, t, :], yacc[:, t, :], gateb[:, t // 2, :], ALU.mult)
                step(m)
                for t in range(tiles):
                    m = stt(tok[:, t, :], tok[:, t, :], ALPHA, yacc[:, t, :], ALU.mult, ALU.add)
                step(m)
                variance(tiles, lambda t: tok[:, t, :], True, EPS_LN)
                dve.wait_ge(rows_in, 16 + 32 * (norms[0] + 1))
                norms[0] += 1
                for t in range(tiles):
                    m = ts(tok[:, t, :], tok[:, t, :], mv[:, t, 0:1], rstd[:, t:t + 1], ALU.subtract, ALU.mult)
                step(m)
                for n, op in enumerate((ALU.mult, ALU.add)):
                    for t in range(tiles):
                        m = tt(tok[:, t, :], tok[:, t, :], lnrow[:, n, :], op)
                    if n == 0:
                        step(m)
                m.then_inc(out_ready if last else rows_used, 1)
                if not last:
                    dve.wait_ge(rows_used, norms[0] + 1)

            ask.send(copy(lgam[:, :], lgam[:, :]))
            from_a.get()
            step(ts(lgam[:, :], lgam[:, :], -1.0, None, ALU.mult))
            dve.memset(yacc[:, :, :], 0.0)
            ts(dpos[:, :, :], dist, 0.0, None, ALU.max)
            step(ts(dneg[:, :, :], dist, -1.0, 0.0, ALU.mult, ALU.max))
            scales(1, 0, None, (1, 2))
            to_tensor.send(dve.memset(idle[:, 2:3], 0.0))
            dve.wait_ge(to_pe, to_tensor.c.at())
            from_features(4, True)
            with turns(dve, RET_HEADS, {**per_gemm(20, 4), S.c: 6, A.c: 6, M.c: 4, ask.c: 3, from_a.c: 3,
                                        to_tensor.c: 2, step.c: 11}) as i:
                copy(lgs[:, 0:1], lgam[:, bass.ds(i, 1)])
                step(copy(lgs[:, 1:2], lgam[:, bass.ds(i + RET_HEADS, 1)]))
                ts(lgx[:, 0:1], lgs[:, 1:2], -1.0, None, ALU.mult)
                ask.send(ts(lgs[:, 2:4], lgs[:, 0:2], float(SEQ), None, ALU.mult))
                for u in range(4):
                    b = G.take(u == 3)
                    G.done(copy(rqk[:, u, :], b[:, :]))
                G.settle()
                for n in range(2):
                    b = S.take()
                    S.done(tt(ro[:, n, :].rearrange("p (a b) -> p a b", a=2), b[:, :].rearrange("p (a b) -> p a b", a=2),
                              rope[:, :, 1, :], ALU.mult))
                    S.settle()
                    step(tt(rqk[:, 2 * n:2 * n + 2, 0:SEQ], rqk[:, 2 * n:2 * n + 2, 0:SEQ], rope[:, :, 0, :], ALU.mult))
                    m = tt(rqk[:, 2 * n:2 * n + 2, 0:SEQ], rqk[:, 2 * n:2 * n + 2, 0:SEQ],
                           ro[:, n, :].rearrange("p (a b) -> p a b", a=2), ALU.add)
                    step(m)
                from_a.get()
                stt(Wd[:, :, :], dist, 0.0, Wd[:, :, :], ALU.is_ge, ALU.mult)
                step(stt(We[:, :, :], dist, 0.0, We[:, :, :], ALU.is_le, ALU.mult))
                step(tt(Wd[:, :, :], Wd[:, :, :], We[:, :, :], ALU.add))
                to_tensor.send(tt(Wc[:, :, :], Wc[:, :, :], rtmp[:, :, :], ALU.add))
                dve.wait_ge(to_pe, to_tensor.c.at())
                for dst in (rv, rg):
                    for t in range(4):
                        b = G.take(t == 3)
                        m = copy(dst[:, t, :], b[:, :])
                        G.done(m)
                G.settle()
                ask.send(copy(lgs[:, 0:1], lgs[:, 0:1]))
                for n in range(6):
                    b = A.take()
                    w = Wc[:, n - 2, :] if n in (2, 3) else Wd[:, n % 2, :]
                    A.done(stt(rsT[:, n, :], b[:, 0:SEQ], 1.0 / 16, w, ALU.mult, ALU.mult))
                for t in range(4):
                    b = M.take()
                    M.done(copy(ro[:, t, :], b[:, :]))
                M.settle()
                from_a.get()
                variance(4, lambda t: ro[:, t, :], True, EPS_LN, width=512)
                for t in range(4):
                    m = ts(ro[:, t, :], ro[:, t, :], mv[:, t, 0:1], rstd[:, t:t + 1], ALU.subtract, ALU.mult)
                step(m)
                for t in range(4):
                    m = tt(ro[:, t, :], ro[:, t, :], rg[:, t, :], ALU.mult)
                to_tensor.send(m)
                for k in range(4):
                    b = S.take()
                    S.done(copy(roT[:, k, :], b[:, :]))
                for c in range(2):
                    for t in range(4):
                        s = slice(512 * c, 512 * c + 512)
                        b = G.take(c == 1 and t == 3)
                        G.done(tt(yacc[:, t, s], yacc[:, t, s], b[:, :], ALU.add))
                G.settle()
            spread_gates(1, 2, (1, 2))
            layer_norm(4)

            def mlp(layer, conds, last=False):
                tiles = 2 * len(conds)
                width = tiles * P
                scales(layer, 3, None, conds)
                to_tensor.send(dve.memset(idle[:, 2:3], 0.0))
                dve.wait_ge(to_pe, to_tensor.c.at())
                step(dve.memset(yacc[:, 0:tiles, :], 0.0))
                from_features(tiles, True)
                with turns(dve, 4, {**per_gemm(8 + 2 * tiles, 4), step.c: 7, to_tensor.c: 1}) as i:
                    for u in range(8):
                        b = G.take(u % 4 == 3)
                        G.done(ts(mtmp[:, 0:width], b[:, 0:width], 0.0, None, ALU.max))
                        G.settle()
                        m = tt(hid[:, u, 0:width], mtmp[:, 0:width], mtmp[:, 0:width], ALU.mult)
                        if u < 7:
                            step(m)
                        else:
                            to_tensor.send(m)
                    for c in range(2):
                        for t in range(tiles):
                            s = slice(512 * c, 512 * c + 512)
                            b = G.take(t == tiles - 1)
                            G.done(tt(yacc[:, t, s], yacc[:, t, s], b[:, :], ALU.add))
                    G.settle()
                spread_gates(layer, 5, conds)
                layer_norm(tiles, last)

            mlp(1, (1, 2))

            scales(2, 0, None, (1, 2))
            dve.memset(idle[:, 1:2], 0.0).then_inc(nat_go, 1)
            to_tensor.send(dve.memset(idle[:, 2:3], 0.0))
            dve.wait_ge(to_pe, to_tensor.c.at())
            from_features(4, True)
            freed = Post(dve, bias_used)
            with turns(dve, NAT_GROUPS // 2, {**per_gemm(6, 2), S.c: 16, A.c: 16, M.c: 16, ask.c: 16, freed.c: 8,
                                              step.c: 40}) as i:
                for g in range(2):
                    b = G.take()
                    G.done(ts(nq[:, :], b[:, 0:SEQ], NAT_HD ** -0.5, None, ALU.mult))
                    b = G.take()
                    G.done(copy(nk[:, :], b[:, :]))
                    b = G.take(True)
                    G.done(copy(nv[:, :, :].rearrange("p a b -> p (a b)"), b[:, :]))

                    def soften(n):
                        p = n % 2
                        b = A.take()
                        m = tt(ns[:, p, 0:SEQ].rearrange("p (a b) -> p a b", a=4),
                               b[:, 0:SEQ].rearrange("p (a b) -> p a b", a=4),
                               natmask.unsqueeze(1).to_broadcast([P, 4, GRID_W]), ALU.add)
                        if n % 2:
                            freed.send(m)
                            dve.wait_ge(bias_used, freed.c.at())
                        else:
                            step(m)
                        A.done(copy(ns[:, p, SEQ:2 * SEQ], b[:, SEQ:2 * SEQ]))
                        A.settle()
                        step(dve.tensor_reduce(nmax[:, p:p + 1], ns[:, p, :], AX, ALU.max))
                        ask.send(ts(nneg[:, p:p + 1], nmax[:, p:p + 1], -1.0, None, ALU.mult))

                    soften(0)
                    for n in range(8):
                        if n < 7:
                            soften(n + 1)
                        b = M.take()
                        M.done(copy(npT[:, :, :].rearrange("p a b -> p (a b)"), b[:, :]))
                        step(dve.reciprocal(nrec[:, n % 2:n % 2 + 1], nden[:, n % 2:n % 2 + 1]))
                        b = S.take()
                        S.done(ts(no[:, n % 2, bass.ds(i * 256 + (g * P + NAT_HD * (n // 2)), NAT_HD)], b[:, 0:NAT_HD],
                                  nrec[:, n % 2:n % 2 + 1], None, ALU.mult))
            S.settle()
            to_tensor.send(dve.memset(idle[:, 2:3], 0.0))
            dve.wait_ge(to_pe, to_tensor.c.at())
            from_features(XT, False)
            for c in range(2):
                for t in range(XT):
                    b = G.take(t == XT - 1)
                    G.done(copy(yacc[:, t, 512 * c:512 * c + 512], b[:, :]))
            G.settle()
            spread_gates(2, 2, (1,))
            layer_norm(2)
            mlp(2, (1,), last=True)


def kernel(**inputs):
    import concourse.bacc as _bacc
    from concourse.bass_utils import run_bass_kernel_spmd as _run

    x = {n: np.asarray(v) for n, v in inputs.items()}
    nc = _bacc.Bacc("TRN2", target_bir_lowering=False, num_devices=1)

    def cut(w, c0, width=512, r0=0):
        v = w[r0:r0 + D, c0:c0 + width]
        return v.reshape(KT, P, width).transpose(1, 0, 2).reshape(P, -1)

    def heads(w, firsts, i, width):
        return np.concatenate([w[:, f + i * width:f + (i + 1) * width] for f in firsts], axis=1)

    w_in = x["w_in"][0]
    pa = [cut(x["w_ada"][0], 512 * j) for j in range(12)]
    pa += [cut(x["ada_w_2"][l], 512 * j) for l in range(2) for j in range(12)]
    for i in range(DN_HEADS):
        three = heads(w_in, (0, 512, 1024), i, P)
        pa.append(cut(np.concatenate([three, np.zeros_like(three[:, 0:P])], axis=1), 0))
        pa.append(cut(heads(w_in, (1536, 2048, 2560, 3072), i, P), 0))
    pa += [cut(x["w_out"][0], 512 * c) for c in range(2)]
    pe = np.empty((EXPERTS, 6, P, KT * 512), np.float32)
    for e in range(EXPERTS):
        for j, c0 in enumerate((0, 1024, 512, 1536)):
            pe[e, j] = cut(x["w1"][0, e], c0)
        for c in range(2):
            pe[e, 4 + c] = cut(x["w2"][0, e], 512 * c)
    pb = []
    rw, ro = x["ret_w_in_2"][0], x["ret_w_o_2"][0]
    for i in range(RET_HEADS):
        pb += [cut(heads(rw, (0, 1024), i, 256), 0), cut(rw, 2048 + 512 * i), cut(rw, 4096 + 512 * i)]
        v = ro[512 * i:512 * i + 512].reshape(4, P, 2, 512)
        pb.append(v.transpose(1, 2, 0, 3).reshape(P, -1))

    def mlp_panels(l):
        r = []
        for i in range(4):
            r += [cut(x["mlp_w1_2"][l], D * i + 512 * j) for j in range(2)]
            r += [cut(x["mlp_w2_2"][l], 512 * j, r0=D * i) for j in range(2)]
        return r

    pb += mlp_panels(0)
    pn = [cut(heads(x["nat_w_in_2"][0], (0, D, 2 * D), i, P), 0, width=3 * P) for i in range(NAT_GROUPS)]
    pc = [cut(x["nat_w_o_2"][0], 512 * c) for c in range(2)] + mlp_panels(1)
    rows = lambda v: v.reshape(-1, P)
    par = np.zeros((3, P, P), np.float32)
    one = np.concatenate([rows(x["c"]), rows(x["c_2"]), rows(x["c_ctx_2"])])
    par[0, 0:24] = one
    par[1, 0:96] = rows(x["ada_b_2"])
    taps = x["conv_w"][0].reshape(4, 3, DN_HEADS, P).transpose(2, 0, 1, 3)
    par[2, 0:112] = np.concatenate([rows(x["b_ada"]), rows(x["norm1_w"]), rows(x["norm2_w"]), rows(taps)])
    small = np.concatenate([cut(w_in, 3584, width=8), cut(x["w_router"][0], 0, width=EXPERTS)], axis=1)
    rpb = np.zeros((NAT_HEADS, 15, RPB_W), np.float32)
    rpb[:, :, 48:79] = x["nat_rpb_2"][0]

    arrays = {
        "x": x["x"], "ctx_2": x["ctx_2"], "panels_a": np.stack(pa), "panels_e": pe.reshape(-1, P, KT * 512),
        "panels_b": np.stack(pb), "panels_n": np.stack(pn), "panels_c": np.stack(pc),
        "consts": constants(), "params": par.reshape(3 * P, P), "smallw": small, "rpb": rpb,
        "A_log": x["A_log"], "dt_bias": x["dt_bias"], "dn_norm_w": x["dn_norm_w"], "b_router": x["b_router"],
        "ret_decay": x["ret_decay_2"].reshape(8), "b1": x["b1"][0], "b2": x["b2"], "final_norm_w": x["final_norm_w"],
        "ln_g_2": x["ln_g_2"], "ln_b_2": x["ln_b_2"],
    }
    arrays = {n: np.ascontiguousarray(v) for n, v in arrays.items()}
    a = {n: nc.dram_tensor("in_" + n, v.shape, mybir.dt.from_np(v.dtype), kind="ExternalInput").ap()
         for n, v in arrays.items()}
    out = nc.dram_tensor("out_0", (1, SEQ, D), F32, kind="ExternalOutput").ap()
    program(nc, a, out)
    r = _run(nc, [{"in_" + n: v for n, v in arrays.items()}], core_ids=[0])
    return r.results[0]["out_0"]
```

```python
from contextlib import ExitStack, contextmanager

import numpy as np

import concourse.bass as bass
from concourse import mybir

F32 = mybir.dt.float32
I32 = mybir.dt.int32
ALU = mybir.AluOpType
ACT = mybir.ActivationFunctionType
AX = mybir.AxisListType.X

P = 128
D = 1024
KT = D // P
SEQ = 256
XT = SEQ // P
AT_W = 512
DN_HEADS = 4
EXPERTS = 32
TOP_K = 4
F_EXP = 1024
RET_HEADS = 4
RET_V = 512
MLP_HID = 4096
NAT_HEADS = 32
NAT_HD = 32
NAT_GROUPS = NAT_HEADS * NAT_HD // P
GRID_W = 64
REACH = 2 * GRID_W
EPS_RMS = 1e-6
EPS_LN = 1e-5
ALPHA = (2.0 * 2) ** 0.25
RPB_W = 2 * GRID_W - 1
NEG = -1e30
LEVELS = 7
CAP = 64
LIST = 16


class Count:

    def __init__(self, start=0):
        self.n, self.turn, self.per, self.start = start, None, 0, 0
        self.name = ''

    def at(self, k=0):
        return self.n + k if self.turn is None else self.turn * self.per + (self.n + k)

    def dma(self, slots=2, each=16):
        use = (self.n // slots + 1) * each
        return use if self.turn is None else self.turn * (self.per * each // slots) + use


@contextmanager
def turns(eng, number, per):
    with eng.Fori(0, number) as i:
        for c, step in per.items():
            c.turn, c.per, c.start = i, step, c.n
        yield i
        for c, step in per.items():
            assert c.n - c.start == step, ("a turn moves the count by", c.n - c.start, "not", step, c.name)
    for c, step in per.items():
        c.turn, c.n = None, c.start + number * step


class Pair:

    def __init__(self, banks, full, free):
        self.banks, self.full, self.free = banks, full, free


class Filler:
    def __init__(self, pe, pair):
        self.pe, self.pair, self.c = pe, pair, Count()

    def open(self):
        self.pe.wait_ge(self.pair.free, self.c.at(1))
        return self.pair.banks[self.c.n % 2]

    def close(self, last):
        last.then_inc(self.pair.full, 1)
        self.c.n += 1

    def read(self, ago=0):
        self.pe.wait_ge(self.pair.free, self.c.at(2 - ago))


class Reader:
    def __init__(self, eng, pair):
        self.eng, self.pair, self.c = eng, pair, Count()

    def take(self):
        self.eng.wait_ge(self.pair.full, self.c.at(1))
        return self.pair.banks[self.c.n % 2]

    def done(self, last):
        last.then_inc(self.pair.free, 1)
        self.c.n += 1

    def settle(self):
        self.eng.wait_ge(self.pair.free, self.c.at(2))


class GemmFiller(Filler):

    def __init__(self, pe, pair, slots, landed, half0_used, panel_done):
        super().__init__(pe, pair)
        self.others, self.panels = Count(), Count()
        self.slots, self.landed, self.half0_used, self.panel_done = slots, landed, half0_used, panel_done
        self.seen = set()

    def half(self, h):
        slot = self.panels.n % len(self.slots)
        if h not in self.seen:
            self.pe.wait_ge(self.landed[slot][h], self.panels.dma(len(self.slots)))
            self.seen.add(h)
        return self.slots[slot][:, 4 * h:4 * h + 4, :]

    def close(self, last, ends_panel=False):
        last.then_inc(self.panel_done if ends_panel else self.pair.full, 1)
        self.c.n += 1
        if ends_panel:
            self.panels.n += 1
            self.seen = set()
        else:
            self.others.n += 1

    def product(self, lhs, rhs, ends_panel=False, depth=KT, dst=lambda b: b[:, :]):
        b = self.open()
        for k in range(depth):
            v = self.half(k // 4)[:, k % 4, :]
            m = self.pe.matmul(dst(b), lhs(k, v), rhs(k, v), start=(k == 0), stop=(k == depth - 1))
            if ends_panel and k == 3:
                m.then_inc(self.half0_used, 1)
        self.close(m, ends_panel)

    def split_product(self, lhs, parts, depth=KT):
        b = self.open()
        rows, cols = P // parts, 512 // parts
        for k in range(depth):
            v = self.half(k // 4)[:, k % 4, :]
            for s in range(parts):
                m = self.pe.matmul(b[s * rows:(s + 1) * rows, 0:cols], lhs(k), v[:, s * cols:(s + 1) * cols],
                                   start=(k == 0), stop=(k == depth - 1))
            if k == 3:
                m.then_inc(self.half0_used, 1)
        self.close(m, True)


class GemmReader:

    def __init__(self, eng, pair, panel_done, credit=0):
        self.eng, self.pair, self.panel_done, self.credit = eng, pair, panel_done, credit
        self.c, self.others, self.panels = Count(), Count(), Count()

    def take(self, ends_panel=False):
        if ends_panel:
            self.eng.wait_ge(self.panel_done, self.panels.at(1 + self.credit))
            self.panels.n += 1
        else:
            self.eng.wait_ge(self.pair.full, self.others.at(1))
            self.others.n += 1
        return self.pair.banks[self.c.n % 2]

    def done(self, last):
        last.then_inc(self.pair.free, 1)
        self.c.n += 1

    def settle(self):
        self.eng.wait_ge(self.pair.free, self.c.at(2))


class Chain:

    def __init__(self, eng, sem):
        self.eng, self.sem, self.c = eng, sem, Count()

    def __call__(self, ins):
        ins.then_inc(self.sem, 1)
        self.c.n += 1
        self.eng.wait_ge(self.sem, self.c.at())


class Post:

    def __init__(self, eng, sem):
        self.eng, self.sem, self.c = eng, sem, Count()

    def send(self, ins):
        ins.then_inc(self.sem, 1)
        self.c.n += 1

    def get(self, k=1):
        self.c.n += k
        self.eng.wait_ge(self.sem, self.c.at())


CONSTS, CONST_COLS = {}, 0
for _name, _shape in (("ident", (P,)), ("upper", (P,)), ("strict", (P,)), ("lvl", (LEVELS, P)),
                      ("lcount", (3 * P,)), ("swap", (P,)), ("anti", (P,)), ("dist", (2, SEQ)),
                      ("rope", (2, 2, SEQ)), ("natmask", (GRID_W,)), ("iota", (P,)), ("tab_e", (3 * EXPERTS,)), ("tab_s", (3 * EXPERTS,)),
                      ("tab_j", (LIST,))):
    CONSTS[_name] = (CONST_COLS, _shape)
    CONST_COLS += int(np.prod(_shape))


def constants():
    c = {}
    r = np.arange(P)
    c["ident"] = r[:, None] == r[None, :]
    c["upper"] = r[:, None] <= r[None, :]
    c["strict"] = r[:, None] < r[None, :]
    c["lvl"] = np.stack([((r[None, :] >> (l + 1)) == (r[:, None] >> (l + 1)))
                         & ((r[None, :] >> l) % 2 == 1) & ((r[:, None] >> l) % 2 == 0)
                         for l in range(LEVELS)], axis=1)
    t, s = np.arange(SEQ)[:, None], np.arange(SEQ)[None, :]
    d = t - s
    seen = ((d >= 0) & (d <= 128)) * 1 + ((d >= 0) & (d % 4 == 0)) + ((d >= 0) & (d % 16 == 0))
    lc = np.where(seen > 0, np.log(np.maximum(seen, 1)), NEG)
    c["lcount"] = np.concatenate([lc[0:P, 0:P], lc[P:SEQ, :]], axis=1)
    c["swap"] = r[:, None] == (r[None, :] + 64) % P
    c["anti"] = (r[:, None] // 64 == r[None, :] // 64) & (r[:, None] % 64 == 63 - r[None, :] % 64)
    c["dist"] = np.stack([s[0][None, :] - (r[:, None] + P * n) for n in range(2)], axis=1)
    inv = (1.0 / (10000.0 ** (np.arange(0, P, 2, dtype=np.float32) / P))).astype(np.float32)
    pos = np.arange(SEQ)
    ang = [inv[r % 64][:, None] * x[None, :].astype(np.float32) for x in (pos // GRID_W, pos % GRID_W)]
    sign = np.where(r < 64, -1.0, 1.0)[:, None]
    c["rope"] = np.stack([np.stack([np.cos(x), np.sin(x) * sign], axis=1) for x in ang], axis=1)
    q, k = (r % GRID_W)[:, None], np.arange(GRID_W)[None, :]
    start = np.clip(q - 8, 0, GRID_W - 16)
    c["natmask"] = np.where((k >= start) & (k < start + 16), 0.0, NEG)
    c["iota"] = np.broadcast_to(r[None, :] % CAP, (P, P))
    c["tab_e"] = np.broadcast_to(np.tile(np.arange(EXPERTS), 3)[None, :], (P, 3 * EXPERTS))
    c["tab_s"] = np.broadcast_to(np.repeat(np.arange(1, 4) * CAP, EXPERTS)[None, :], (P, 3 * EXPERTS))
    c["tab_j"] = np.broadcast_to(np.arange(1, LIST + 1)[None, :], (P, LIST))
    return np.concatenate([c[n].reshape(P, -1).astype(np.float32) for n in CONSTS], axis=1)


def program(nc, a, out, dbg=None):
    ctx = ExitStack()
    with ctx:
        def sb(name, *shape, dt=F32):
            return ctx.enter_context(nc.sbuf_tensor(name, [P, *shape], dt))

        def sem(name):
            return ctx.enter_context(nc.semaphore(name))

        bank = [ctx.enter_context(nc.psum_tensor(f"bank{i}", [P, 512], F32)) for i in range(8)]

        ring = sb("ring", 2, KT, 512)
        tok = sb("tok", 4, D)
        xn = sb("xn", XT, D)
        hT = sb("hT", KT, 512)
        hid = sb("hid", KT, 512)
        yacc = sb("yacc", 4, D)
        gateb = sb("gateb", 2, D)
        lnrow = sb("lnrow", 2, D)
        cst = sb("cst", CONST_COLS)

        def const(name):
            first, shape = CONSTS[name]
            v = cst[:, first:first + int(np.prod(shape))]
            if len(shape) == 2:
                return v.rearrange("p (a b) -> p a b", a=shape[0])
            if len(shape) == 3:
                return v.rearrange("p (a b c) -> p a b c", a=shape[0], b=shape[1])
            return v

        ident, upper, strict, lvl = const("ident"), const("upper"), const("strict"), const("lvl")
        lcount, swap, anti, dist = const("lcount"), const("swap"), const("anti"), const("dist")
        rope, natmask, iota = const("rope"), const("natmask"), const("iota")
        tab_e, tab_s, tab_j = const("tab_e"), const("tab_s"), const("tab_j")
        ones = sb("ones", P)
        params = sb("params", 3, P)
        csil = sb("csil", KT, 32)
        biascol = sb("biascol", 144)
        parcol = sb("parcol", 64)
        convcol = sb("convcol", DN_HEADS, 12)
        modcol = sb("modcol", 144, 3)
        arow = sb("arow", 2, P)
        scol = sb("scol", 4, KT)
        diag = sb("diag", KT, P)
        stats = sb("stats", 4, 2, 6)
        mv = sb("mv", 4, 2)
        std = sb("std", 4)
        rstd = sb("rstd", 4)
        hsel = sb("hsel", 10, 2)
        gmul = sb("gmul", 4, KT)
        headp = sb("headp", 2, 4)
        dnw = sb("dnw", P)
        smallw = sb("smallw", KT * 8 + KT * EXPERTS)
        wdba = smallw[:, 0:KT * 8].rearrange("p (k n) -> p k n", k=KT)
        wr = smallw[:, KT * 8:].rearrange("p (k n) -> p k n", k=KT)
        brow = sb("brow", EXPERTS)
        lgam = sb("lgam", 8)
        idle = sb("idle", 4)
        scratch = sb("scratch", 14 * 1024)
        more_i = sb("more_i", 1, dt=I32)
        list_e = sb("list_e", LIST, dt=I32)
        list_s = sb("list_s", LIST)
        slots = [ring[:, 0], ring[:, 1]]
        wide = slots + [hT, hid]

        def carve(start, *shape):
            n = int(np.prod(shape))
            v = scratch[:, start:start + n]
            if len(shape) == 2:
                return v.rearrange("p (a b) -> p a b", a=shape[0])
            if len(shape) == 3:
                return v.rearrange("p (a b c) -> p a b c", a=shape[0], b=shape[1])
            return v

        gemm = Pair(bank[0:2], sem("gemm_full"), sem("gemm_free"))
        side = Pair(bank[2:4], sem("side_full"), sem("side_free"))
        att = Pair(bank[4:6], sem("att_full"), sem("att_free"))
        mixp = Pair(bank[6:8], sem("mix_full"), sem("mix_free"))
        landed = [[sem(f"landed_{s}{h}") for h in range(2)] for s in range(2)]
        half0_used = sem("half0_used")
        panel_done = sem("panel_done")
        consts_in = sem("consts_in")
        params_in = sem("params_in")
        tok_in = sem("tok_in")
        small_in = sem("small_in")
        dve_step = sem("dve_step")
        act_step = sem("act_step")
        act_to_pe = sem("act_to_pe")
        b2_go = sem("b2_go")
        nat_go = sem("nat_go")
        to_act = sem("to_act")
        from_act = sem("from_act")
        to_pe = sem("to_pe")
        b2_in = sem("b2_in")
        rows_in = sem("rows_in")
        rows_used = sem("rows_used")
        ones_ready = sem("ones_ready")
        count_ready = sem("count_ready")
        bias_in = [sem("bias_in0"), sem("bias_in1")]
        bias_used = sem("bias_used")
        out_ready = sem("out_ready")
        out_done = sem("out_done")
        def expert_sems(x, n):
            return dict(
                gemm=Pair(bank[0:2], sem(x + "gemm_full"), sem(x + "gemm_free")),
                side=Pair(bank[2:4], sem(x + "side_full"), sem(x + "side_free")),
                att=Pair(bank[4:6], sem(x + "att_full"), sem(x + "att_free")),
                mix=Pair(bank[6:8], sem(x + "mix_full"), sem(x + "mix_free")),
                landed=[[sem(f"{x}landed_{s}{h}") for h in range(2)] for s in range(n)],
                half0=sem(x + "half0_used"), done=sem(x + "panel_done"), step=sem(x + "dve_step"),
                to_act=sem(x + "to_act"), from_act=sem(x + "from_act"), to_pe=sem(x + "to_pe"),
                b1=[sem(x + "b1_in0"), sem(x + "b1_in1")], b1_used=sem(x + "b1_used"))

        E = expert_sems("e_", 4)
        O = expert_sems("o_", 2)
        tiles_free = sem("tiles_free")
        further_done = sem("further_done")

        qkT = carve(0, 512)
        vtok = carve(512, 2, P)
        cin = carve(768, 3, 260)
        cy = carve(1552, 3, SEQ)
        cs = carve(2320, 3, SEQ)
        dz = carve(3088, 2, P)
        qkv = carve(3344, 6, P)
        qn = carve(4112, 2, P)
        kn = carve(4368, 2, P)
        kb = carve(4624, 2, P)
        vb = carve(4880, 2, P)
        kbg = carve(5136, P)
        qd = carve(5264, P)
        kd = carve(5392, P)
        featT = carve(5520, 7, P)
        decay = carve(6416, 2, P)
        LT = carve(6672, 2, P)
        IT = carve(6928, 2, P)
        LM = carve(7184, 2, P)
        TU = carve(7440, 4, P)
        P1 = carve(7952, 2, P)
        unew = carve(8208, 2, P)
        wT = carve(8464, P)
        state = carve(8592, P)
        osb = carve(8720, 2, P)
        gb = carve(8976, 2, P)
        cw = carve(9232, 12)
        gates = carve(9248, 10, 8)
        satt = carve(9344, 3 * P)
        pT = carve(9728, 3 * P)
        amax = carve(10112, 8)
        aden = carve(10120, 8)
        arec = carve(10128, 8)
        dss = carve(10136, 16)
        mix = hid[:, 0:4, :].rearrange("p a b -> p (a b)").rearrange("p (t n) -> p t n", t=2)
        lg = carve(0, 2, EXPERTS)
        m8 = carve(64, 2, 8)
        eq = carve(80, 2, EXPERTS)
        cum = carve(144, 2, 2, EXPERTS)
        sel = carve(272, 2, EXPERTS)
        eg = carve(336, 2, EXPERTS)
        gt = carve(400, 2, EXPERTS)
        rs = carve(464, 16)
        cntf = carve(480, EXPERTS)
        gate = carve(512, 2, EXPERTS + 1)
        pos = carve(578, 2, EXPERTS + 1)
        gT = carve(644, SEQ)
        b2sb = carve(900, D)
        flags = carve(1924, 3, EXPERTS)
        fcum = carve(2020, 2, 3 * EXPERTS)
        match = carve(2212, LIST, 3 * EXPERTS)
        match2 = carve(3748, LIST, 3 * EXPERTS)
        E0 = 5300
        pg = carve(5288, 2, 2, 2)
        OH = carve(E0, 2, CAP)
        GD = carve(E0 + 128, 2, 2, P)
        xg = carve(E0 + 640, KT, CAP)
        act_h = carve(E0 + 1152, 2, 256)
        up_h = carve(E0 + 1664, 2, 256)
        sig = carve(E0 + 2176, 2, 256)
        aT = carve(E0 + 2688, 2, 2, P)
        ysb = carve(E0 + 3200, 2, 256)
        comb = carve(E0 + 3712, 2, P)
        b1b = carve(E0 + 3968, 2, 4, 256)
        rqk = carve(0, 4, 512)
        rv = carve(2048, 4, 512)
        rg = carve(4096, 4, 512)
        dpos = carve(6144, 2, SEQ)
        dneg = carve(6656, 2, SEQ)
        Wd = carve(7168, 2, SEQ)
        Wc = carve(7680, 2, SEQ)
        We = carve(8192, 2, SEQ)
        rsT = carve(8704, 6, SEQ)
        ro = carve(10240, 4, 512)
        lgs = carve(12296, 4)
        rtmp = carve(12304, 2, SEQ)
        lgx = carve(12816, 4)
        roT = hid[:, 0:4, :]
        mtmp = carve(0, 512)
        nq = carve(0, SEQ)
        nk = carve(256, 512)
        nv = carve(768, 4, P)
        nbias = carve(1280, 2, 6, GRID_W)
        ns = carve(2048, 2, 512)
        nmax = carve(3072, 4)
        nneg = carve(3076, 4)
        nden = carve(3080, 4)
        nrec = carve(3084, 4)
        npT = carve(3088, 4, P)
        no = xn

        def param_row(src, t):
            n = src.shape[-1]
            return bass.AP(src.tensor, src.offset, [[0, P], [1, n]])

        block = ctx.enter_context(nc.Block())


        @block.sync
        def _(sp):
            panels = Count()

            def panel(src, width=512, start=False, at_slots=slots, sems=(landed, half0_used, panel_done),
                      panels=panels, credit=0):
                arrived, half0, done = sems
                slot = panels.n % len(at_slots)
                for h, used in enumerate((half0, done)):
                    if not start:
                        sp.wait_ge(used, panels.at(1 - len(at_slots) + credit))
                    dst = at_slots[slot][:, 4 * h:4 * h + 4, 0:width]
                    part = 4 * width
                    sp.dma_start(dst, src[:, h * part:(h + 1) * part].rearrange("p (k n) -> p k n", k=4))\
                        .then_inc(arrived[slot][h], 16)
                panels.n += 1

            for j in range(2):
                panel(a["panels_a"][j], start=True)
            for name, row0 in (("x", 0), ("ctx_2", 2)):
                sp.dma_start(tok[:, row0:row0 + 2, :],
                             a[name][0].rearrange("(t p) n -> p t n", p=P)).then_inc(tok_in, 16)

            def at(src, index):
                return src[bass.ds(index, 1)].rearrange("a p n -> (a p) n")

            def stream(src, first, number, **kw):
                with turns(sp, (number - first) // 2, {panels: 2}) as i:
                    for j in range(2):
                        panel(at(src, i * 2 + (first + j)), **kw)

            stream(a["panels_a"], 2, a["panels_a"].shape[0])
            per = dict(at_slots=wide, sems=(E["landed"], E["half0"], E["done"]), panels=Count())
            pe_ = a["panels_e"]
            sp.wait_ge(panel_done, panels.at())
            for j in range(2):
                panel(pe_[j], start=True, **per)
            sp.wait_ge(tiles_free, 1)
            for j in range(2, 4):
                panel(pe_[j], start=True, **per)
            with turns(sp, pe_.shape[0] // 4 - 1, {per["panels"]: 4}) as i:
                for j in range(4):
                    panel(at(pe_, i * 4 + (4 + j)), **per)
            sp.wait_ge(E["done"], per["panels"].at())
            sp.wait_ge(count_ready, 1)
            more = sp.value_load(more_i[0:1, 0:1], min_val=0, max_val=LIST - 1)
            with sp.If(more > 0):
                sp.sem_inc(O["half0"], 2)
                sp.sem_inc(O["done"], 2)
                per = dict(sems=(O["landed"], O["half0"], O["done"]), panels=Count(), credit=2)
                with turns(sp, more, {per["panels"]: 6}) as i:
                    e = sp.value_load(list_e[0:1, bass.ds(i, 1)], min_val=0, max_val=EXPERTS - 1)
                    for j in range(6):
                        panel(at(pe_, e * 6 + j), **per)
                sp.wait_ge(O["done"], per["panels"].at(2))
                sp.sem_inc(further_done, 1)
            stream(a["panels_b"], 0, a["panels_b"].shape[0])
            stream(a["panels_n"], 0, a["panels_n"].shape[0], width=3 * P)
            stream(a["panels_c"], 0, a["panels_c"].shape[0])
            sp.wait_ge(out_ready, 1)
            sp.dma_start(out[0].rearrange("(t p) n -> p t n", p=P), tok[:, 0:2, :]).then_inc(out_done, 16)
            sp.wait_ge(out_done, 16)

        @block.gpsimd
        def _(pool):
            pool.dma_start(cst[:, :], a["consts"]).then_inc(consts_in, 16)
            pool.dma_start(params[:, :, :], a["params"].rearrange("(t p) n -> p t n", p=P)).then_inc(params_in, 16)
            pool.memset(ones[:, :], 1.0).then_inc(ones_ready, 1)
            pool.memset(cin[:, :, 0:4], 0.0).then_inc(ones_ready, 1)
            pool.dma_start(smallw[:, :], a["smallw"]).then_inc(small_in, 16)
            pool.dma_start(headp[:, 0, :], param_row(a["A_log"][0], 4)).then_inc(small_in, 16)
            pool.dma_start(headp[:, 1, :], param_row(a["dt_bias"][0], 4)).then_inc(small_in, 16)
            pool.dma_start(dnw[:, :], param_row(a["dn_norm_w"][0], P)).then_inc(small_in, 16)
            pool.dma_start(brow[:, :], param_row(a["b_router"][0], EXPERTS)).then_inc(small_in, 16)
            pool.dma_start(lgam[:, :], param_row(a["ret_decay"], 8)).then_inc(small_in, 16)
            pool.dma_start(lnrow[:, 0, :], param_row(a["final_norm_w"], D)).then_inc(rows_in, 16)
            pool.wait_ge(b2_go, 1)
            pool.dma_start(b2sb[0:EXPERTS, :], a["b2"][0]).then_inc(b2_in, 16)

            b1 = a["b1"]

            def load_b1(e, parity, arrived):
                for s in range(2):
                    src = bass.AP(b1.tensor, e * (2 * F_EXP) + 256 * s, [[0, CAP], [512, 4], [1, 256]])
                    pool.dma_start(b1b[CAP * s:CAP * s + CAP, parity, :, :], src).then_inc(arrived[parity], 16)

            uses = Count()
            for p in range(2):
                load_b1(p, p, E["b1"])
                uses.n += 1
            with turns(pool, EXPERTS // 2 - 1, {uses: 2}) as i:
                for p in range(2):
                    pool.wait_ge(E["b1_used"], uses.at(-1))
                    load_b1(i * 2 + (2 + p), p, E["b1"])
                    uses.n += 1
            pool.wait_ge(E["b1_used"], uses.at())
            pool.wait_ge(count_ready, 1)
            more = pool.value_load(more_i[0:1, 0:1], min_val=0, max_val=LIST - 1)
            with pool.If(more > 0):
                pool.sem_inc(O["b1_used"], 1)
                uses = Count()
                with turns(pool, more, {uses: 1}) as i:
                    e = pool.value_load(list_e[0:1, bass.ds(i, 1)], min_val=0, max_val=EXPERTS - 1)
                    pool.wait_ge(O["b1_used"], uses.at(1))
                    load_b1(e, 0, O["b1"])
                    uses.n += 1
            for n in range(4):
                pool.wait_ge(rows_used, n + 1)
                for j, name in enumerate(("ln_g_2", "ln_b_2")):
                    pool.dma_start(lnrow[:, j, :], param_row(a[name][n // 2, n % 2], D)).then_inc(rows_in, 16)
                if n == 1:
                    uses = Count()
                    rp = a["rpb"]

                    def load_bias(uses, head, parity, start=False):
                        if not start:
                            pool.wait_ge(bias_used, uses.at(-1))
                        for b in range(2):
                            src = bass.AP(rp.tensor, head * (15 * RPB_W) + (5 - b) * RPB_W,
                                          [[1, GRID_W], [RPB_W, 6], [1, GRID_W]])
                            pool.dma_start(nbias[64 * b:64 * b + 64, parity, :, :], src)\
                                .then_inc(bias_in[parity], 16)
                        uses.n += 1

                    pool.wait_ge(nat_go, 1)
                    for p in range(2):
                        load_bias(uses, p, p, start=True)
                    with turns(pool, NAT_HEADS // 2 - 1, {uses: 2}) as i:
                        for p in range(2):
                            load_bias(uses, i * 2 + (2 + p), p)

        @block.scalar
        def _(act):
            step = Chain(act, act_step)
            asked = Post(act, to_act)
            to_dve = Post(act, from_act)
            to_tensor = Post(act, act_to_pe)

            act.wait_ge(params_in, 16)
            to_tensor.send(act.activation(params[:, 0, :], params[:, 0, :], ACT.Silu))

            def root(n, post=None):
                asked.get()
                to_dve.send(act.activation(std[:, 0:n], mv[:, 0:n, 1], ACT.Sqrt))

            root(XT)
            act.wait_ge(small_in, 96)
            asked.get()
            act.activation(gates[:, 0, :], gates[:, 0, :], ACT.Sigmoid)
            step(act.activation(gates[:, 2, :], gates[:, 2, :], ACT.Abs))
            step(act.activation(gates[:, 2, :], gates[:, 2, :], ACT.Exp, scale=-1.0))
            act.activation(headp[:, 0, :], headp[:, 0, :], ACT.Exp)
            to_dve.send(act.activation(gates[:, 3, :], gates[:, 2, :], ACT.Ln, bias=1.0))
            asked.get()
            act.activation(gates[:, 5, :], gates[:, 4, :], ACT.Exp)
            to_dve.send(act.activation(gates[:, 6, :], gates[:, 6, :], ACT.Exp))

            with turns(act, DN_HEADS, {asked.c: 6, to_dve.c: 3, to_tensor.c: 3}) as i:
                for h in range(2):
                    asked.get()
                    for t, cols in enumerate((slice(0, P), slice(P, 3 * P))):
                        m = act.activation(satt[:, cols], satt[:, cols], ACT.Exp, bias=amax[:, t:t + 1],
                                           accum_out=aden[:, t:t + 1])
                    to_tensor.send(m)
                asked.get()
                act.activation(dz[:, :, :], dz[:, :, :], ACT.Silu)
                to_tensor.send(act.activation(cs[:, :, :], cy[:, :, :], ACT.Silu))
                asked.get()
                to_dve.send(act.activation(dss[:, 4:8], dss[:, 0:4], ACT.Sqrt))
                asked.get()
                to_dve.send(act.activation(decay[:, :, :], decay[:, :, :], ACT.Exp))
                asked.get()
                to_dve.send(act.activation(dss[:, 12:14], dss[:, 8:10], ACT.Sqrt))

            root(XT)
            asked.get()
            for t in range(XT):
                m = act.activation(eg[:, t, :], lg[:, t, :], ACT.Exp, bias=rs[:, t:t + 1])
            to_dve.send(m)

            def expert_gates(asked, to_dve, number, each):
                with turns(act, number, {asked.c: 2 * each, to_dve.c: 2 * each}) as i:
                    for _ in range(each):
                        for c in range(2):
                            asked.get()
                            to_dve.send(act.activation(sig[:, c, :], act_h[:, c, :], ACT.Sigmoid, scale=1.702))

            expert_gates(Post(act, E["to_act"]), Post(act, E["from_act"]), EXPERTS // 2, 2)
            act.wait_ge(count_ready, 1)
            more = act.value_load(more_i[0:1, 0:1], min_val=0, max_val=LIST - 1)
            with act.If(more > 0):
                expert_gates(Post(act, O["to_act"]), Post(act, O["from_act"]), more, 1)
            root(XT)

            asked.get()
            to_dve.send(act.activation(lgam[:, :], lgam[:, :], ACT.Exp))
            with turns(act, RET_HEADS, {asked.c: 3, to_dve.c: 3}) as i:
                asked.get()
                act.activation(Wd[:, :, :], dpos[:, :, :], ACT.Exp, scale=lgs[:, 0:1])
                act.activation(We[:, :, :], dneg[:, :, :], ACT.Exp, scale=lgs[:, 1:2])
                act.activation(Wc[:, :, :], dist[:, :, :], ACT.Exp, scale=lgs[:, 0:1], bias=lgs[:, 2:3])
                to_dve.send(act.activation(rtmp[:, :, :], dist[:, :, :], ACT.Exp, scale=lgx[:, 0:1],
                                           bias=lgs[:, 3:4]))
                asked.get()
                to_dve.send(act.activation(rg[:, :, :], rg[:, :, :], ACT.Silu))
                root(4)
            root(4)
            root(4)
            with turns(act, NAT_GROUPS // 2, {asked.c: 16, to_tensor.c: 16}) as i:
                for n in range(16):
                    asked.get()
                    to_tensor.send(act.activation(ns[:, n % 2, :], ns[:, n % 2, :], ACT.Exp,
                                                  bias=nneg[:, n % 2:n % 2 + 1],
                                                  accum_out=nden[:, n % 2:n % 2 + 1]))
            root(XT)
            root(XT)

        @block.tensor
        def _(pe):
            G = GemmFiller(pe, gemm, slots, landed, half0_used, panel_done)
            S, A, M = Filler(pe, side), Filler(pe, att), Filler(pe, mixp)
            from_dve = Post(pe, to_pe)
            from_a = Post(pe, act_to_pe)
            per_gemm = lambda fills, panels: {G.c: fills, G.others: fills - panels, G.panels: panels}

            pe.wait_ge(consts_in, 16)
            pe.wait_ge(params_in, 16)
            pe.wait_ge(ones_ready, 2)
            from_a.get()
            b = S.open()
            for n in range(3):
                m = pe.transpose(b[:, n * P:n * P + P], params[:, n, :], ident)
            S.close(m)
            S.read()

            def ada_product(j):
                G.split_product(lambda k: csil[:, k, :], 4)

            def ada_turn(j, ago):
                G.read(ago)
                b = S.open()
                S.close(pe.transpose(b[:, 0:P], arow[:, j % 2, :], ident))

            def ada_four():
                for j in range(4):
                    ada_product(j)
                    if j:
                        ada_turn(j - 1, 1)
                ada_turn(3, 0)

            ada_four()
            with turns(pe, 8, {**per_gemm(4, 4), S.c: 4}) as i:
                ada_four()

            def spread_gate(number):
                for _ in range(number):
                    from_dve.get()
                    for c in range(2):
                        b = S.open()
                        S.close(pe.matmul(b[:, :], ones[:, :], diag[:, 4 * c:4 * c + 4, :], start=True, stop=True))
                    S.read()

            def to_features(src, tiles):
                from_dve.get()
                for k in range(KT):
                    b = S.open()
                    for t in range(tiles):
                        m = pe.transpose(b[:, t * P:t * P + P], src(t, k), ident)
                    S.close(m)
                S.read()

            x_part = lambda t, k: xn[:, t, k * P:k * P + P]
            tok_part = lambda t, k: tok[:, t, k * P:k * P + P]
            mix_part = lambda t, k: mix[:, t, k * P:k * P + P]
            spread_gate(1)
            to_features(x_part, XT)

            pe.wait_ge(small_in, 96)
            b = S.open()
            for t in range(XT):
                for k in range(KT):
                    m = pe.matmul(b[:, 8 * t:8 * t + 8], hT[:, k, t * P:t * P + P], wdba[:, k, :],
                                  start=(k == 0), stop=(k == KT - 1))
            S.close(m)
            from_dve.get()
            b = S.open()
            pe.matmul(b[:, 0:8], upper, gates[:, 1, :], start=True, stop=True)
            S.close(pe.matmul(b[:, 8:16], ones[:, :], gates[:, 1, :], start=True, stop=True))

            def mixer_products():
                def features(b, dst, cols, mark):
                    for k in range(KT):
                        m = pe.matmul(b[:, dst:dst + SEQ], G.half(k // 4)[:, k % 4, cols:cols + P],
                                      hT[:, k, 0:SEQ], start=(k == 0), stop=(k == KT - 1))
                    return m

                def tokens(b, dst, cols, mark):
                    for t in range(XT):
                        for k in range(KT):
                            m = pe.matmul(b[:, dst + t * P:dst + t * P + P], hT[:, k, t * P:t * P + P],
                                          G.half(k // 4)[:, k % 4, cols:cols + P],
                                          start=(k == 0), stop=(k == KT - 1))
                            if mark and t == XT - 1 and k == 3:
                                m.then_inc(half0_used, 1)
                    return m

                b = G.open()
                features(b, 0, 0, False)
                G.close(features(b, SEQ, P, False))
                b = G.open()
                G.close(tokens(b, 0, 2 * P, True), ends_panel=True)
                b = G.open()
                features(b, 0, 0, False)
                G.close(features(b, SEQ, P, False))
                b = G.open()
                features(b, 0, 2 * P, False)
                G.close(tokens(b, SEQ, 3 * P, True), ends_panel=True)

            with turns(pe, DN_HEADS, {**per_gemm(4, 2), S.c: 24, A.c: 6, from_dve.c: 9, from_a.c: 3}) as i:
                mixer_products()
                G.read(2)
                for h in range(2):
                    r = slice(64 * h, 64 * h + 64)
                    b = A.open()
                    pe.matmul(b[:, 0:P], qkT[r, 0:P], qkT[r, SEQ:SEQ + P], start=True, stop=True)
                    A.close(pe.matmul(b[:, P:3 * P], qkT[r, P:SEQ], qkT[r, SEQ:2 * SEQ], start=True, stop=True))
                    from_a.get()
                    b = A.open()
                    for n in range(3):
                        m = pe.transpose(b[:, n * P:n * P + P], satt[:, n * P:n * P + P], ident)
                    A.close(m)
                    A.read()
                    b = A.open()
                    pe.matmul(b[:, 0:64], pT[:, 0:P], vtok[:, 0, r], start=True, stop=True)
                    pe.matmul(b[:, 64:128], pT[:, P:2 * P], vtok[:, 0, r], start=True, stop=False)
                    A.close(pe.matmul(b[:, 64:128], pT[:, 2 * P:3 * P], vtok[:, 1, r], start=False, stop=True))
                from_a.get()
                for ns_ in (range(4), range(4, 6)):
                    b = S.open()
                    for c, n in enumerate(ns_):
                        m = pe.transpose(b[:, c * P:c * P + P], cs[:, n // 2, (n % 2) * P:(n % 2) * P + P], ident)
                    S.close(m)
                from_dve.get()
                b = S.open()
                for n in range(2):
                    m = pe.matmul(b[:, n * P:n * P + P], gb[:, n, :], upper, start=True, stop=True)
                S.close(m)
                from_dve.get()
                for srcs in ((kn[:, 0, :], kn[:, 1, :], kb[:, 0, :], kb[:, 1, :]),
                             (qn[:, 0, :], qn[:, 1, :], qd[:, :])):
                    b = S.open()
                    for c, src in enumerate(srcs):
                        m = pe.transpose(b[:, c * P:c * P + P], src, ident)
                    S.close(m)
                S.read()
                b = S.open()
                for n in range(2):
                    pe.matmul(b[:, n * P:n * P + P], featT[:, n, :], featT[:, 2 + n, :], start=True, stop=True)
                    m = pe.matmul(b[:, (2 + n) * P:(3 + n) * P], featT[:, n, :], featT[:, 4 + n, :],
                                  start=True, stop=True)
                S.close(m)
                for l in range(LEVELS):
                    from_dve.get()
                    b = S.open()
                    for n in range(2):
                        m = pe.matmul(b[:, n * P:n * P + P], LM[:, n, :], TU[:, n, :], start=True, stop=True)
                    S.close(m)
                    S.read()
                    b = S.open()
                    for n in range(2):
                        pe.matmul(b[:, n * P:n * P + P], TU[:, 2 + n, :], P1[:, n, :], start=True, stop=True)
                        m = pe.matmul(b[:, (2 + n) * P:(3 + n) * P], P1[:, n, :], TU[:, 2 + n, :],
                                      start=True, stop=True)
                    S.close(m)
                S.read()
                b = S.open()
                for n in range(2):
                    pe.matmul(b[:, n * P:n * P + P], TU[:, 2 + n, :], vb[:, n, :], start=True, stop=True)
                S.close(pe.matmul(b[:, 2 * P:3 * P], kbg[:, :], TU[:, 3, :], start=True, stop=True))
                S.read()
                b = S.open()
                pe.matmul(b[:, 0:P], IT[:, 0, :], unew[:, 0, :], start=True, stop=True)
                S.close(pe.matmul(b[:, P:2 * P], kd[:, :], unew[:, 0, :], start=True, stop=True))
                S.read()
                b = S.open()
                S.close(pe.matmul(b[:, 0:P], wT[:, :], state[:, :], start=True, stop=True))
                S.read()
                b = S.open()
                pe.matmul(b[:, 0:P], featT[:, 6, :], state[:, :], start=True, stop=False)
                S.close(pe.matmul(b[:, 0:P], IT[:, 1, :], unew[:, 1, :], start=False, stop=True))

            to_features(mix_part, XT)

            def rows_product(tiles):
                for t in range(tiles):
                    G.product(lambda k, v: hT[:, k, t * P:t * P + P], lambda k, v: v, ends_panel=(t == tiles - 1))

            for c in range(2):
                rows_product(XT)

            to_features(x_part, XT)
            b = S.open()
            for t in range(XT):
                for k in range(KT):
                    m = pe.matmul(b[:, EXPERTS * t:EXPERTS * (t + 1)], hT[:, k, t * P:t * P + P], wr[:, k, :],
                                  start=(k == 0), stop=(k == KT - 1))
            S.close(m)
            from_dve.get()
            b = S.open()
            pe.matmul(b[:, 0:EXPERTS], strict, sel[:, 0, :], start=True, stop=True)
            pe.matmul(b[:, EXPERTS:2 * EXPERTS], strict, sel[:, 1, :], start=True, stop=False)
            pe.matmul(b[:, EXPERTS:2 * EXPERTS], ones[:, :], sel[:, 0, :], start=False, stop=True)
            pe.matmul(b[:, 2 * EXPERTS:3 * EXPERTS], ones[:, :], sel[:, 0, :], start=True, stop=False)
            S.close(pe.matmul(b[:, 2 * EXPERTS:3 * EXPERTS], ones[:, :], sel[:, 1, :], start=False, stop=True))
            from_dve.get()
            b = S.open()
            for t in range(XT):
                m = pe.transpose(b[0:EXPERTS, t * P:t * P + P], gate[:, t, 0:EXPERTS], ident)
            S.close(m)
            S.read()
            pe.wait_ge(b2_in, 16)
            for t in range(XT):
                for c in range(2):
                    b = S.open()
                    S.close(pe.matmul(b[:, :], gT[0:EXPERTS, t * P:t * P + P], b2sb[0:EXPERTS, 512 * c:512 * c + 512],
                                      start=True, stop=True))
            S.read()

            def expert_filler(x, at_slots):
                return (GemmFiller(pe, x["gemm"], at_slots, x["landed"], x["half0"], x["done"]),
                        Filler(pe, x["side"]), Filler(pe, x["att"]), Filler(pe, x["mix"]), Post(pe, x["to_pe"]))

            def gather(A, from_dve):
                from_dve.get()
                b = A.open()
                for k in range(KT):
                    for t in range(XT):
                        m = pe.matmul(b[:, k * CAP:(k + 1) * CAP], xn[:, t, k * P:k * P + P], OH[:, t, :],
                                      start=(t == 0), stop=(t == XT - 1))
                A.close(m)

            def expert(fillers, parity, ahead):
                G, S, A, M, from_dve = fillers

                def turn_act(c):
                    from_dve.get()
                    b = S.open()
                    for n in range(2):
                        m = pe.transpose(b[:, n * P:n * P + P], act_h[:, c, n * P:n * P + P], ident)
                    S.close(m)

                if not ahead:
                    gather(A, from_dve)
                A.read()
                for _ in range(3):
                    G.split_product(lambda k: xg[:, k, :], 2)
                turn_act(0)
                G.split_product(lambda k: xg[:, k, :], 2)
                if ahead:
                    gather(A, from_dve)
                b = A.open()
                for t in range(XT):
                    m = pe.transpose(b[:, t * P:t * P + P], GD[:, parity, t, :], ident)
                A.close(m)
                turn_act(1)
                S.read()
                for c in range(2):
                    G.split_product(lambda k: aT[:, k // 4, k % 2, CAP * (k % 4 // 2):CAP * (k % 4 // 2) + CAP], 2)
                A.read()
                G.read()
                for t in range(XT):
                    M.read()
                    for c in range(2):
                        for s in range(2):
                            r = slice(CAP * s, CAP * s + CAP)
                            m = pe.matmul(M.pair.banks[s][:, 256 * c:256 * c + 256], comb[r, t, :], ysb[r, c, :],
                                          start=True, stop=True)
                            if c == 1:
                                M.close(m)

            counts = lambda f, n: {f[0].c: 6 * n, f[0].panels: 6 * n, f[1].c: 2 * n, f[2].c: 2 * n,
                                   f[3].c: 4 * n, f[4].c: 3 * n}
            f = expert_filler(E, wide)
            G.read()
            S.read()
            A.read()
            gather(f[2], f[4])
            f[2].c.n += 1
            m = pe.transpose(f[2].pair.banks[1][:, 0:P], ident, ident)
            m.then_inc(f[2].pair.full, 1)
            with turns(pe, EXPERTS // 2, counts(f, 2)) as i:
                for e in range(2):
                    expert(f, e, True)
            for x in f[0:4]:
                x.read()
            pe.wait_ge(count_ready, 1)
            more = pe.value_load(more_i[0:1, 0:1], min_val=0, max_val=LIST - 1)
            with pe.If(more > 0):
                f = expert_filler(O, slots)
                with turns(pe, more, counts(f, 1)) as i:
                    expert(f, 0, False)
                for x in f[0:4]:
                    x.read()
            spread_gate(1)

            to_features(tok_part, 4)
            with turns(pe, RET_HEADS, {**per_gemm(20, 4), S.c: 6, A.c: 6, M.c: 4, from_dve.c: 2}) as i:
                for u in range(4):
                    G.product(lambda k, v: v[:, u * P:u * P + P], lambda k, v: hT[:, k, :], ends_panel=(u == 3))
                G.read()
                for n in range(2):
                    b = S.open()
                    for j in range(2):
                        m = pe.matmul(b[:, j * SEQ:(j + 1) * SEQ], swap, rqk[:, 2 * n + j, 0:SEQ], start=True, stop=True)
                    S.close(m)
                rows_product(4)
                rows_product(4)
                from_dve.get()
                for n in range(6):
                    keys, queries = (n, 0) if n < 4 else (n - 2, SEQ)
                    b = A.open()
                    for c in range(2):
                        m = pe.matmul(b[:, 0:SEQ], rqk[:, 2 + c, keys * P:keys * P + P], rqk[:, c, queries:queries + SEQ],
                                      start=(c == 0), stop=(c == 1))
                    A.close(m)
                A.read()
                for t in range(4):
                    b = M.open()
                    src = [(n, n) for n in range(4)] if t < 2 else [(4, 2), (5, 3)]
                    for n, key in src:
                        m = pe.matmul(b[:, :], rsT[:, n, (t % 2) * P:(t % 2) * P + P], rv[:, key, :],
                                      start=(n == src[0][0]), stop=(n == src[-1][0]))
                    M.close(m)
                from_dve.get()
                for k in range(4):
                    b = S.open()
                    for t in range(4):
                        m = pe.transpose(b[:, t * P:t * P + P], ro[:, t, k * P:k * P + P], ident)
                    S.close(m)
                S.read()
                for c in range(2):
                    for t in range(4):
                        b = G.open()
                        for k in range(4):
                            m = pe.matmul(b[:, :], roT[:, k, t * P:t * P + P], G.half(c)[:, k, :],
                                          start=(k == 0), stop=(k == 3))
                            if c == 1 and t == 0 and k == 0:
                                m.then_inc(half0_used, 1)
                        G.close(m, ends_panel=(c == 1 and t == 3))

            def mlp(tiles):
                width = tiles * P
                to_features(tok_part, tiles)
                with turns(pe, 4, {**per_gemm(8 + 2 * tiles, 4), from_dve.c: 1}) as i:
                    for j in range(2):
                        for u in range(4):
                            G.product(lambda k, v: v[:, u * P:u * P + P], lambda k, v: hT[:, k, 0:width],
                                      ends_panel=(u == 3), dst=lambda b: b[:, 0:width])
                    from_dve.get()
                    for c in range(2):
                        for t in range(tiles):
                            G.product(lambda k, v: hid[:, k, t * P:t * P + P], lambda k, v: v,
                                      ends_panel=(t == tiles - 1))

            spread_gate(2)
            mlp(4)
            spread_gate(2)

            to_features(tok_part, 4)
            heads = Count()
            with turns(pe, NAT_GROUPS // 2, {**per_gemm(6, 2), S.c: 16, A.c: 16, M.c: 16, from_a.c: 16, heads: 8}) as i:
                for g in range(2):
                    b = G.open()
                    for k in range(KT):
                        m = pe.matmul(b[:, 0:SEQ], G.half(k // 4)[:, k % 4, 0:P], hT[:, k, 0:SEQ],
                                      start=(k == 0), stop=(k == KT - 1))
                    G.close(m)
                    b = G.open()
                    for k in range(KT):
                        m = pe.matmul(b[:, :], G.half(k // 4)[:, k % 4, P:2 * P], hT[:, k, :],
                                      start=(k == 0), stop=(k == KT - 1))
                    G.close(m)
                    b = G.open()
                    for t in range(4):
                        for k in range(KT):
                            m = pe.matmul(b[:, t * P:t * P + P], hT[:, k, t * P:t * P + P],
                                          G.half(k // 4)[:, k % 4, 2 * P:3 * P], start=(k == 0), stop=(k == KT - 1))
                            if t == 3 and k == 3:
                                m.then_inc(half0_used, 1)
                    G.close(m, ends_panel=True)
                    G.read()

                    def scores(n):
                        h, t = n // 2, n % 2
                        r = slice(NAT_HD * h, NAT_HD * h + NAT_HD)
                        b = A.open()
                        if t == 0:
                            use = heads.n % 2
                            pe.wait_ge(bias_in[use], (heads.n // 2 + 1) * 32 + heads.turn * (heads.per * 16))
                        pe.matmul(b[:, :], nq[r, t * P:t * P + P], nk[r, :], start=True, stop=False)
                        A.close(pe.matmul(b[:, 0:SEQ], anti, nbias[:, heads.n % 2, 2 - 2 * t:6 - 2 * t, :],
                                          start=False, stop=True))
                        if t == 1:
                            heads.n += 1

                    scores(0)
                    for n in range(8):
                        if n < 7:
                            scores(n + 1)
                        h = n // 2
                        from_a.get()
                        b = M.open()
                        for k in range(4):
                            m = pe.transpose(b[:, k * P:k * P + P], ns[:, n % 2, k * P:k * P + P], ident)
                        M.close(m)
                        M.read()
                        b = S.open()
                        for k in range(4):
                            m = pe.matmul(b[:, 0:NAT_HD], npT[:, k, :], nv[:, k, NAT_HD * h:NAT_HD * (h + 1)],
                                          start=(k == 0), stop=(k == 3))
                        S.close(m)
            to_features(x_part, XT)
            for c in range(2):
                rows_product(XT)
            spread_gate(1)
            mlp(2)
            spread_gate(1)

        @block.vector
        def _(dve):
            step = Chain(dve, dve_step)
            G = GemmReader(dve, gemm, panel_done)
            S, A, M = Reader(dve, side), Reader(dve, att), Reader(dve, mixp)
            ask = Post(dve, to_act)
            from_a = Post(dve, from_act)
            to_tensor = Post(dve, to_pe)
            per_gemm = lambda fills, panels: {G.c: fills, G.others: fills - panels, G.panels: panels}
            tt, ts, stt, copy = dve.tensor_tensor, dve.tensor_scalar, dve.scalar_tensor_tensor, dve.tensor_copy

            def col(tile, *index):
                v = tile[(slice(None), *index[:-1], slice(index[-1], index[-1] + 1))]
                return v

            for pair in (gemm, side, att, mixp):
                dve.sem_inc(pair.free, 2)
            b = S.take()
            step(dve.memset(csil[:, :, :], 0.0))
            copy(csil[:, :, 0:3], b[:, 0:3 * KT].rearrange("p (c k) -> p k c", c=3))
            copy(biascol[:, 0:48], b[:, 2 * P:2 * P + 48])
            copy(biascol[:, 48:144], b[:, P:P + 96])
            copy(parcol[:, 0:16], b[:, 2 * P + 48:2 * P + 64])
            S.done(copy(convcol[:, :, :], b[:, 2 * P + 64:2 * P + 112].rearrange("p (h n) -> p h n", h=4)))

            def ada_four(first):
                for j in range(5):
                    if j < 4:
                        b = G.take(ends_panel=True)
                        G.done(copy(arow[:, j % 2, :], b[:, 0:P]))
                    if j:
                        b = S.take()
                        dst = modcol[:, 4 * (j - 1):4 * j, :] if first is None else \
                            modcol[:, bass.ds(first + 4 * (j - 1), 4), :]
                        S.done(copy(dst, b[:, 0:P].rearrange("p (n c) -> p n c", n=4)[:, :, 0:3]))

            ada_four(None)
            with turns(dve, 8, {**per_gemm(4, 4), S.c: 4}) as i:
                ada_four(i * 16 + 16)
            S.settle()
            step(tt(modcol[:, :, :], modcol[:, :, :], biascol[:, :].unsqueeze(2).to_broadcast([P, 144, 3]), ALU.add))

            def mod(layer, part, cond):
                j = 48 * layer + 8 * part
                return modcol[:, j:j + 8, cond]

            def scales(layer, part, norm, conds):
                for n, c in enumerate(conds):
                    step(ts(scol[:, 2 * n, :], mod(layer, part + 1, c), 1.0, None, ALU.add))
                    if norm is not None:
                        step(tt(scol[:, 2 * n, :], scol[:, 2 * n, :], parcol[:, norm:norm + 8], ALU.mult))
                    step(copy(scol[:, 2 * n + 1, :], mod(layer, part, c)))

            def spread_gate(cols, dst):
                for k in range(KT):
                    m = ts(diag[:, k, :], ident, cols[:, k:k + 1], None, ALU.mult)
                to_tensor.send(m)
                for c in range(2):
                    b = S.take()
                    S.done(copy(gateb[:, dst, 512 * c:512 * c + 512], b[:, :]))
                S.settle()

            def spread_gates(layer, part, conds):
                for n, c in enumerate(conds):
                    step(copy(gmul[:, n, :], mod(layer, part, c)))
                    spread_gate(gmul[:, n, :], n)

            def variance(tiles, src, center, eps, width=D):
                parts = width // 512
                for t in range(tiles):
                    for c in range(parts):
                        m = dve.bn_stats(stats[:, t, c, :], src(t)[:, 512 * c:512 * c + 512])
                step(m)
                dve.memset(idle[:, 0:1], 0.0)
                for t in range(tiles):
                    m = dve.bn_aggr(mv[:, t, :], stats[:, t, 0:parts, :])
                step(m)
                if not center:
                    for t in range(tiles):
                        m = stt(mv[:, t, 1:2], mv[:, t, 0:1], mv[:, t, 0:1], mv[:, t, 1:2], ALU.mult, ALU.add)
                    step(m)
                ask.send(ts(mv[:, 0:tiles, 1], mv[:, 0:tiles, 1], eps, None, ALU.add))
                from_a.get()
                step(dve.reciprocal(rstd[:, 0:tiles], std[:, 0:tiles]))

            def from_features(tiles, scaled):
                for k in range(KT):
                    b = S.take()
                    if not scaled:
                        m = copy(hT[:, k, 0:tiles * P], b[:, 0:tiles * P])
                    for n in range(tiles // 2 if scaled else 0):
                        m = ts(hT[:, k, SEQ * n:SEQ * (n + 1)], b[:, SEQ * n:SEQ * (n + 1)],
                               scol[:, 2 * n, k:k + 1], scol[:, 2 * n + 1, k:k + 1], ALU.mult, ALU.add)
                    S.done(m)

            def rms_rows():
                variance(XT, lambda t: tok[:, t, :], False, EPS_RMS)
                for t in range(XT):
                    m = ts(xn[:, t, :], tok[:, t, :], rstd[:, t:t + 1], None, ALU.mult)
                return m

            spread_gates(0, 2, (0,))
            scales(0, 0, 0, (0,))
            dve.wait_ge(tok_in, 32)
            to_tensor.send(rms_rows())
            from_features(XT, True)

            dve.wait_ge(small_in, 96)
            b = S.take()
            bv = b[:, 0:16].rearrange("p (t n) -> p t n", t=2)
            gr = lambda n: gates[:, n, :]
            g3 = lambda n: gates[:, n, :].rearrange("p (t h) -> p t h", t=2)
            copy(g3(0), bv[:, :, 0:4])
            S.done(tt(g3(1), bv[:, :, 4:8], headp[:, 1, :].unsqueeze(1).to_broadcast([P, 2, 4]), ALU.add))
            S.settle()
            ask.send(copy(gr(2), gr(1)))
            from_a.get()
            step(stt(gr(1), gr(1), 0.0, gr(3), ALU.max, ALU.add))
            to_tensor.send(stt(g3(1), g3(1), -1.0, headp[:, 0, :].unsqueeze(1).to_broadcast([P, 2, 4]),
                               ALU.mult, ALU.mult))
            b = S.take()
            copy(gr(4), b[:, 0:8])
            S.done(copy(gr(6), b[:, 8:16]))
            S.settle()
            ask.send(tt(gr(6), gr(6), gr(4), ALU.subtract))
            from_a.get()
            for n in range(4):
                m = copy(TU[:, n, :], ident)
            step(m)

            def attention_head(i, h):
                r = slice(64 * h, 64 * h + 64)
                b = A.take()
                A.done(stt(satt[:, :], b[:, 0:3 * P], 0.125, lcount, ALU.mult, ALU.add))
                A.settle()
                dve.tensor_reduce(amax[:, 0:1], satt[:, 0:P], AX, ALU.max)
                step(dve.tensor_reduce(amax[:, 1:2], satt[:, P:3 * P], AX, ALU.max))
                ask.send(ts(amax[:, 0:2], amax[:, 0:2], -1.0, None, ALU.mult))
                b = A.take()
                A.done(copy(pT[:, :], b[:, 0:3 * P]))
                step(dve.reciprocal(arec[:, 0:2], aden[:, 0:2]))
                b = A.take()
                for t in range(2):
                    m = ts(mix[:, t, bass.ds(i * P + 64 * h, 64)], b[:, 64 * t:64 * t + 64],
                           arec[:, t:t + 1], None, ALU.mult)
                A.done(m)

            with turns(dve, DN_HEADS, {**per_gemm(4, 2), S.c: 24, A.c: 6, ask.c: 6, from_a.c: 3, to_tensor.c: 9,
                                       step.c: 21}) as i:
                b = G.take()
                G.done(copy(qkT[:, :], b[:, :]))
                b = G.take(True)
                G.done(copy(vtok[:, :, :].rearrange("p a b -> p (a b)"), b[:, 0:SEQ]))
                b = G.take()
                G.done(copy(cin[:, 0:2, 4:260], b[:, :].rearrange("p (a b) -> p a b", a=2)))
                b = G.take(True)
                copy(cin[:, 2, 4:260], b[:, 0:SEQ])
                G.done(copy(dz[:, :, :].rearrange("p a b -> p (a b)"), b[:, SEQ:2 * SEQ]))
                for h in range(2):
                    attention_head(i, h)
                for n in range(7):
                    copy(hsel[:, n, :], g3(n)[:, :, bass.ds(i, 1)].rearrange("p t a -> p (t a)"))
                step(copy(cw[:, :], convcol[:, bass.ds(i, 1), :].rearrange("p a n -> p (a n)")))
                G.settle()
                for p in range(3):
                    m = ts(cy[:, p, :], cin[:, p, 4:260], cw[:, 9 + p:10 + p], None, ALU.mult)
                step(m)
                for j in range(3):
                    for p in range(3):
                        m = stt(cy[:, p, :], cin[:, p, 1 + j:257 + j], cw[:, 3 * j + p:3 * j + p + 1], cy[:, p, :],
                                ALU.mult, ALU.add)
                    if j < 2:
                        step(m)
                ask.send(m)
                for n in range(2):
                    m = ts(gb[:, n, :], ones[:, :], hsel[:, 1, n:n + 1], None, ALU.mult)
                to_tensor.send(m)
                for first, number in ((0, 4), (4, 2)):
                    b = S.take()
                    S.done(copy(qkv[:, first:first + number, :].rearrange("p a b -> p (a b)"), b[:, 0:number * P]))
                S.settle()
                for n in range(4):
                    m = dve.tensor_tensor_reduce(osb[:, n % 2, :], qkv[:, n, :], qkv[:, n, :], 1.0, 0.0,
                                                 ALU.mult, ALU.add, dss[:, n:n + 1])
                    step(m)
                ask.send(ts(dss[:, 0:4], dss[:, 0:4], EPS_RMS, None, ALU.add))
                b = S.take()
                for n in range(2):
                    m = ts(decay[:, n, :], b[:, n * P:n * P + P], hsel[:, 4, n:n + 1], 0.0, ALU.subtract, ALU.min)
                S.done(m)
                S.settle()
                from_a.get()
                ask.send(dve.reciprocal(dss[:, 4:8], dss[:, 4:8]))
                dve.wait_ge(to_act, ask.c.at())
                for n in range(2):
                    ts(qn[:, n, :], qkv[:, n, :], dss[:, 4 + n:5 + n], P ** -0.5, ALU.mult, ALU.mult)
                    ts(kn[:, n, :], qkv[:, 2 + n, :], dss[:, 6 + n:7 + n], None, ALU.mult)
                    m = ts(vb[:, n, :], qkv[:, 4 + n, :], hsel[:, 0, n:n + 1], None, ALU.mult)
                step(m)
                for n in range(2):
                    m = ts(kb[:, n, :], kn[:, n, :], hsel[:, 0, n:n + 1], None, ALU.mult)
                step(m)
                ts(kbg[:, :], kb[:, 1, :], hsel[:, 5, 1:2], None, ALU.mult)
                ts(qd[:, :], qn[:, 1, :], hsel[:, 5, 1:2], None, ALU.mult)
                to_tensor.send(ts(kd[:, :], kn[:, 0, :], hsel[:, 6, 0:1], None, ALU.mult))
                from_a.get()
                step(tt(decay[:, :, :], decay[:, :, :], upper.unsqueeze(1).to_broadcast([P, 2, P]), ALU.mult))
                for first, number in ((0, 4), (4, 3)):
                    b = S.take()
                    S.done(copy(featT[:, first:first + number, :].rearrange("p a b -> p (a b)"), b[:, 0:number * P]))
                b = S.take()
                bb = b[:, :].rearrange("p (a n) -> p a n", a=4)
                tt(LT[:, :, :], bb[:, 0:2, :], decay[:, :, :], ALU.mult)
                S.done(tt(IT[:, :, :], bb[:, 2:4, :], decay[:, :, :], ALU.mult))
                for n in range(4):
                    m = copy(TU[:, n, :], ident)
                step(m)
                S.settle()
                for l in range(LEVELS):
                    to_tensor.send(tt(LM[:, :, :], LT[:, :, :], lvl[:, l, :].unsqueeze(1).to_broadcast([P, 2, P]),
                                      ALU.mult))
                    b = S.take()
                    S.done(copy(P1[:, :, :].rearrange("p a b -> p (a b)"), b[:, 0:SEQ]))
                    b = S.take()
                    S.done(tt(TU[:, :, :].rearrange("p a b -> p (a b)"), TU[:, :, :].rearrange("p a b -> p (a b)"),
                              b[:, :], ALU.subtract))
                    S.settle()
                b = S.take()
                copy(unew[:, :, :].rearrange("p a b -> p (a b)"), b[:, 0:SEQ])
                S.done(copy(wT[:, :], b[:, 2 * P:3 * P]))
                b = S.take()
                copy(osb[:, 0, :], b[:, 0:P])
                S.done(copy(state[:, :], b[:, P:2 * P]))
                b = S.take()
                S.done(tt(unew[:, 1, :], unew[:, 1, :], b[:, 0:P], ALU.subtract))
                b = S.take()
                S.done(copy(osb[:, 1, :], b[:, 0:P]))
                S.settle()
                for n in range(2):
                    step(dve.tensor_tensor_reduce(qn[:, n, :], osb[:, n, :], osb[:, n, :], 1.0, 0.0,
                                                  ALU.mult, ALU.add, dss[:, 8 + n:9 + n]))
                ask.send(ts(dss[:, 8:10], dss[:, 8:10], 1.0 / P, EPS_RMS, ALU.mult, ALU.add))
                from_a.get()
                step(dve.reciprocal(dss[:, 14:16], dss[:, 12:14]))
                for n in range(2):
                    m = stt(osb[:, n, :], osb[:, n, :], dss[:, 14 + n:15 + n], dnw[:, :], ALU.mult, ALU.mult)
                step(m)
                step(tt(mix[:, :, bass.ds(i * P + AT_W, P)], osb[:, :, :], dz[:, :, :], ALU.mult))

            to_tensor.send(ts(mix[:, 0, 0:1], mix[:, 0, 0:1], 1.0, None, ALU.mult))
            from_features(XT, False)

            def gated_rows(c, t):
                cols = slice(512 * c, 512 * c + 512)
                b = G.take(t == XT - 1)
                G.done(tt(xn[:, t, cols], b[:, :], gateb[:, 0, cols], ALU.mult))
                G.settle()
                step(tt(tok[:, t, cols], tok[:, t, cols], xn[:, t, cols], ALU.add))

            for c in range(2):
                for t in range(XT):
                    gated_rows(c, t)

            scales(0, 3, 8, (0,))
            to_tensor.send(rms_rows())
            from_features(XT, True)
            b = S.take()
            S.done(tt(lg[:, :, :], b[:, 0:2 * EXPERTS].rearrange("p (t n) -> p t n", t=2),
                      brow[:, :].unsqueeze(1).to_broadcast([P, 2, EXPERTS]), ALU.add))
            S.settle()
            dve.memset(m8[:, :, :], 0.0)
            dve.memset(gate[:, :, EXPERTS:EXPERTS + 1], 0.0)
            step(dve.memset(pos[:, :, EXPERTS:EXPERTS + 1], -1.0))
            for t in range(XT):
                m = dve.max(m8[:, t, :], lg[:, t, :])
            step(m)
            ask.send(ts(rs[:, 0:2], m8[:, :, 0], -1.0, None, ALU.mult))
            fourth = lambda t: m8[:, t, TOP_K - 1:TOP_K]
            for t in range(XT):
                ts(eq[:, t, :], lg[:, t, :], fourth(t), None, ALU.is_equal)
                m = ts(sel[:, t, :], lg[:, t, :], fourth(t), None, ALU.is_gt)
            step(m)
            dve.tensor_reduce(rs[:, 2:4], sel[:, :, :], AX, ALU.add)
            step(copy(cum[:, 0, :, :], eq[:, :, :]))
            for l in range(5):
                s, d, w = cum[:, l % 2, :, :], cum[:, (l + 1) % 2, :, :], 1 << l
                copy(d[:, :, 0:w], s[:, :, 0:w])
                step(tt(d[:, :, w:EXPERTS], s[:, :, w:EXPERTS], s[:, :, 0:EXPERTS - w], ALU.add))
            step(ts(rs[:, 2:4], rs[:, 2:4], -1.0, float(TOP_K), ALU.mult, ALU.add))
            for t in range(XT):
                m = stt(eq[:, t, :], cum[:, 1, t, :], rs[:, 2 + t:3 + t], eq[:, t, :], ALU.is_le, ALU.mult)
            step(m)
            to_tensor.send(tt(sel[:, :, :], sel[:, :, :], eq[:, :, :], ALU.add))
            dve.wait_ge(to_pe, to_tensor.c.at())
            from_a.get()
            step(tt(eg[:, :, :], eg[:, :, :], sel[:, :, :], ALU.mult))
            step(dve.tensor_reduce(rs[:, 4:6], eg[:, :, :], AX, ALU.add))
            step(dve.reciprocal(rs[:, 6:8], rs[:, 4:6]))
            for t in range(XT):
                m = ts(gate[:, t, 0:EXPERTS], eg[:, t, :], rs[:, 6 + t:7 + t], None, ALU.mult)
            step(m)
            b = S.take()
            copy(cntf[:, :], b[:, 2 * EXPERTS:3 * EXPERTS])
            bp = b[:, 0:2 * EXPERTS].rearrange("p (t n) -> p t n", t=2)
            S.done(stt(pos[:, :, 0:EXPERTS], bp, 1.0, sel[:, :, :], ALU.add, ALU.mult))
            S.settle()
            step(ts(pos[:, :, 0:EXPERTS], pos[:, :, 0:EXPERTS], -1.0, None, ALU.add))
            to_tensor.send(ts(gate[:, 0, EXPERTS:EXPERTS + 1], gate[:, 0, EXPERTS:EXPERTS + 1], 0.0, None, ALU.mult))
            dve.memset(rs[:, 9:10], 0.0).then_inc(b2_go, 1)
            dve.memset(idle[:, 3:4], 0.0).then_inc(tiles_free, 1)
            b = S.take()
            S.done(copy(gT[0:EXPERTS, :], b[0:EXPERTS, 0:SEQ]))
            for t in range(XT):
                for c in range(2):
                    b = S.take()
                    S.done(copy(yacc[:, t, 512 * c:512 * c + 512], b[:, :]))
            S.settle()

            for r in range(3):
                m = ts(flags[:, r, :], cntf[:, :], float(CAP * (r + 1)), None, ALU.is_gt)
            step(m)
            flat = flags[:, :, :].rearrange("p a b -> p (a b)")
            step(copy(fcum[:, 0, :], flat))
            n = 3 * EXPERTS
            for l in range(7):
                s, d, w = fcum[:, l % 2, :], fcum[:, (l + 1) % 2, :], 1 << l
                copy(d[:, 0:w], s[:, 0:w])
                step(tt(d[:, w:n], s[:, w:n], s[:, 0:n - w], ALU.add))
            copy(more_i[:, :], fcum[:, 1, n - 1:n])
            over = lambda v: v.unsqueeze(1).to_broadcast([P, LIST, n])
            step(tt(match[:, :, :], over(fcum[:, 1, :]), tab_j.unsqueeze(2).to_broadcast([P, LIST, n]), ALU.is_equal))
            step(tt(match[:, :, :], match[:, :, :], over(flat), ALU.mult))
            step(tt(match2[:, :, :], match[:, :, :], over(tab_e), ALU.mult))
            step(dve.tensor_reduce(rs[:, 0:LIST], match2[:, :, :], AX, ALU.add))
            step(copy(list_e[:, :], rs[:, 0:LIST]))
            step(tt(match2[:, :, :], match[:, :, :], over(tab_s), ALU.mult))
            dve.tensor_reduce(list_s[:, :], match2[:, :, :], AX, ALU.add).then_inc(count_ready, 1)
            dve.wait_ge(count_ready, 1)

            def expert_reader(x, credit):
                return dict(G=GemmReader(dve, x["gemm"], x["done"], credit), S=Reader(dve, x["side"]),
                            A=Reader(dve, x["att"]), M=Reader(dve, x["mix"]), ask=Post(dve, x["to_act"]),
                            from_a=Post(dve, x["from_act"]), to_tensor=Post(dve, x["to_pe"]),
                            step=Chain(dve, x["step"]), freed=Post(dve, x["b1_used"]), uses=Count(),
                            arrived=x["b1"])

            def prepare(r, e, parity, base=None):
                e1 = pos[:, :, bass.ds(e, 1)].rearrange("p t a -> p (t a)")
                if base is None:
                    copy(pg[:, 0, parity, :], e1)
                else:
                    r["step"](copy(pg[:, 1, 1, 0:1], list_s[:, bass.ds(base, 1)]))
                    ts(pg[:, 0, parity, :], e1, pg[:, 1, 1, 0:1], None, ALU.subtract)
                r["step"](copy(pg[:, 1, parity, :], gate[:, :, bass.ds(e, 1)].rearrange("p t a -> p (t a)")))
                for t in range(XT):
                    ts(OH[:, t, :], iota[:, 0:CAP], pg[:, 0, parity, t:t + 1], None, ALU.is_equal)
                    m = ts(GD[:, parity, t, :], iota, pg[:, 0, parity, t:t + 1], pg[:, 1, parity, t:t + 1],
                           ALU.is_equal, ALU.mult)
                r["to_tensor"].send(m)

            def gathered(r):
                b = r["A"].take()
                for k in range(KT):
                    m = ts(xg[:, k, :], b[:, k * CAP:(k + 1) * CAP], scol[:, 0, k:k + 1], scol[:, 1, k:k + 1],
                           ALU.mult, ALU.add)
                r["A"].done(m)

            def expert(r, parity, ahead):
                G, S, A, M, step = r["G"], r["S"], r["A"], r["M"], r["step"]

                def biased(c, n):
                    b = G.take(True)
                    G.done(tt((act_h, up_h)[n][:, c, :], b[:, 0:256], b1b[:, parity, 2 * n + c, :], ALU.add))

                def swiglu(c):
                    G.settle()
                    r["ask"].send(ts(act_h[:, c, :], act_h[:, c, :], 7.0, None, ALU.min))
                    m = ts(up_h[:, c, :], up_h[:, c, :], 7.0, -7.0, ALU.min, ALU.max)
                    if c == 0:
                        step(m)
                    else:
                        r["freed"].send(m)
                        dve.wait_ge(r["freed"].sem, r["freed"].c.at(r.get("b1_credit", 0)))
                    dve.wait_ge(r["ask"].sem, r["ask"].c.at())
                    step(stt(up_h[:, c, :], up_h[:, c, :], 1.0, act_h[:, c, :], ALU.add, ALU.mult))
                    r["from_a"].get()
                    r["to_tensor"].send(tt(act_h[:, c, :], up_h[:, c, :], sig[:, c, :], ALU.mult))

                def turned(c):
                    b = S.take()
                    S.done(copy(aT[:, c, :, :].rearrange("p a b -> p (a b)"), b[:, 0:2 * P]))

                if not ahead:
                    gathered(r)
                buffers = 2 if ahead else 1
                dve.wait_ge(r["arrived"][parity], r["uses"].dma(buffers, 32))
                r["uses"].n += 1
                biased(0, 0)
                biased(0, 1)
                swiglu(0)
                if ahead:
                    prepare(r, ahead[0], 1 - parity)
                biased(1, 0)
                turned(0)
                biased(1, 1)
                swiglu(1)
                if ahead:
                    gathered(r)
                b = A.take()
                A.done(copy(comb[:, :, :].rearrange("p a b -> p (a b)"), b[:, 0:SEQ]))
                turned(1)
                for c in range(2):
                    b = G.take(True)
                    G.done(copy(ysb[:, c, :], b[:, 0:256]))
                for t in range(XT):
                    for s in range(2):
                        b = M.take()
                        y = yacc[:, t, :].rearrange("p (c s n) -> p c s n", c=2, s=2)[:, :, s, :]
                        M.done(tt(y, y, b[:, :].rearrange("p (c n) -> p c n", c=2), ALU.add))

            def counts(r, n, steps):
                return {r["G"].c: 6 * n, r["G"].panels: 6 * n, r["S"].c: 2 * n, r["A"].c: 2 * n, r["M"].c: 4 * n,
                        r["to_tensor"].c: 3 * n, r["ask"].c: 2 * n, r["from_a"].c: 2 * n, r["uses"]: n,
                        r["freed"].c: n, r["step"].c: steps * n}

            for x in ("gemm", "side", "att", "mix"):
                dve.sem_inc(E[x].free, 2)
            r = expert_reader(E, 0)
            prepare(r, 0, 0)
            gathered(r)
            b = r["A"].take()
            r["A"].done(copy(comb[:, 0, :], b[:, 0:P]))
            with turns(dve, EXPERTS // 2, counts(r, 2, 4)) as i:
                for e in range(2):
                    expert(r, e, (i * 2 + (e + 1),))
            r["M"].settle()
            dve.wait_ge(count_ready, 1)
            more = dve.value_load(more_i[0:1, 0:1], min_val=0, max_val=LIST - 1)
            with dve.If(more > 0):
                for x in ("gemm", "side", "att", "mix"):
                    dve.sem_inc(O[x].free, 2)
                r = expert_reader(O, 2)
                r["b1_credit"] = 1
                with turns(dve, more, counts(r, 1, 5)) as i:
                    e = dve.value_load(list_e[0:1, bass.ds(i, 1)], min_val=0, max_val=EXPERTS - 1)
                    prepare(r, e, 0, i)
                    expert(r, 0, None)
                r["M"].settle()
                dve.sem_inc(further_done, 1)

            spread_gates(0, 5, (0,))
            for t in range(XT):
                m = tt(yacc[:, t, :], yacc[:, t, :], gateb[:, 0, :], ALU.mult)
            step(m)
            for t in range(XT):
                m = tt(tok[:, t, :], tok[:, t, :], yacc[:, t, :], ALU.add)
            step(m)
            variance(XT, lambda t: tok[:, t, :], False, EPS_RMS)
            dve.wait_ge(rows_in, 16)
            for t in range(XT):
                m = stt(tok[:, t, :], tok[:, t, :], rstd[:, t:t + 1], lnrow[:, 0, :], ALU.mult, ALU.mult)
            m.then_inc(rows_used, 1)
            dve.wait_ge(rows_used, 1)

            norms = [0]

            def layer_norm(tiles, last=False):
                for t in range(tiles):
                    m = tt(yacc[:, t, :], yacc[:, t, :], gateb[:, t // 2, :], ALU.mult)
                step(m)
                for t in range(tiles):
                    m = stt(tok[:, t, :], tok[:, t, :], ALPHA, yacc[:, t, :], ALU.mult, ALU.add)
                step(m)
                variance(tiles, lambda t: tok[:, t, :], True, EPS_LN)
                dve.wait_ge(rows_in, 16 + 32 * (norms[0] + 1))
                norms[0] += 1
                for t in range(tiles):
                    m = ts(tok[:, t, :], tok[:, t, :], mv[:, t, 0:1], rstd[:, t:t + 1], ALU.subtract, ALU.mult)
                step(m)
                for n, op in enumerate((ALU.mult, ALU.add)):
                    for t in range(tiles):
                        m = tt(tok[:, t, :], tok[:, t, :], lnrow[:, n, :], op)
                    if n == 0:
                        step(m)
                m.then_inc(out_ready if last else rows_used, 1)
                if not last:
                    dve.wait_ge(rows_used, norms[0] + 1)

            ask.send(copy(lgam[:, :], lgam[:, :]))
            from_a.get()
            step(ts(lgam[:, :], lgam[:, :], -1.0, None, ALU.mult))
            dve.memset(yacc[:, :, :], 0.0)
            ts(dpos[:, :, :], dist, 0.0, None, ALU.max)
            step(ts(dneg[:, :, :], dist, -1.0, 0.0, ALU.mult, ALU.max))
            scales(1, 0, None, (1, 2))
            to_tensor.send(dve.memset(idle[:, 2:3], 0.0))
            dve.wait_ge(to_pe, to_tensor.c.at())
            from_features(4, True)
            with turns(dve, RET_HEADS, {**per_gemm(20, 4), S.c: 6, A.c: 6, M.c: 4, ask.c: 3, from_a.c: 3,
                                        to_tensor.c: 2, step.c: 11}) as i:
                copy(lgs[:, 0:1], lgam[:, bass.ds(i, 1)])
                step(copy(lgs[:, 1:2], lgam[:, bass.ds(i + RET_HEADS, 1)]))
                ts(lgx[:, 0:1], lgs[:, 1:2], -1.0, None, ALU.mult)
                ask.send(ts(lgs[:, 2:4], lgs[:, 0:2], float(SEQ), None, ALU.mult))
                for u in range(4):
                    b = G.take(u == 3)
                    G.done(copy(rqk[:, u, :], b[:, :]))
                G.settle()
                for n in range(2):
                    b = S.take()
                    S.done(tt(ro[:, n, :].rearrange("p (a b) -> p a b", a=2), b[:, :].rearrange("p (a b) -> p a b", a=2),
                              rope[:, :, 1, :], ALU.mult))
                    S.settle()
                    step(tt(rqk[:, 2 * n:2 * n + 2, 0:SEQ], rqk[:, 2 * n:2 * n + 2, 0:SEQ], rope[:, :, 0, :], ALU.mult))
                    m = tt(rqk[:, 2 * n:2 * n + 2, 0:SEQ], rqk[:, 2 * n:2 * n + 2, 0:SEQ],
                           ro[:, n, :].rearrange("p (a b) -> p a b", a=2), ALU.add)
                    step(m)
                from_a.get()
                stt(Wd[:, :, :], dist, 0.0, Wd[:, :, :], ALU.is_ge, ALU.mult)
                step(stt(We[:, :, :], dist, 0.0, We[:, :, :], ALU.is_le, ALU.mult))
                step(tt(Wd[:, :, :], Wd[:, :, :], We[:, :, :], ALU.add))
                to_tensor.send(tt(Wc[:, :, :], Wc[:, :, :], rtmp[:, :, :], ALU.add))
                dve.wait_ge(to_pe, to_tensor.c.at())
                for dst in (rv, rg):
                    for t in range(4):
                        b = G.take(t == 3)
                        m = copy(dst[:, t, :], b[:, :])
                        G.done(m)
                G.settle()
                ask.send(copy(lgs[:, 0:1], lgs[:, 0:1]))
                for n in range(6):
                    b = A.take()
                    w = Wc[:, n - 2, :] if n in (2, 3) else Wd[:, n % 2, :]
                    A.done(stt(rsT[:, n, :], b[:, 0:SEQ], 1.0 / 16, w, ALU.mult, ALU.mult))
                for t in range(4):
                    b = M.take()
                    M.done(copy(ro[:, t, :], b[:, :]))
                M.settle()
                from_a.get()
                variance(4, lambda t: ro[:, t, :], True, EPS_LN, width=512)
                for t in range(4):
                    m = ts(ro[:, t, :], ro[:, t, :], mv[:, t, 0:1], rstd[:, t:t + 1], ALU.subtract, ALU.mult)
                step(m)
                for t in range(4):
                    m = tt(ro[:, t, :], ro[:, t, :], rg[:, t, :], ALU.mult)
                to_tensor.send(m)
                for k in range(4):
                    b = S.take()
                    S.done(copy(roT[:, k, :], b[:, :]))
                for c in range(2):
                    for t in range(4):
                        s = slice(512 * c, 512 * c + 512)
                        b = G.take(c == 1 and t == 3)
                        G.done(tt(yacc[:, t, s], yacc[:, t, s], b[:, :], ALU.add))
                G.settle()
            spread_gates(1, 2, (1, 2))
            layer_norm(4)

            def mlp(layer, conds, last=False):
                tiles = 2 * len(conds)
                width = tiles * P
                scales(layer, 3, None, conds)
                to_tensor.send(dve.memset(idle[:, 2:3], 0.0))
                dve.wait_ge(to_pe, to_tensor.c.at())
                step(dve.memset(yacc[:, 0:tiles, :], 0.0))
                from_features(tiles, True)
                with turns(dve, 4, {**per_gemm(8 + 2 * tiles, 4), step.c: 7, to_tensor.c: 1}) as i:
                    for u in range(8):
                        b = G.take(u % 4 == 3)
                        G.done(ts(mtmp[:, 0:width], b[:, 0:width], 0.0, None, ALU.max))
                        G.settle()
                        m = tt(hid[:, u, 0:width], mtmp[:, 0:width], mtmp[:, 0:width], ALU.mult)
                        if u < 7:
                            step(m)
                        else:
                            to_tensor.send(m)
                    for c in range(2):
                        for t in range(tiles):
                            s = slice(512 * c, 512 * c + 512)
                            b = G.take(t == tiles - 1)
                            G.done(tt(yacc[:, t, s], yacc[:, t, s], b[:, :], ALU.add))
                    G.settle()
                spread_gates(layer, 5, conds)
                layer_norm(tiles, last)

            mlp(1, (1, 2))

            scales(2, 0, None, (1, 2))
            dve.memset(idle[:, 1:2], 0.0).then_inc(nat_go, 1)
            to_tensor.send(dve.memset(idle[:, 2:3], 0.0))
            dve.wait_ge(to_pe, to_tensor.c.at())
            from_features(4, True)
            freed = Post(dve, bias_used)
            with turns(dve, NAT_GROUPS // 2, {**per_gemm(6, 2), S.c: 16, A.c: 16, M.c: 16, ask.c: 16, freed.c: 8,
                                              step.c: 40}) as i:
                for g in range(2):
                    b = G.take()
                    G.done(ts(nq[:, :], b[:, 0:SEQ], NAT_HD ** -0.5, None, ALU.mult))
                    b = G.take()
                    G.done(copy(nk[:, :], b[:, :]))
                    b = G.take(True)
                    G.done(copy(nv[:, :, :].rearrange("p a b -> p (a b)"), b[:, :]))

                    def soften(n):
                        p = n % 2
                        b = A.take()
                        m = tt(ns[:, p, 0:SEQ].rearrange("p (a b) -> p a b", a=4),
                               b[:, 0:SEQ].rearrange("p (a b) -> p a b", a=4),
                               natmask.unsqueeze(1).to_broadcast([P, 4, GRID_W]), ALU.add)
                        if n % 2:
                            freed.send(m)
                            dve.wait_ge(bias_used, freed.c.at())
                        else:
                            step(m)
                        A.done(copy(ns[:, p, SEQ:2 * SEQ], b[:, SEQ:2 * SEQ]))
                        A.settle()
                        step(dve.tensor_reduce(nmax[:, p:p + 1], ns[:, p, :], AX, ALU.max))
                        ask.send(ts(nneg[:, p:p + 1], nmax[:, p:p + 1], -1.0, None, ALU.mult))

                    soften(0)
                    for n in range(8):
                        if n < 7:
                            soften(n + 1)
                        b = M.take()
                        M.done(copy(npT[:, :, :].rearrange("p a b -> p (a b)"), b[:, :]))
                        step(dve.reciprocal(nrec[:, n % 2:n % 2 + 1], nden[:, n % 2:n % 2 + 1]))
                        b = S.take()
                        S.done(ts(no[:, n % 2, bass.ds(i * 256 + (g * P + NAT_HD * (n // 2)), NAT_HD)], b[:, 0:NAT_HD],
                                  nrec[:, n % 2:n % 2 + 1], None, ALU.mult))
            S.settle()
            to_tensor.send(dve.memset(idle[:, 2:3], 0.0))
            dve.wait_ge(to_pe, to_tensor.c.at())
            from_features(XT, False)
            for c in range(2):
                for t in range(XT):
                    b = G.take(t == XT - 1)
                    G.done(copy(yacc[:, t, 512 * c:512 * c + 512], b[:, :]))
            G.settle()
            spread_gates(2, 2, (1,))
            layer_norm(2)
            mlp(2, (1,), last=True)


def kernel(**inputs):
    import concourse.bacc as _bacc
    from concourse.bass_utils import run_bass_kernel_spmd as _run

    x = {n: np.asarray(v) for n, v in inputs.items()}
    nc = _bacc.Bacc("TRN2", target_bir_lowering=False, num_devices=1)

    def cut(w, c0, width=512, r0=0):
        v = w[r0:r0 + D, c0:c0 + width]
        return v.reshape(KT, P, width).transpose(1, 0, 2).reshape(P, -1)

    def heads(w, firsts, i, width):
        return np.concatenate([w[:, f + i * width:f + (i + 1) * width] for f in firsts], axis=1)

    w_in = x["w_in"][0]
    pa = [cut(x["w_ada"][0], 512 * j) for j in range(12)]
    pa += [cut(x["ada_w_2"][l], 512 * j) for l in range(2) for j in range(12)]
    for i in range(DN_HEADS):
        three = heads(w_in, (0, 512, 1024), i, P)
        pa.append(cut(np.concatenate([three, np.zeros_like(three[:, 0:P])], axis=1), 0))
        pa.append(cut(heads(w_in, (1536, 2048, 2560, 3072), i, P), 0))
    pa += [cut(x["w_out"][0], 512 * c) for c in range(2)]
    pe = np.empty((EXPERTS, 6, P, KT * 512), np.float32)
    for e in range(EXPERTS):
        for j, c0 in enumerate((0, 1024, 512, 1536)):
            pe[e, j] = cut(x["w1"][0, e], c0)
        for c in range(2):
            pe[e, 4 + c] = cut(x["w2"][0, e], 512 * c)
    pb = []
    rw, ro = x["ret_w_in_2"][0], x["ret_w_o_2"][0]
    for i in range(RET_HEADS):
        pb += [cut(heads(rw, (0, 1024), i, 256), 0), cut(rw, 2048 + 512 * i), cut(rw, 4096 + 512 * i)]
        v = ro[512 * i:512 * i + 512].reshape(4, P, 2, 512)
        pb.append(v.transpose(1, 2, 0, 3).reshape(P, -1))

    def mlp_panels(l):
        r = []
        for i in range(4):
            r += [cut(x["mlp_w1_2"][l], D * i + 512 * j) for j in range(2)]
            r += [cut(x["mlp_w2_2"][l], 512 * j, r0=D * i) for j in range(2)]
        return r

    pb += mlp_panels(0)
    pn = [cut(heads(x["nat_w_in_2"][0], (0, D, 2 * D), i, P), 0, width=3 * P) for i in range(NAT_GROUPS)]
    pc = [cut(x["nat_w_o_2"][0], 512 * c) for c in range(2)] + mlp_panels(1)
    rows = lambda v: v.reshape(-1, P)
    par = np.zeros((3, P, P), np.float32)
    one = np.concatenate([rows(x["c"]), rows(x["c_2"]), rows(x["c_ctx_2"])])
    par[0, 0:24] = one
    par[1, 0:96] = rows(x["ada_b_2"])
    taps = x["conv_w"][0].reshape(4, 3, DN_HEADS, P).transpose(2, 0, 1, 3)
    par[2, 0:112] = np.concatenate([rows(x["b_ada"]), rows(x["norm1_w"]), rows(x["norm2_w"]), rows(taps)])
    small = np.concatenate([cut(w_in, 3584, width=8), cut(x["w_router"][0], 0, width=EXPERTS)], axis=1)
    rpb = np.zeros((NAT_HEADS, 15, RPB_W), np.float32)
    rpb[:, :, 48:79] = x["nat_rpb_2"][0]

    arrays = {
        "x": x["x"], "ctx_2": x["ctx_2"], "panels_a": np.stack(pa), "panels_e": pe.reshape(-1, P, KT * 512),
        "panels_b": np.stack(pb), "panels_n": np.stack(pn), "panels_c": np.stack(pc),
        "consts": constants(), "params": par.reshape(3 * P, P), "smallw": small, "rpb": rpb,
        "A_log": x["A_log"], "dt_bias": x["dt_bias"], "dn_norm_w": x["dn_norm_w"], "b_router": x["b_router"],
        "ret_decay": x["ret_decay_2"].reshape(8), "b1": x["b1"][0], "b2": x["b2"], "final_norm_w": x["final_norm_w"],
        "ln_g_2": x["ln_g_2"], "ln_b_2": x["ln_b_2"],
    }
    arrays = {n: np.ascontiguousarray(v) for n, v in arrays.items()}
    a = {n: nc.dram_tensor("in_" + n, v.shape, mybir.dt.from_np(v.dtype), kind="ExternalInput").ap()
         for n, v in arrays.items()}
    out = nc.dram_tensor("out_0", (1, SEQ, D), F32, kind="ExternalOutput").ap()
    program(nc, a, out)
    r = _run(nc, [{"in_" + n: v for n, v in arrays.items()}], core_ids=[0])
    return r.results[0]["out_0"]
```

```python
from contextlib import ExitStack, contextmanager

import numpy as np

import concourse.bass as bass
from concourse import mybir

F32 = mybir.dt.float32
F32R = mybir.dt.float32r
I32 = mybir.dt.int32
ALU = mybir.AluOpType
ACT = mybir.ActivationFunctionType
AX = mybir.AxisListType.X

P = 128
D = 1024
KT = D // P
SEQ = 256
XT = SEQ // P
AT_W = 512
DN_HEADS = 4
EXPERTS = 32
TOP_K = 4
F_EXP = 1024
RET_HEADS = 4
RET_V = 512
MLP_HID = 4096
NAT_HEADS = 32
NAT_HD = 32
NAT_GROUPS = NAT_HEADS * NAT_HD // P
GRID_W = 64
REACH = 2 * GRID_W
EPS_RMS = 1e-6
EPS_LN = 1e-5
ALPHA = (2.0 * 2) ** 0.25
RPB_W = 2 * GRID_W - 1
NEG = -1e30
LEVELS = 7
CAP = 64
UNIT = KT * 256
MLP_UNITS = 2 * MLP_HID * D // (P * UNIT)
LIST = 16


class Count:

    def __init__(self, start=0):
        self.n, self.turn, self.per, self.start = start, None, 0, 0
        self.name = ''

    def at(self, k=0):
        return self.n + k if self.turn is None else self.turn * self.per + (self.n + k)

    def dma(self, slots=2, each=16):
        use = (self.n // slots + 1) * each
        return use if self.turn is None else self.turn * (self.per * each // slots) + use


@contextmanager
def turns(eng, number, per):
    with eng.Fori(0, number) as i:
        for c, step in per.items():
            c.turn, c.per, c.start = i, step, c.n
        yield i
        for c, step in per.items():
            assert c.n - c.start == step, ("a turn moves the count by", c.n - c.start, "not", step, c.name)
    for c, step in per.items():
        c.turn, c.n = None, c.start + number * step


class Pair:

    def __init__(self, banks, full, free):
        self.banks, self.full, self.free = banks, full, free


class Filler:
    def __init__(self, pe, pair):
        self.pe, self.pair, self.c = pe, pair, Count()

    def open(self):
        self.pe.wait_ge(self.pair.free, self.c.at(1))
        return self.pair.banks[self.c.n % 2]

    def close(self, last):
        last.then_inc(self.pair.full, 1)
        self.c.n += 1

    def read(self, ago=0):
        self.pe.wait_ge(self.pair.free, self.c.at(2 - ago))


class Reader:
    def __init__(self, eng, pair):
        self.eng, self.pair, self.c = eng, pair, Count()

    def take(self):
        self.eng.wait_ge(self.pair.full, self.c.at(1))
        return self.pair.banks[self.c.n % 2]

    def done(self, last):
        last.then_inc(self.pair.free, 1)
        self.c.n += 1

    def settle(self):
        self.eng.wait_ge(self.pair.free, self.c.at(2))


class GemmFiller(Filler):

    def __init__(self, pe, pair, slots, landed, half0_used, panel_done):
        super().__init__(pe, pair)
        self.others, self.panels = Count(), Count()
        self.slots, self.landed, self.half0_used, self.panel_done = slots, landed, half0_used, panel_done
        self.seen = set()

    def half(self, h):
        slot = self.panels.n % len(self.slots)
        if h not in self.seen:
            self.pe.wait_ge(self.landed[slot][h], self.panels.dma(len(self.slots)))
            self.seen.add(h)
        return self.slots[slot][:, 4 * h:4 * h + 4, :]

    def close(self, last, ends_panel=False):
        last.then_inc(self.panel_done if ends_panel else self.pair.full, 1)
        self.c.n += 1
        if ends_panel:
            self.panels.n += 1
            self.seen = set()
        else:
            self.others.n += 1

    def product(self, lhs, rhs, ends_panel=False, depth=KT, dst=lambda b: b[:, :]):
        b = self.open()
        for k in range(depth):
            v = self.half(k // 4)[:, k % 4, :]
            m = self.pe.matmul(dst(b), lhs(k, v), rhs(k, v), start=(k == 0), stop=(k == depth - 1))
            if ends_panel and k == 3:
                m.then_inc(self.half0_used, 1)
        self.close(m, ends_panel)

    def split_product(self, lhs, parts, depth=KT):
        b = self.open()
        rows, cols = P // parts, 512 // parts
        for k in range(depth):
            v = self.half(k // 4)[:, k % 4, :]
            for s in range(parts):
                m = self.pe.matmul(b[s * rows:(s + 1) * rows, 0:cols], lhs(k), v[:, s * cols:(s + 1) * cols],
                                   start=(k == 0), stop=(k == depth - 1))
            if k == 3:
                m.then_inc(self.half0_used, 1)
        self.close(m, True)


class GemmReader:

    def __init__(self, eng, pair, panel_done, credit=0):
        self.eng, self.pair, self.panel_done, self.credit = eng, pair, panel_done, credit
        self.c, self.others, self.panels = Count(), Count(), Count()

    def take(self, ends_panel=False):
        if ends_panel:
            self.eng.wait_ge(self.panel_done, self.panels.at(1 + self.credit))
            self.panels.n += 1
        else:
            self.eng.wait_ge(self.pair.full, self.others.at(1))
            self.others.n += 1
        return self.pair.banks[self.c.n % 2]

    def done(self, last):
        last.then_inc(self.pair.free, 1)
        self.c.n += 1

    def settle(self):
        self.eng.wait_ge(self.pair.free, self.c.at(2))


class Chain:

    def __init__(self, eng, sem):
        self.eng, self.sem, self.c = eng, sem, Count()

    def __call__(self, ins):
        ins.then_inc(self.sem, 1)
        self.c.n += 1
        self.eng.wait_ge(self.sem, self.c.at())


class Post:

    def __init__(self, eng, sem):
        self.eng, self.sem, self.c = eng, sem, Count()

    def send(self, ins):
        ins.then_inc(self.sem, 1)
        self.c.n += 1

    def get(self, k=1):
        self.c.n += k
        self.eng.wait_ge(self.sem, self.c.at())


CONSTS, CONST_COLS = {}, 0
for _name, _shape in (("ident", (P,)), ("upper", (P,)), ("strict", (P,)), ("lvl", (LEVELS, P)),
                      ("lcount", (3 * P,)), ("swap", (P,)), ("anti", (P,)), ("dist", (2, SEQ)),
                      ("rope", (2, 2, SEQ)), ("natmask", (GRID_W,)), ("iota", (P,)), ("tab_e", (3 * EXPERTS,)), ("tab_s", (3 * EXPERTS,)),
                      ("tab_j", (LIST,))):
    CONSTS[_name] = (CONST_COLS, _shape)
    CONST_COLS += int(np.prod(_shape))


def constants():
    c = {}
    r = np.arange(P)
    c["ident"] = r[:, None] == r[None, :]
    c["upper"] = r[:, None] <= r[None, :]
    c["strict"] = r[:, None] < r[None, :]
    c["lvl"] = np.stack([((r[None, :] >> (l + 1)) == (r[:, None] >> (l + 1)))
                         & ((r[None, :] >> l) % 2 == 1) & ((r[:, None] >> l) % 2 == 0)
                         for l in range(LEVELS)], axis=1)
    t, s = np.arange(SEQ)[:, None], np.arange(SEQ)[None, :]
    d = t - s
    seen = ((d >= 0) & (d <= 128)) * 1 + ((d >= 0) & (d % 4 == 0)) + ((d >= 0) & (d % 16 == 0))
    lc = np.where(seen > 0, np.log(np.maximum(seen, 1)), NEG)
    c["lcount"] = np.concatenate([lc[0:P, 0:P], lc[P:SEQ, :]], axis=1)
    c["swap"] = r[:, None] == (r[None, :] + 64) % P
    c["anti"] = (r[:, None] // 64 == r[None, :] // 64) & (r[:, None] % 64 == 63 - r[None, :] % 64)
    c["dist"] = np.stack([s[0][None, :] - (r[:, None] + P * n) for n in range(2)], axis=1)
    inv = (1.0 / (10000.0 ** (np.arange(0, P, 2, dtype=np.float32) / P))).astype(np.float32)
    pos = np.arange(SEQ)
    ang = [inv[r % 64][:, None] * x[None, :].astype(np.float32) for x in (pos // GRID_W, pos % GRID_W)]
    sign = np.where(r < 64, -1.0, 1.0)[:, None]
    c["rope"] = np.stack([np.stack([np.cos(x), np.sin(x) * sign], axis=1) for x in ang], axis=1)
    q, k = (r % GRID_W)[:, None], np.arange(GRID_W)[None, :]
    start = np.clip(q - 8, 0, GRID_W - 16)
    c["natmask"] = np.where((k >= start) & (k < start + 16), 0.0, NEG)[(r // 64) * 64 + 63 - r % 64]
    c["iota"] = np.broadcast_to(r[None, :] % CAP, (P, P))
    c["tab_e"] = np.broadcast_to(np.tile(np.arange(EXPERTS), 3)[None, :], (P, 3 * EXPERTS))
    c["tab_s"] = np.broadcast_to(np.repeat(np.arange(1, 4) * CAP, EXPERTS)[None, :], (P, 3 * EXPERTS))
    c["tab_j"] = np.broadcast_to(np.arange(1, LIST + 1)[None, :], (P, LIST))
    return np.concatenate([c[n].reshape(P, -1).astype(np.float32) for n in CONSTS], axis=1)


def program(nc, a, out, dbg=None):
    ctx = ExitStack()
    with ctx:
        def sb(name, *shape, dt=F32):
            return ctx.enter_context(nc.sbuf_tensor(name, [P, *shape], dt))

        def sem(name):
            return ctx.enter_context(nc.semaphore(name))

        bank = [ctx.enter_context(nc.psum_tensor(f"bank{i}", [P, 512], F32)) for i in range(8)]

        ring = sb("ring", 2, KT, 512)
        tok = sb("tok", 4, D)
        xn = sb("xn", XT, D)
        gateb = sb("gateb", 2, D)
        lnrow = sb("lnrow", 2, D)
        cst = sb("cst", CONST_COLS)

        def const(name):
            first, shape = CONSTS[name]
            v = cst[:, first:first + int(np.prod(shape))]
            if len(shape) == 2:
                return v.rearrange("p (a b) -> p a b", a=shape[0])
            if len(shape) == 3:
                return v.rearrange("p (a b c) -> p a b c", a=shape[0], b=shape[1])
            return v

        ident, upper, strict, lvl = const("ident"), const("upper"), const("strict"), const("lvl")
        lcount, swap, anti, dist = const("lcount"), const("swap"), const("anti"), const("dist")
        rope, natmask, iota = const("rope"), const("natmask"), const("iota")
        tab_e, tab_s, tab_j = const("tab_e"), const("tab_s"), const("tab_j")
        ones = sb("ones", P)
        params = sb("params", 4, P)
        csil = sb("csil", KT, 32)
        biascol = sb("biascol", 144)
        parcol = sb("parcol", 16)
        normcol = sb("normcol", 9, KT)
        convcol = sb("convcol", DN_HEADS, 12)
        modcol = sb("modcol", 144, 3)
        arow = sb("arow", 2, P)
        scol = sb("scol", 4, KT)
        diag = sb("diag", KT, P)
        stats = sb("stats", 4, 2, 6)
        mv = sb("mv", 4, 2)
        std = sb("std", 4)
        rstd = sb("rstd", 4)
        hsel = sb("hsel", 10, 2)
        gmul = sb("gmul", 4, KT)
        headp = sb("headp", 2, 4)
        dnw = sb("dnw", P)
        smallw = sb("smallw", KT * 8 + KT * EXPERTS)
        wdba = smallw[:, 0:KT * 8].rearrange("p (k n) -> p k n", k=KT)
        wr = smallw[:, KT * 8:].rearrange("p (k n) -> p k n", k=KT)
        brow = sb("brow", EXPERTS)
        lgam = sb("lgam", 8)
        idle = sb("idle", 4)
        gtmp = sb("gtmp", 2, 512)
        more_i = sb("more_i", 1, dt=I32)
        list_e = sb("list_e", LIST, dt=I32)
        list_s = sb("list_s", LIST)
        with ExitStack() as stages:
            held = lambda name, *shape: stages.enter_context(nc.sbuf_tensor(name, [P, *shape], F32))
            yacc = held("yacc", 4, D)
            hT = held("hT", KT, 512)
            hid = held("hid", KT, 512)
            scratch = held("scratch", 12820)
        hT_hi, hT_lo = sb("hT_hi", KT, 512, dt=F32R), sb("hT_lo", KT, 512, dt=F32R)
        hid_hi, hid_lo = sb("hid_hi", KT, 512, dt=F32R), sb("hid_lo", KT, 512, dt=F32R)
        w_hi, w_lo = sb("w_hi", 2, KT, 256, dt=F32R), sb("w_lo", 2, KT, 256, dt=F32R)
        mtmp = sb("mtmp", 2, 512)

        def split_slots(tiles):
            slots = [(w_hi[:, n], w_lo[:, n]) for n in range(2)]
            if tiles == 2:
                slots += [(hi[:, :, 256:512], lo[:, :, 256:512]) for hi, lo in ((hT_hi, hT_lo), (hid_hi, hid_lo))]
            return slots

        units = ring.rearrange("p s k (h n) -> p (s k h n)", h=2).rearrange("p (u k n) -> p u k n", u=4, k=KT)
        slots = [ring[:, 0], ring[:, 1]]
        wide = slots + [hT, hid]

        def carve(start, *shape):
            n = int(np.prod(shape))
            v = scratch[:, start:start + n]
            if len(shape) == 2:
                return v.rearrange("p (a b) -> p a b", a=shape[0])
            if len(shape) == 3:
                return v.rearrange("p (a b c) -> p a b c", a=shape[0], b=shape[1])
            return v

        gemm = Pair(bank[0:2], sem("gemm_full"), sem("gemm_free"))
        side = Pair(bank[2:4], sem("side_full"), sem("side_free"))
        att = Pair(bank[4:6], sem("att_full"), sem("att_free"))
        mixp = Pair(bank[6:8], sem("mix_full"), sem("mix_free"))
        landed = [[sem(f"landed_{s}{h}") for h in range(2)] for s in range(2)]
        half0_used = sem("half0_used")
        panel_done = sem("panel_done")
        consts_in = sem("consts_in")
        params_in = sem("params_in")
        tok_in = sem("tok_in")
        small_in = sem("small_in")
        dve_step = sem("dve_step")
        act_step = sem("act_step")
        act_to_pe = sem("act_to_pe")
        b2_go = sem("b2_go")
        nat_go = sem("nat_go")
        to_act = sem("to_act")
        from_act = sem("from_act")
        to_pe = sem("to_pe")
        b2_in = sem("b2_in")
        rows_in = sem("rows_in")
        rows_used = sem("rows_used")
        ones_ready = sem("ones_ready")
        count_ready = sem("count_ready")
        bias_in = [sem(f"bias_in{n}") for n in range(4)]
        bias_used = sem("bias_used")
        bias_ready = sem("bias_ready")
        unit_in = [sem(f"unit_in{n}") for n in range(4)]
        mlp_go = sem("mlp_go")
        hi_ready = sem("hi_ready")
        lo_ready = sem("lo_ready")
        unit_done = sem("unit_done")
        out_ready = sem("out_ready")
        out_done = sem("out_done")
        def expert_sems(x, n):
            return dict(
                gemm=Pair(bank[0:2], sem(x + "gemm_full"), sem(x + "gemm_free")),
                side=Pair(bank[2:4], sem(x + "side_full"), sem(x + "side_free")),
                att=Pair(bank[4:6], sem(x + "att_full"), sem(x + "att_free")),
                mix=Pair(bank[6:8], sem(x + "mix_full"), sem(x + "mix_free")),
                landed=[[sem(f"{x}landed_{s}{h}") for h in range(2)] for s in range(n)],
                half0=sem(x + "half0_used"), done=sem(x + "panel_done"), step=sem(x + "dve_step"),
                to_act=sem(x + "to_act"), from_act=sem(x + "from_act"), to_pe=sem(x + "to_pe"),
                b1=[sem(x + "b1_in0"), sem(x + "b1_in1")], b1_used=sem(x + "b1_used"))

        E = expert_sems("e_", 4)
        O = expert_sems("o_", 2)
        tiles_free = sem("tiles_free")
        further_done = sem("further_done")

        qkT = carve(0, 512)
        vtok = carve(512, 2, P)
        cin = carve(768, 3, 260)
        cy = carve(1552, 3, SEQ)
        cs = carve(2320, 3, SEQ)
        dz = carve(3088, 2, P)
        qkv = carve(3344, 6, P)
        qn = carve(4112, 2, P)
        kn = carve(4368, 2, P)
        kb = carve(4624, 2, P)
        vb = carve(4880, 2, P)
        kbg = carve(5136, P)
        qd = carve(5264, P)
        kd = carve(5392, P)
        featT = carve(5520, 7, P)
        decay = carve(6416, 2, P)
        LT = carve(6672, 2, P)
        IT = carve(6928, 2, P)
        LM = carve(7184, 2, P)
        TU = carve(7440, 4, P)
        P1 = carve(7952, 2, P)
        unew = carve(8208, 2, P)
        wT = carve(8464, P)
        state = carve(8592, P)
        osb = carve(8720, 2, P)
        gb = carve(8976, 2, P)
        cw = carve(9232, 12)
        gates = carve(9248, 10, 8)
        satt = carve(9344, 3 * P)
        pT = carve(9728, 3 * P)
        amax = carve(10112, 8)
        aden = carve(10120, 8)
        arec = carve(10128, 8)
        dss = carve(10136, 16)
        mix = hid[:, 0:4, :].rearrange("p a b -> p (a b)").rearrange("p (t n) -> p t n", t=2)
        lg = carve(0, 2, EXPERTS)
        m8 = carve(64, 2, 8)
        eq = carve(80, 2, EXPERTS)
        cum = carve(144, 2, 2, EXPERTS)
        sel = carve(272, 2, EXPERTS)
        eg = carve(336, 2, EXPERTS)
        gt = carve(400, 2, EXPERTS)
        rs = carve(464, 16)
        cntf = carve(480, EXPERTS)
        gate = carve(512, 2, EXPERTS + 1)
        pos = carve(578, 2, EXPERTS + 1)
        gT = carve(644, SEQ)
        b2sb = carve(900, D)
        flags = carve(1924, 3, EXPERTS)
        fcum = carve(2020, 2, 3 * EXPERTS)
        match = carve(2212, LIST, 3 * EXPERTS)
        match2 = carve(3748, LIST, 3 * EXPERTS)
        E0 = 5300
        pg = carve(5288, 2, 2, 2)
        OH = carve(E0, 2, CAP)
        GD = carve(E0 + 128, 2, 2, P)
        xg = carve(E0 + 640, KT, CAP)
        act_h = carve(E0 + 1152, 2, 256)
        up_h = carve(E0 + 1664, 2, 256)
        sig = carve(E0 + 2176, 2, 256)
        aT = carve(E0 + 2688, 2, 2, P)
        ysb = carve(E0 + 3200, 2, 256)
        comb = carve(E0 + 3712, 2, P)
        b1b = carve(E0 + 3968, 2, 4, 256)
        rqk = carve(0, 4, 512)
        rv = carve(2048, 4, 512)
        rg = carve(4096, 4, 512)
        dpos = carve(6144, 2, SEQ)
        dneg = carve(6656, 2, SEQ)
        Wd = carve(7168, 2, SEQ)
        Wc = carve(7680, 2, SEQ)
        We = carve(8192, 2, SEQ)
        rsT = carve(8704, 6, SEQ)
        ro = carve(10240, 4, 512)
        lgs = carve(12296, 4)
        rtmp = carve(12304, 2, SEQ)
        lgx = carve(12816, 4)
        roT = hid[:, 0:4, :]
        nq = carve(0, 2, SEQ)
        nk = carve(512, 2, 512)
        nv = carve(1536, 8, P).rearrange("p (a t) n -> p a t n", a=2)
        nbias = carve(5400, 4, 6, GRID_W)
        ns = carve(3328, 2, 512)
        nmax = carve(4352, 4)
        nneg = carve(4356, 4)
        nden = carve(4360, 4)
        nrec = carve(4364, 4)
        npT = carve(4368, 8, P).rearrange("p (a k) n -> p a k n", a=2)
        no = xn

        def param_row(src, t):
            n = src.shape[-1]
            return bass.AP(src.tensor, src.offset, [[0, P], [1, n]])

        block = ctx.enter_context(nc.Block())


        @block.sync
        def _(sp):
            panels = Count()

            def panel(src, width=512, start=False, at_slots=slots, sems=(landed, half0_used, panel_done),
                      panels=panels, credit=0):
                arrived, half0, done = sems
                slot = panels.n % len(at_slots)
                for h, used in enumerate((half0, done)):
                    if not start:
                        sp.wait_ge(used, panels.at(1 - len(at_slots) + credit))
                    dst = at_slots[slot][:, 4 * h:4 * h + 4, 0:width]
                    part = 4 * width
                    sp.dma_start(dst, src[:, h * part:(h + 1) * part].rearrange("p (k n) -> p k n", k=4))\
                        .then_inc(arrived[slot][h], 16)
                panels.n += 1

            for j in range(2):
                panel(a["panels_a"][j], start=True)
            for name, row0 in (("x", 0), ("ctx_2", 2)):
                sp.dma_start(tok[:, row0:row0 + 2, :],
                             a[name][0].rearrange("(t p) n -> p t n", p=P)).then_inc(tok_in, 16)

            def at(src, index):
                return src[bass.ds(index, 1)].rearrange("a p n -> (a p) n")

            def stream(src, first, number, **kw):
                with turns(sp, (number - first) // 2, {panels: 2}) as i:
                    for j in range(2):
                        panel(at(src, i * 2 + (first + j)), **kw)

            unit_loads = Count()

            def unit(src, h, start=False):
                n = unit_loads.n % 4
                if not start:
                    sp.wait_ge(lo_ready, unit_loads.at(-3))
                sp.dma_start(units[:, n].rearrange("p k n -> p (k n)"), src[:, h * UNIT:(h + 1) * UNIT])\
                    .then_inc(unit_in[n], 16)
                unit_loads.n += 1

            def stream_units(src):
                for j in range(2):
                    sp.wait_ge(panel_done, panels.at(j - 1))
                    for h in range(2):
                        unit(src[j], h, start=True)
                with turns(sp, src.shape[0] // 2 - 1, {unit_loads: 4}) as i:
                    for j in range(4):
                        unit(at(src, i * 2 + (2 + j // 2)), j % 2)

            stream(a["panels_a"], 2, a["panels_a"].shape[0])
            per = dict(at_slots=wide, sems=(E["landed"], E["half0"], E["done"]), panels=Count())
            pe_ = a["panels_e"]
            sp.wait_ge(panel_done, panels.at())
            for j in range(2):
                panel(pe_[j], start=True, **per)
            sp.wait_ge(tiles_free, 1)
            for j in range(2, 4):
                panel(pe_[j], start=True, **per)
            with turns(sp, pe_.shape[0] // 4 - 1, {per["panels"]: 4}) as i:
                for j in range(4):
                    panel(at(pe_, i * 4 + (4 + j)), **per)
            sp.wait_ge(E["done"], per["panels"].at())
            sp.wait_ge(count_ready, 1)
            more = sp.value_load(more_i[0:1, 0:1], min_val=0, max_val=LIST - 1)
            with sp.If(more > 0):
                sp.sem_inc(O["half0"], 2)
                sp.sem_inc(O["done"], 2)
                per = dict(sems=(O["landed"], O["half0"], O["done"]), panels=Count(), credit=2)
                with turns(sp, more, {per["panels"]: 6}) as i:
                    e = sp.value_load(list_e[0:1, bass.ds(i, 1)], min_val=0, max_val=EXPERTS - 1)
                    for j in range(6):
                        panel(at(pe_, e * 6 + j), **per)
                sp.wait_ge(O["done"], per["panels"].at(2))
                sp.sem_inc(further_done, 1)
            stream(a["panels_b"], 0, a["panels_b"].shape[0])
            stream_units(a["panels_m0"])
            for j in range(2):
                sp.wait_ge(lo_ready, unit_loads.at(2 * j - 2))
                panel(a["panels_n"][j], start=True, width=3 * P)
            stream(a["panels_n"], 2, a["panels_n"].shape[0], width=3 * P)
            stream(a["panels_c"], 0, a["panels_c"].shape[0])
            stream_units(a["panels_m1"])
            sp.wait_ge(out_ready, 1)
            sp.dma_start(out[0].rearrange("(t p) n -> p t n", p=P), tok[:, 0:2, :]).then_inc(out_done, 16)
            sp.wait_ge(out_done, 16)

        @block.gpsimd
        def _(pool):
            pool.dma_start(cst[:, :], a["consts"]).then_inc(consts_in, 16)
            pool.dma_start(params[:, :, :], a["params"].rearrange("(t p) n -> p t n", p=P)).then_inc(params_in, 16)
            pool.memset(ones[:, :], 1.0).then_inc(ones_ready, 1)
            pool.memset(cin[:, :, 0:4], 0.0).then_inc(ones_ready, 1)
            pool.dma_start(smallw[:, :], a["smallw"]).then_inc(small_in, 16)
            pool.dma_start(headp[:, 0, :], param_row(a["A_log"][0], 4)).then_inc(small_in, 16)
            pool.dma_start(headp[:, 1, :], param_row(a["dt_bias"][0], 4)).then_inc(small_in, 16)
            pool.dma_start(dnw[:, :], param_row(a["dn_norm_w"][0], P)).then_inc(small_in, 16)
            pool.dma_start(brow[:, :], param_row(a["b_router"][0], EXPERTS)).then_inc(small_in, 16)
            pool.dma_start(lgam[:, :], param_row(a["ret_decay"], 8)).then_inc(small_in, 16)
            pool.dma_start(lnrow[:, 0, :], param_row(a["final_norm_w"], D)).then_inc(rows_in, 16)
            pool.wait_ge(b2_go, 1)
            pool.dma_start(b2sb[0:EXPERTS, :], a["b2"][0]).then_inc(b2_in, 16)

            b1 = a["b1"]

            def load_b1(e, parity, arrived):
                for s in range(2):
                    src = bass.AP(b1.tensor, e * (2 * F_EXP) + 256 * s, [[0, CAP], [512, 4], [1, 256]])
                    pool.dma_start(b1b[CAP * s:CAP * s + CAP, parity, :, :], src).then_inc(arrived[parity], 16)

            uses = Count()
            for p in range(2):
                load_b1(p, p, E["b1"])
                uses.n += 1
            with turns(pool, EXPERTS // 2 - 1, {uses: 2}) as i:
                for p in range(2):
                    pool.wait_ge(E["b1_used"], uses.at(-1))
                    load_b1(i * 2 + (2 + p), p, E["b1"])
                    uses.n += 1
            pool.wait_ge(E["b1_used"], uses.at())
            pool.wait_ge(count_ready, 1)
            more = pool.value_load(more_i[0:1, 0:1], min_val=0, max_val=LIST - 1)
            with pool.If(more > 0):
                pool.sem_inc(O["b1_used"], 1)
                uses = Count()
                with turns(pool, more, {uses: 1}) as i:
                    e = pool.value_load(list_e[0:1, bass.ds(i, 1)], min_val=0, max_val=EXPERTS - 1)
                    pool.wait_ge(O["b1_used"], uses.at(1))
                    load_b1(e, 0, O["b1"])
                    uses.n += 1
            lo = Count()

            def lower_parts(tiles):
                at_slots = split_slots(tiles)
                with turns(pool, MLP_UNITS // 4, {lo: 4}) as i:
                    for n in range(4):
                        pool.wait_ge(hi_ready, lo.at(1))
                        upper, lower = at_slots[n % len(at_slots)]
                        pool.tensor_tensor(lower, units[:, n], upper, ALU.subtract)\
                            .then_inc(lo_ready, 1)
                        lo.n += 1

            for n in range(4):
                if n % 2:
                    lower_parts(4 if n == 1 else 2)
                pool.wait_ge(rows_used, n + 1)
                for j, name in enumerate(("ln_g_2", "ln_b_2")):
                    pool.dma_start(lnrow[:, j, :], param_row(a[name][n // 2, n % 2], D)).then_inc(rows_in, 16)
                if n == 1:
                    uses = Count()
                    rp = a["rpb"]

                    def load_bias(uses, head, parity, start=False):
                        if not start:
                            pool.wait_ge(bias_used, uses.at(-3))
                        for b in range(2):
                            src = bass.AP(rp.tensor, head * (15 * RPB_W) + (5 - b) * RPB_W,
                                          [[1, GRID_W], [RPB_W, 6], [1, GRID_W]])
                            pool.dma_start(nbias[64 * b:64 * b + 64, parity, :, :], src)\
                                .then_inc(bias_in[parity], 16)
                        uses.n += 1

                    def mask_bias(masked, parity):
                        pool.wait_ge(bias_in[parity], masked.dma(4, 32))
                        pool.tensor_tensor(nbias[:, parity, :, :], nbias[:, parity, :, :],
                                           natmask.unsqueeze(1).to_broadcast([P, 6, GRID_W]), ALU.add)\
                            .then_inc(bias_ready, 1)
                        masked.n += 1

                    pool.wait_ge(nat_go, 1)
                    masked = Count()
                    pool.wait_ge(consts_in, 16)
                    for p in range(4):
                        load_bias(uses, p, p, start=True)
                    for p in range(2):
                        mask_bias(masked, p)
                    with turns(pool, NAT_HEADS // 4 - 1, {uses: 4, masked: 4}) as i:
                        for p in range(4):
                            load_bias(uses, i * 4 + (4 + p), p)
                            mask_bias(masked, (p + 2) % 4)
                    for p in range(2):
                        mask_bias(masked, 2 + p)

        @block.scalar
        def _(act):
            step = Chain(act, act_step)
            asked = Post(act, to_act)
            to_dve = Post(act, from_act)
            to_tensor = Post(act, act_to_pe)

            act.wait_ge(params_in, 16)
            to_tensor.send(act.activation(params[:, 0, :], params[:, 0, :], ACT.Silu))

            def root(n, post=None):
                asked.get()
                to_dve.send(act.activation(std[:, 0:n], mv[:, 0:n, 1], ACT.Sqrt))

            root(XT)
            act.wait_ge(small_in, 96)
            asked.get()
            act.activation(gates[:, 0, :], gates[:, 0, :], ACT.Sigmoid)
            step(act.activation(gates[:, 2, :], gates[:, 2, :], ACT.Abs))
            step(act.activation(gates[:, 2, :], gates[:, 2, :], ACT.Exp, scale=-1.0))
            act.activation(headp[:, 0, :], headp[:, 0, :], ACT.Exp)
            to_dve.send(act.activation(gates[:, 3, :], gates[:, 2, :], ACT.Ln, bias=1.0))
            asked.get()
            act.activation(gates[:, 5, :], gates[:, 4, :], ACT.Exp)
            to_dve.send(act.activation(gates[:, 6, :], gates[:, 6, :], ACT.Exp))

            with turns(act, DN_HEADS, {asked.c: 6, to_dve.c: 3, to_tensor.c: 3}) as i:
                asked.get()
                act.activation(dz[:, :, :], dz[:, :, :], ACT.Silu)
                to_tensor.send(act.activation(cs[:, :, :], cy[:, :, :], ACT.Silu))
                asked.get()
                to_dve.send(act.activation(dss[:, 4:8], dss[:, 0:4], ACT.Sqrt))
                asked.get()
                to_dve.send(act.activation(decay[:, :, :], decay[:, :, :], ACT.Exp))
                for h in range(2):
                    asked.get()
                    for t, cols in enumerate((slice(0, P), slice(P, 3 * P))):
                        m = act.activation(satt[:, cols], satt[:, cols], ACT.Exp, bias=amax[:, t:t + 1],
                                           accum_out=aden[:, t:t + 1])
                    to_tensor.send(m)
                asked.get()
                to_dve.send(act.activation(dss[:, 12:14], dss[:, 8:10], ACT.Sqrt))

            root(XT)
            asked.get()
            for t in range(XT):
                m = act.activation(eg[:, t, :], lg[:, t, :], ACT.Exp, bias=rs[:, t:t + 1])
            to_dve.send(m)

            def expert_gates(asked, to_dve, number, each):
                with turns(act, number, {asked.c: 2 * each, to_dve.c: 2 * each}) as i:
                    for _ in range(each):
                        for c in range(2):
                            asked.get()
                            to_dve.send(act.activation(sig[:, c, :], act_h[:, c, :], ACT.Sigmoid, scale=1.702))

            expert_gates(Post(act, E["to_act"]), Post(act, E["from_act"]), EXPERTS // 2, 2)
            act.wait_ge(count_ready, 1)
            more = act.value_load(more_i[0:1, 0:1], min_val=0, max_val=LIST - 1)
            with act.If(more > 0):
                expert_gates(Post(act, O["to_act"]), Post(act, O["from_act"]), more, 1)
            root(XT)

            asked.get()
            to_dve.send(act.activation(lgam[:, :], lgam[:, :], ACT.Exp))
            with turns(act, RET_HEADS, {asked.c: 3, to_dve.c: 3}) as i:
                asked.get()
                act.activation(Wd[:, :, :], dpos[:, :, :], ACT.Exp, scale=lgs[:, 0:1])
                act.activation(We[:, :, :], dneg[:, :, :], ACT.Exp, scale=lgs[:, 1:2])
                act.activation(Wc[:, :, :], dist[:, :, :], ACT.Exp, scale=lgs[:, 0:1], bias=lgs[:, 2:3])
                to_dve.send(act.activation(rtmp[:, :, :], dist[:, :, :], ACT.Exp, scale=lgx[:, 0:1],
                                           bias=lgs[:, 3:4]))
                asked.get()
                to_dve.send(act.activation(rg[:, :, :], rg[:, :, :], ACT.Silu))
                root(4)
            hi = Count()

            def upper_parts(tiles):
                at_slots = split_slots(tiles)
                asked_go.get()
                with turns(act, MLP_UNITS // 4, {hi: 4}) as i:
                    for n in range(4):
                        act.wait_ge(unit_in[n], hi.dma(4))
                        act.wait_ge(unit_done, hi.at(3 - len(at_slots)))
                        act.copy(at_slots[n % len(at_slots)][0], units[:, n]).then_inc(hi_ready, 1)
                        hi.n += 1

            asked_go = Post(act, mlp_go)
            root(4)
            upper_parts(4)
            root(4)
            with turns(act, NAT_GROUPS // 2, {asked.c: 16}) as i:
                for n in range(16):
                    asked.get()
                    act.activation(ns[:, n % 2, :], att.banks[n % 2][:, :], ACT.Exp, bias=nneg[:, n % 2:n % 2 + 1],
                                   accum_out=nden[:, n % 2:n % 2 + 1]).then_inc(att.free, 1)
            root(XT)
            upper_parts(2)
            root(XT)

        @block.tensor
        def _(pe):
            G = GemmFiller(pe, gemm, slots, landed, half0_used, panel_done)
            S, A, M = Filler(pe, side), Filler(pe, att), Filler(pe, mixp)
            from_dve = Post(pe, to_pe)
            from_a = Post(pe, act_to_pe)
            per_gemm = lambda fills, panels: {G.c: fills, G.others: fills - panels, G.panels: panels}

            pe.wait_ge(consts_in, 16)
            pe.wait_ge(params_in, 16)
            pe.wait_ge(ones_ready, 2)
            from_a.get()
            b = S.open()
            for n in range(4):
                m = pe.transpose(b[:, n * P:n * P + P], params[:, n, :], ident)
            S.close(m)
            S.read()

            def ada_product(j):
                G.split_product(lambda k: csil[:, k, :], 4)

            def ada_turn(j, ago):
                G.read(ago)
                b = S.open()
                S.close(pe.transpose(b[:, 0:P], arow[:, j % 2, :], ident))

            def ada_four():
                for j in range(4):
                    ada_product(j)
                    if j:
                        ada_turn(j - 1, 1)
                ada_turn(3, 0)

            ada_four()
            with turns(pe, 2, {**per_gemm(4, 4), S.c: 4}) as i:
                ada_four()

            def spread_gate(number):
                for _ in range(number):
                    from_dve.get()
                    for c in range(2):
                        b = S.open()
                        S.close(pe.matmul(b[:, :], ones[:, :], diag[:, 4 * c:4 * c + 4, :], start=True, stop=True))
                    S.read()

            def to_features(src, tiles):
                from_dve.get()
                for k in range(KT):
                    b = S.open()
                    for t in range(tiles):
                        m = pe.transpose(b[:, t * P:t * P + P], src(t, k), ident)
                    S.close(m)
                S.read()

            x_part = lambda t, k: xn[:, t, k * P:k * P + P]
            tok_part = lambda t, k: tok[:, t, k * P:k * P + P]
            mix_part = lambda t, k: mix[:, t, k * P:k * P + P]
            spread_gate(1)
            to_features(x_part, XT)

            pe.wait_ge(small_in, 96)
            b = S.open()
            for t in range(XT):
                for k in range(KT):
                    m = pe.matmul(b[:, 8 * t:8 * t + 8], hT[:, k, t * P:t * P + P], wdba[:, k, :],
                                  start=(k == 0), stop=(k == KT - 1))
            S.close(m)
            from_dve.get()
            b = S.open()
            pe.matmul(b[:, 0:8], upper, gates[:, 1, :], start=True, stop=True)
            S.close(pe.matmul(b[:, 8:16], ones[:, :], gates[:, 1, :], start=True, stop=True))

            def mixer_products():
                def features(b, dst, cols, mark):
                    for k in range(KT):
                        m = pe.matmul(b[:, dst:dst + SEQ], G.half(k // 4)[:, k % 4, cols:cols + P],
                                      hT[:, k, 0:SEQ], start=(k == 0), stop=(k == KT - 1))
                    return m

                def tokens(b, dst, cols, mark):
                    for t in range(XT):
                        for k in range(KT):
                            m = pe.matmul(b[:, dst + t * P:dst + t * P + P], hT[:, k, t * P:t * P + P],
                                          G.half(k // 4)[:, k % 4, cols:cols + P],
                                          start=(k == 0), stop=(k == KT - 1))
                            if mark and t == XT - 1 and k == 3:
                                m.then_inc(half0_used, 1)
                    return m

                b = G.open()
                features(b, 0, 0, False)
                G.close(features(b, SEQ, P, False))
                b = G.open()
                G.close(tokens(b, 0, 2 * P, True), ends_panel=True)
                b = G.open()
                features(b, 0, 0, False)
                G.close(features(b, SEQ, P, False))
                b = G.open()
                features(b, 0, 2 * P, False)
                G.close(tokens(b, SEQ, 3 * P, True), ends_panel=True)

            with turns(pe, DN_HEADS, {**per_gemm(10, 8), S.c: 30, A.c: 6, from_dve.c: 9, from_a.c: 3}) as i:
                mixer_products()
                def att_scores(h):
                    r = slice(64 * h, 64 * h + 64)
                    b = A.open()
                    pe.matmul(b[:, 0:P], qkT[r, 0:P], qkT[r, SEQ:SEQ + P], start=True, stop=True)
                    A.close(pe.matmul(b[:, P:3 * P], qkT[r, P:SEQ], qkT[r, SEQ:2 * SEQ], start=True, stop=True))

                def att_turn(h):
                    from_a.get()
                    b = A.open()
                    for n in range(3):
                        m = pe.transpose(b[:, n * P:n * P + P], satt[:, n * P:n * P + P], ident)
                    A.close(m)

                def att_values(h):
                    r = slice(64 * h, 64 * h + 64)
                    A.read()
                    b = A.open()
                    pe.matmul(b[:, 0:64], pT[:, 0:P], vtok[:, 0, r], start=True, stop=True)
                    pe.matmul(b[:, 64:128], pT[:, P:2 * P], vtok[:, 0, r], start=True, stop=False)
                    A.close(pe.matmul(b[:, 64:128], pT[:, 2 * P:3 * P], vtok[:, 1, r], start=False, stop=True))

                beside = {0: [(att_scores, 0)], 1: [(att_turn, 0)], 2: [(att_values, 0), (att_scores, 1)],
                          3: [(att_turn, 1)], 4: [(att_values, 1)]}
                from_a.get()
                for ns_ in (range(4), range(4, 6)):
                    b = S.open()
                    for c, n in enumerate(ns_):
                        m = pe.transpose(b[:, c * P:c * P + P], cs[:, n // 2, (n % 2) * P:(n % 2) * P + P], ident)
                    S.close(m)
                from_dve.get()
                b = S.open()
                for n in range(2):
                    m = pe.matmul(b[:, n * P:n * P + P], gb[:, n, :], upper, start=True, stop=True)
                S.close(m)
                from_dve.get()
                for srcs in ((kn[:, 0, :], kn[:, 1, :], kb[:, 0, :], kb[:, 1, :]),
                             (qn[:, 0, :], qn[:, 1, :], qd[:, :])):
                    b = S.open()
                    for c, src in enumerate(srcs):
                        m = pe.transpose(b[:, c * P:c * P + P], src, ident)
                    S.close(m)
                S.read()
                b = S.open()
                for n in range(2):
                    pe.matmul(b[:, n * P:n * P + P], featT[:, n, :], featT[:, 2 + n, :], start=True, stop=True)
                    m = pe.matmul(b[:, (2 + n) * P:(3 + n) * P], featT[:, n, :], featT[:, 4 + n, :],
                                  start=True, stop=True)
                S.close(m)
                for l in range(LEVELS):
                    from_dve.get()
                    b = S.open()
                    for n in range(2):
                        m = pe.matmul(b[:, n * P:n * P + P], LM[:, n, :], TU[:, n, :], start=True, stop=True)
                    S.close(m)
                    if l < 6:
                        ada_product(l)
                    for part, h in beside.get(l, ()):
                        part(h)
                    S.read()
                    b = S.open()
                    for n in range(2):
                        pe.matmul(b[:, n * P:n * P + P], TU[:, 2 + n, :], P1[:, n, :], start=True, stop=True)
                        m = pe.matmul(b[:, (2 + n) * P:(3 + n) * P], P1[:, n, :], TU[:, 2 + n, :],
                                      start=True, stop=True)
                    S.close(m)
                    if l < 6:
                        ada_turn(l, 0)
                    if l < LEVELS - 1:
                        S.read(1 if l < 6 else 0)
                S.read()
                b = S.open()
                for n in range(2):
                    pe.matmul(b[:, n * P:n * P + P], TU[:, 2 + n, :], vb[:, n, :], start=True, stop=True)
                S.close(pe.matmul(b[:, 2 * P:3 * P], kbg[:, :], TU[:, 3, :], start=True, stop=True))
                S.read()
                b = S.open()
                pe.matmul(b[:, 0:P], IT[:, 0, :], unew[:, 0, :], start=True, stop=True)
                S.close(pe.matmul(b[:, P:2 * P], kd[:, :], unew[:, 0, :], start=True, stop=True))
                S.read()
                b = S.open()
                S.close(pe.matmul(b[:, 0:P], wT[:, :], state[:, :], start=True, stop=True))
                S.read()
                b = S.open()
                pe.matmul(b[:, 0:P], featT[:, 6, :], state[:, :], start=True, stop=False)
                S.close(pe.matmul(b[:, 0:P], IT[:, 1, :], unew[:, 1, :], start=False, stop=True))

            to_features(mix_part, XT)

            def rows_product(tiles):
                for t in range(tiles):
                    G.product(lambda k, v: hT[:, k, t * P:t * P + P], lambda k, v: v, ends_panel=(t == tiles - 1))

            for c in range(2):
                rows_product(XT)

            to_features(x_part, XT)
            b = S.open()
            for t in range(XT):
                for k in range(KT):
                    m = pe.matmul(b[:, EXPERTS * t:EXPERTS * (t + 1)], hT[:, k, t * P:t * P + P], wr[:, k, :],
                                  start=(k == 0), stop=(k == KT - 1))
            S.close(m)
            from_dve.get()
            b = S.open()
            pe.matmul(b[:, 0:EXPERTS], strict, sel[:, 0, :], start=True, stop=True)
            pe.matmul(b[:, EXPERTS:2 * EXPERTS], strict, sel[:, 1, :], start=True, stop=False)
            pe.matmul(b[:, EXPERTS:2 * EXPERTS], ones[:, :], sel[:, 0, :], start=False, stop=True)
            pe.matmul(b[:, 2 * EXPERTS:3 * EXPERTS], ones[:, :], sel[:, 0, :], start=True, stop=False)
            S.close(pe.matmul(b[:, 2 * EXPERTS:3 * EXPERTS], ones[:, :], sel[:, 1, :], start=False, stop=True))
            from_dve.get()
            b = S.open()
            for t in range(XT):
                m = pe.transpose(b[0:EXPERTS, t * P:t * P + P], gate[:, t, 0:EXPERTS], ident)
            S.close(m)
            S.read()
            pe.wait_ge(b2_in, 16)
            for t in range(XT):
                for c in range(2):
                    b = S.open()
                    S.close(pe.matmul(b[:, :], gT[0:EXPERTS, t * P:t * P + P], b2sb[0:EXPERTS, 512 * c:512 * c + 512],
                                      start=True, stop=True))
            S.read()

            def expert_filler(x, at_slots):
                return (GemmFiller(pe, x["gemm"], at_slots, x["landed"], x["half0"], x["done"]),
                        Filler(pe, x["side"]), Filler(pe, x["att"]), Filler(pe, x["mix"]), Post(pe, x["to_pe"]))

            def gather(A, from_dve):
                from_dve.get()
                b = A.open()
                for k in range(KT):
                    for t in range(XT):
                        m = pe.matmul(b[:, k * CAP:(k + 1) * CAP], xn[:, t, k * P:k * P + P], OH[:, t, :],
                                      start=(t == 0), stop=(t == XT - 1))
                A.close(m)

            def expert(fillers, parity, ahead):
                G, S, A, M, from_dve = fillers

                def turn_act(c):
                    from_dve.get()
                    b = S.open()
                    for n in range(2):
                        m = pe.transpose(b[:, n * P:n * P + P], act_h[:, c, n * P:n * P + P], ident)
                    S.close(m)

                if not ahead:
                    gather(A, from_dve)
                A.read()
                for _ in range(3):
                    G.split_product(lambda k: xg[:, k, :], 2)
                turn_act(0)
                G.split_product(lambda k: xg[:, k, :], 2)
                if ahead:
                    gather(A, from_dve)
                b = A.open()
                for t in range(XT):
                    m = pe.transpose(b[:, t * P:t * P + P], GD[:, parity, t, :], ident)
                A.close(m)
                turn_act(1)
                S.read()
                for c in range(2):
                    G.split_product(lambda k: aT[:, k // 4, k % 2, CAP * (k % 4 // 2):CAP * (k % 4 // 2) + CAP], 2)
                A.read()
                G.read()
                for t in range(XT):
                    M.read()
                    for c in range(2):
                        for s in range(2):
                            r = slice(CAP * s, CAP * s + CAP)
                            m = pe.matmul(M.pair.banks[s][:, 256 * c:256 * c + 256], comb[r, t, :], ysb[r, c, :],
                                          start=True, stop=True)
                            if c == 1:
                                M.close(m)

            counts = lambda f, n: {f[0].c: 6 * n, f[0].panels: 6 * n, f[1].c: 2 * n, f[2].c: 2 * n,
                                   f[3].c: 4 * n, f[4].c: 3 * n}
            f = expert_filler(E, wide)
            G.read()
            S.read()
            A.read()
            spread_gate(1)
            gather(f[2], f[4])
            f[2].c.n += 1
            m = pe.transpose(f[2].pair.banks[1][:, 0:P], ident, ident)
            m.then_inc(f[2].pair.full, 1)
            with turns(pe, EXPERTS // 2, counts(f, 2)) as i:
                for e in range(2):
                    expert(f, e, True)
            for x in f[0:4]:
                x.read()
            pe.wait_ge(count_ready, 1)
            more = pe.value_load(more_i[0:1, 0:1], min_val=0, max_val=LIST - 1)
            with pe.If(more > 0):
                f = expert_filler(O, slots)
                with turns(pe, more, counts(f, 1)) as i:
                    expert(f, 0, False)
                for x in f[0:4]:
                    x.read()
            to_features(tok_part, 4)
            spread_gate(2)
            with turns(pe, RET_HEADS, {**per_gemm(20, 4), S.c: 6, A.c: 6, M.c: 4, from_dve.c: 2}) as i:
                for u in range(4):
                    G.product(lambda k, v: v[:, u * P:u * P + P], lambda k, v: hT[:, k, :], ends_panel=(u == 3))
                G.read()
                for n in range(2):
                    b = S.open()
                    for j in range(2):
                        m = pe.matmul(b[:, j * SEQ:(j + 1) * SEQ], swap, rqk[:, 2 * n + j, 0:SEQ], start=True, stop=True)
                    S.close(m)
                rows_product(4)
                rows_product(4)
                from_dve.get()
                for n in range(6):
                    keys, queries = (n, 0) if n < 4 else (n - 2, SEQ)
                    b = A.open()
                    for c in range(2):
                        m = pe.matmul(b[:, 0:SEQ], rqk[:, 2 + c, keys * P:keys * P + P], rqk[:, c, queries:queries + SEQ],
                                      start=(c == 0), stop=(c == 1))
                    A.close(m)
                A.read()
                for t in range(4):
                    b = M.open()
                    src = [(n, n) for n in range(4)] if t < 2 else [(4, 2), (5, 3)]
                    for n, key in src:
                        m = pe.matmul(b[:, :], rsT[:, n, (t % 2) * P:(t % 2) * P + P], rv[:, key, :],
                                      start=(n == src[0][0]), stop=(n == src[-1][0]))
                    M.close(m)
                from_dve.get()
                for k in range(4):
                    b = S.open()
                    for t in range(4):
                        m = pe.transpose(b[:, t * P:t * P + P], ro[:, t, k * P:k * P + P], ident)
                    S.close(m)
                S.read()
                for c in range(2):
                    for t in range(4):
                        b = G.open()
                        for k in range(4):
                            m = pe.matmul(b[:, :], roT[:, k, t * P:t * P + P], G.half(c)[:, k, :],
                                          start=(k == 0), stop=(k == 3))
                            if c == 1 and t == 0 and k == 0:
                                m.then_inc(half0_used, 1)
                        G.close(m, ends_panel=(c == 1 and t == 3))

            lo_units = Count()

            def mlp(tiles):
                width = tiles * P
                three = ((0, 0), (0, 1), (1, 0))
                at_slots = split_slots(tiles)
                cols, rows = (hT_hi, hT_lo), (hid_hi, hid_lo)

                def close(m, ends_unit):
                    m.then_inc(unit_done if ends_unit else gemm.full, 1)
                    G.c.n += 1
                    if ends_unit:
                        lo_units.n += 1
                    else:
                        G.others.n += 1

                spread_gate(tiles // 2)
                to_features(tok_part, tiles)
                from_dve.get()
                with turns(pe, 4, {G.c: 8 + 2 * tiles, G.others: 2 * tiles, lo_units: 8, from_dve.c: 1}) as i:
                    for j in range(4):
                        pe.wait_ge(lo_ready, lo_units.at(1))
                        w = at_slots[j % len(at_slots)]
                        for u in range(2):
                            b = G.open()
                            for k in range(KT):
                                for n, (x, y) in enumerate(three):
                                    m = pe.matmul(b[:, 0:width], w[x][:, k, u * P:u * P + P],
                                                  cols[y][:, k, 0:width], start=(k == n == 0),
                                                  stop=(k == KT - 1 and n == 2))
                            close(m, u == 1)
                    from_dve.get()
                    for j in range(4):
                        pe.wait_ge(lo_ready, lo_units.at(1))
                        w = at_slots[j % len(at_slots)]
                        for t in range(0, tiles, 2):
                            b = G.open()
                            for u in range(2):
                                for k in range(KT):
                                    for n, (x, y) in enumerate(three):
                                        m = pe.matmul(b[:, u * 256:u * 256 + 256],
                                                      rows[x][:, k, (t + u) * P:(t + u + 1) * P],
                                                      w[y][:, k, :], start=(k == n == 0),
                                                      stop=(k == KT - 1 and n == 2))
                            close(m, t == tiles - 2)

            mlp(4)

            spread_gate(1)
            to_features(tok_part, 4)
            heads = Count()

            def project(part):
                b = G.open() if part in (0, 1, 3) else G.pair.banks[G.c.n % 2]
                if part < 3:
                    width = 512 if part else SEQ
                    for k in (range(8), range(4), range(4, 8))[part]:
                        first = P if part else 0
                        m = pe.matmul(b[:, 0:width], G.half(k // 4)[:, k % 4, first:first + P], hT[:, k, 0:width],
                                      start=(k == 0), stop=(k == KT - 1))
                else:
                    for t in range(2 * part - 6, 2 * part - 4):
                        for k in range(KT):
                            m = pe.matmul(b[:, t * P:t * P + P], hT[:, k, t * P:t * P + P],
                                          G.half(k // 4)[:, k % 4, 2 * P:3 * P], start=(k == 0), stop=(k == KT - 1))
                            if t == 3 and k == 3:
                                m.then_inc(half0_used, 1)
                if part in (0, 2, 4):
                    G.close(m, ends_panel=(part == 4))

            def scores(n, p):
                h, t, p = n % 8 // 2, n % 2, (p + n // 8) % 2
                r = slice(NAT_HD * h, NAT_HD * h + NAT_HD)
                b = A.open()
                if t == 0:
                    pe.wait_ge(bias_ready, heads.at(1))
                pe.matmul(b[:, :], nq[r, p, t * P:t * P + P], nk[r, p, :], start=True, stop=False)
                A.close(pe.matmul(b[:, 0:SEQ], anti, nbias[:, heads.n % 4, 2 - 2 * t:6 - 2 * t, :],
                                  start=False, stop=True))
                if t == 1:
                    heads.n += 1

            def turn_probs(n, ago):
                A.read(ago)
                b = M.open()
                for k in range(4):
                    m = pe.transpose(b[:, k * P:k * P + P], ns[:, n % 2, k * P:k * P + P], ident)
                M.close(m)

            def group(p, last=False):
                for n in range(8):
                    if n == 6:
                        G.read()
                    if n < 6 or not last:
                        scores(n + 2, p)
                    if n < 7 or not last:
                        turn_probs(n + 1, 1 if n < 6 or not last else 0)
                    if n < 5 and not last:
                        project(n)
                    M.read(1 if n < 7 or not last else 0)
                    b = S.open()
                    h = n // 2
                    for k in range(4):
                        m = pe.matmul(b[:, 0:NAT_HD], npT[:, n % 2, k, :], nv[:, p, k, NAT_HD * h:NAT_HD * (h + 1)],
                                      start=(k == 0), stop=(k == 3))
                    S.close(m)

            for part in range(5):
                project(part)
            G.read()
            scores(0, 0)
            scores(1, 0)
            turn_probs(0, 1)
            with turns(pe, NAT_GROUPS // 2 - 1, {**per_gemm(6, 2), S.c: 16, A.c: 16, M.c: 16, heads: 8}) as i:
                for p in range(2):
                    group(p)
            group(0)
            group(1, last=True)
            to_features(x_part, XT)
            for c in range(2):
                rows_product(XT)
            mlp(2)

        @block.vector
        def _(dve):
            step = Chain(dve, dve_step)
            G = GemmReader(dve, gemm, panel_done)
            S, A, M = Reader(dve, side), Reader(dve, att), Reader(dve, mixp)
            ask = Post(dve, to_act)
            from_a = Post(dve, from_act)
            to_tensor = Post(dve, to_pe)
            per_gemm = lambda fills, panels: {G.c: fills, G.others: fills - panels, G.panels: panels}
            tt, ts, stt, copy = dve.tensor_tensor, dve.tensor_scalar, dve.scalar_tensor_tensor, dve.tensor_copy

            def col(tile, *index):
                v = tile[(slice(None), *index[:-1], slice(index[-1], index[-1] + 1))]
                return v

            for pair in (gemm, side, att, mixp):
                dve.sem_inc(pair.free, 2)
            b = S.take()
            step(dve.memset(csil[:, :, :], 0.0))
            copy(csil[:, :, 0:3], b[:, 0:3 * KT].rearrange("p (c k) -> p k c", c=3))
            copy(biascol[:, 0:48], b[:, 2 * P:2 * P + 48])
            copy(biascol[:, 48:144], b[:, P:P + 96])
            copy(parcol[:, 0:16], b[:, 2 * P + 48:2 * P + 64])
            copy(normcol[:, :, :], b[:, 3 * P:3 * P + 72].rearrange("p (n k) -> p n k", k=KT))
            S.done(copy(convcol[:, :, :], b[:, 2 * P + 64:2 * P + 112].rearrange("p (h n) -> p h n", h=4)))

            def ada_four(first):
                for j in range(5):
                    if j < 4:
                        b = G.take(ends_panel=True)
                        G.done(copy(arow[:, j % 2, :], b[:, 0:P]))
                    if j:
                        b = S.take()
                        dst = modcol[:, 4 * (j - 1):4 * j, :] if first is None else \
                            modcol[:, bass.ds(first + 4 * (j - 1), 4), :]
                        S.done(copy(dst, b[:, 0:P].rearrange("p (n c) -> p n c", n=4)[:, :, 0:3]))

            ada_four(None)
            with turns(dve, 2, {**per_gemm(4, 4), S.c: 4}) as i:
                ada_four(i * 16 + 16)
            S.settle()

            def add_bias(first, last):
                step(tt(modcol[:, first:last, :], modcol[:, first:last, :],
                        biascol[:, first:last].unsqueeze(2).to_broadcast([P, last - first, 3]), ALU.add))

            add_bias(0, 48)

            def mod(layer, part, cond):
                j = 48 * layer + 8 * part
                return modcol[:, j:j + 8, cond]

            def scales(layer, part, norm, conds):
                for n, c in enumerate(conds):
                    step(ts(scol[:, 2 * n, :], mod(layer, part + 1, c), 1.0, None, ALU.add))
                    gain, bias = (norm or {}).get(n, (None, None))
                    if bias is not None:
                        step(tt(scol[:, 2 * n + 1, :], scol[:, 2 * n, :], bias, ALU.mult))
                        step(tt(scol[:, 2 * n + 1, :], scol[:, 2 * n + 1, :], mod(layer, part, c), ALU.add))
                    else:
                        step(copy(scol[:, 2 * n + 1, :], mod(layer, part, c)))
                    if gain is not None:
                        step(tt(scol[:, 2 * n, :], scol[:, 2 * n, :], gain, ALU.mult))

            def spread_gate(cols, dst):
                diagonals(cols)
                spread(dst)

            def diagonals(cols):
                for k in range(KT):
                    m = ts(diag[:, k, :], ident, cols[:, k:k + 1], None, ALU.mult)
                to_tensor.send(m)

            def spread(dst):
                for c in range(2):
                    b = S.take()
                    S.done(copy(gateb[:, dst, 512 * c:512 * c + 512], b[:, :]))
                S.settle()

            def spread_gates(layer, part, conds):
                for n, c in enumerate(conds):
                    step(copy(gmul[:, n, :], mod(layer, part, c)))
                    spread_gate(gmul[:, n, :], n)

            def variance(tiles, src, center, eps, width=D):
                parts = width // 512
                for t in range(tiles):
                    for c in range(parts):
                        m = dve.bn_stats(stats[:, t, c, :], src(t)[:, 512 * c:512 * c + 512])
                step(m)
                dve.memset(idle[:, 0:1], 0.0)
                for t in range(tiles):
                    m = dve.bn_aggr(mv[:, t, :], stats[:, t, 0:parts, :])
                step(m)
                if not center:
                    for t in range(tiles):
                        m = stt(mv[:, t, 1:2], mv[:, t, 0:1], mv[:, t, 0:1], mv[:, t, 1:2], ALU.mult, ALU.add)
                    step(m)
                ask.send(ts(mv[:, 0:tiles, 1], mv[:, 0:tiles, 1], eps, None, ALU.add))
                from_a.get()
                step(dve.reciprocal(rstd[:, 0:tiles], std[:, 0:tiles]))

            def from_features(tiles, scaled):
                for k in range(KT):
                    b = S.take()
                    if not scaled:
                        m = copy(hT[:, k, 0:tiles * P], b[:, 0:tiles * P])
                    for n in range(tiles // 2 if scaled else 0):
                        m = ts(hT[:, k, SEQ * n:SEQ * (n + 1)], b[:, SEQ * n:SEQ * (n + 1)],
                               scol[:, 2 * n, k:k + 1], scol[:, 2 * n + 1, k:k + 1], ALU.mult, ALU.add)
                    S.done(m)

            def split_features(tiles):
                width = tiles * P
                for k in range(KT):
                    b = S.take()
                    for n in range(tiles // 2):
                        m = ts(mtmp[:, k % 2, SEQ * n:SEQ * (n + 1)], b[:, SEQ * n:SEQ * (n + 1)],
                               scol[:, 2 * n, k:k + 1], scol[:, 2 * n + 1, k:k + 1], ALU.mult, ALU.add)
                    S.done(m)
                    S.settle()
                    step(copy(hT_hi[:, k, 0:width], mtmp[:, k % 2, 0:width]))
                    m = tt(hT_lo[:, k, 0:width], mtmp[:, k % 2, 0:width], hT_hi[:, k, 0:width], ALU.subtract)
                to_tensor.send(m)

            def rms_rows():
                variance(XT, lambda t: tok[:, t, :], False, EPS_RMS)
                for t in range(XT):
                    m = ts(xn[:, t, :], tok[:, t, :], rstd[:, t:t + 1], None, ALU.mult)
                return m

            spread_gates(0, 2, (0,))
            scales(0, 0, {0: (parcol[:, 0:8], None)}, (0,))
            dve.wait_ge(tok_in, 32)
            to_tensor.send(rms_rows())
            from_features(XT, True)

            dve.wait_ge(small_in, 96)
            b = S.take()
            bv = b[:, 0:16].rearrange("p (t n) -> p t n", t=2)
            gr = lambda n: gates[:, n, :]
            g3 = lambda n: gates[:, n, :].rearrange("p (t h) -> p t h", t=2)
            copy(g3(0), bv[:, :, 0:4])
            S.done(tt(g3(1), bv[:, :, 4:8], headp[:, 1, :].unsqueeze(1).to_broadcast([P, 2, 4]), ALU.add))
            S.settle()
            ask.send(copy(gr(2), gr(1)))
            from_a.get()
            step(stt(gr(1), gr(1), 0.0, gr(3), ALU.max, ALU.add))
            to_tensor.send(stt(g3(1), g3(1), -1.0, headp[:, 0, :].unsqueeze(1).to_broadcast([P, 2, 4]),
                               ALU.mult, ALU.mult))
            b = S.take()
            copy(gr(4), b[:, 0:8])
            S.done(copy(gr(6), b[:, 8:16]))
            S.settle()
            ask.send(tt(gr(6), gr(6), gr(4), ALU.subtract))
            from_a.get()
            for n in range(4):
                m = copy(TU[:, n, :], ident)
            step(m)

            def att_scores(i, h):
                b = A.take()
                A.done(stt(satt[:, :], b[:, 0:3 * P], 0.125, lcount, ALU.mult, ALU.add))
                A.settle()
                dve.tensor_reduce(amax[:, 0:1], satt[:, 0:P], AX, ALU.max)
                step(dve.tensor_reduce(amax[:, 1:2], satt[:, P:3 * P], AX, ALU.max))
                ask.send(ts(amax[:, 0:2], amax[:, 0:2], -1.0, None, ALU.mult))

            def att_turn(i, h):
                b = A.take()
                A.done(copy(pT[:, :], b[:, 0:3 * P]))
                step(dve.reciprocal(arec[:, 0:2], aden[:, 0:2]))

            def att_values(i, h):
                b = A.take()
                for t in range(2):
                    m = ts(mix[:, t, bass.ds(i * P + 64 * h, 64)], b[:, 64 * t:64 * t + 64],
                           arec[:, t:t + 1], None, ALU.mult)
                A.done(m)

            beside = {0: [(att_scores, 0)], 1: [(att_turn, 0)], 2: [(att_values, 0), (att_scores, 1)],
                      3: [(att_turn, 1)], 4: [(att_values, 1)]}

            with turns(dve, DN_HEADS, {**per_gemm(10, 8), S.c: 30, A.c: 6, ask.c: 6, from_a.c: 3, to_tensor.c: 9,
                                       step.c: 21}) as i:
                b = G.take()
                G.done(copy(qkT[:, :], b[:, :]))
                b = G.take(True)
                G.done(copy(vtok[:, :, :].rearrange("p a b -> p (a b)"), b[:, 0:SEQ]))
                b = G.take()
                G.done(copy(cin[:, 0:2, 4:260], b[:, :].rearrange("p (a b) -> p a b", a=2)))
                b = G.take(True)
                copy(cin[:, 2, 4:260], b[:, 0:SEQ])
                G.done(copy(dz[:, :, :].rearrange("p a b -> p (a b)"), b[:, SEQ:2 * SEQ]))
                for n in range(7):
                    copy(hsel[:, n, :], g3(n)[:, :, bass.ds(i, 1)].rearrange("p t a -> p (t a)"))
                step(copy(cw[:, :], convcol[:, bass.ds(i, 1), :].rearrange("p a n -> p (a n)")))
                G.settle()
                for p in range(3):
                    m = ts(cy[:, p, :], cin[:, p, 4:260], cw[:, 9 + p:10 + p], None, ALU.mult)
                step(m)
                for j in range(3):
                    for p in range(3):
                        m = stt(cy[:, p, :], cin[:, p, 1 + j:257 + j], cw[:, 3 * j + p:3 * j + p + 1], cy[:, p, :],
                                ALU.mult, ALU.add)
                    if j < 2:
                        step(m)
                ask.send(m)
                for n in range(2):
                    m = ts(gb[:, n, :], ones[:, :], hsel[:, 1, n:n + 1], None, ALU.mult)
                to_tensor.send(m)
                for first, number in ((0, 4), (4, 2)):
                    b = S.take()
                    S.done(copy(qkv[:, first:first + number, :].rearrange("p a b -> p (a b)"), b[:, 0:number * P]))
                S.settle()
                for n in range(4):
                    m = dve.tensor_tensor_reduce(osb[:, n % 2, :], qkv[:, n, :], qkv[:, n, :], 1.0, 0.0,
                                                 ALU.mult, ALU.add, dss[:, n:n + 1])
                    step(m)
                ask.send(ts(dss[:, 0:4], dss[:, 0:4], EPS_RMS, None, ALU.add))
                b = S.take()
                for n in range(2):
                    m = ts(decay[:, n, :], b[:, n * P:n * P + P], hsel[:, 4, n:n + 1], 0.0, ALU.subtract, ALU.min)
                S.done(m)
                S.settle()
                from_a.get()
                ask.send(dve.reciprocal(dss[:, 4:8], dss[:, 4:8]))
                dve.wait_ge(to_act, ask.c.at())
                for n in range(2):
                    ts(qn[:, n, :], qkv[:, n, :], dss[:, 4 + n:5 + n], P ** -0.5, ALU.mult, ALU.mult)
                    ts(kn[:, n, :], qkv[:, 2 + n, :], dss[:, 6 + n:7 + n], None, ALU.mult)
                    m = ts(vb[:, n, :], qkv[:, 4 + n, :], hsel[:, 0, n:n + 1], None, ALU.mult)
                step(m)
                for n in range(2):
                    m = ts(kb[:, n, :], kn[:, n, :], hsel[:, 0, n:n + 1], None, ALU.mult)
                step(m)
                ts(kbg[:, :], kb[:, 1, :], hsel[:, 5, 1:2], None, ALU.mult)
                ts(qd[:, :], qn[:, 1, :], hsel[:, 5, 1:2], None, ALU.mult)
                to_tensor.send(ts(kd[:, :], kn[:, 0, :], hsel[:, 6, 0:1], None, ALU.mult))
                from_a.get()
                step(tt(decay[:, :, :], decay[:, :, :], upper.unsqueeze(1).to_broadcast([P, 2, P]), ALU.mult))
                for first, number in ((0, 4), (4, 3)):
                    b = S.take()
                    S.done(copy(featT[:, first:first + number, :].rearrange("p a b -> p (a b)"), b[:, 0:number * P]))
                b = S.take()
                bb = b[:, :].rearrange("p (a n) -> p a n", a=4)
                tt(LT[:, :, :], bb[:, 0:2, :], decay[:, :, :], ALU.mult)
                S.done(tt(IT[:, :, :], bb[:, 2:4, :], decay[:, :, :], ALU.mult))
                for n in range(4):
                    m = copy(TU[:, n, :], ident)
                step(m)
                S.settle()
                def level_part(l):
                    to_tensor.send(tt(LM[:, :, :], LT[:, :, :], lvl[:, l, :].unsqueeze(1).to_broadcast([P, 2, P]),
                                      ALU.mult))

                level_part(0)
                for l in range(LEVELS):
                    b = S.take()
                    S.done(copy(P1[:, :, :].rearrange("p a b -> p (a b)"), b[:, 0:SEQ]))
                    if l < 6:
                        b = G.take(ends_panel=True)
                        G.done(copy(arow[:, l % 2, :], b[:, 0:P]))
                    if l < LEVELS - 1:
                        level_part(l + 1)
                    for part, h in beside.get(l, ()):
                        part(i, h)
                    b = S.take()
                    S.done(tt(TU[:, :, :].rearrange("p a b -> p (a b)"), TU[:, :, :].rearrange("p a b -> p (a b)"),
                              b[:, :], ALU.subtract))
                    if l < 6:
                        b = S.take()
                        S.done(copy(modcol[:, bass.ds(i * 24 + (48 + 4 * l), 4), :],
                                    b[:, 0:P].rearrange("p (n c) -> p n c", n=4)[:, :, 0:3]))
                    S.settle()
                b = S.take()
                copy(unew[:, :, :].rearrange("p a b -> p (a b)"), b[:, 0:SEQ])
                S.done(copy(wT[:, :], b[:, 2 * P:3 * P]))
                b = S.take()
                copy(osb[:, 0, :], b[:, 0:P])
                S.done(copy(state[:, :], b[:, P:2 * P]))
                b = S.take()
                S.done(tt(unew[:, 1, :], unew[:, 1, :], b[:, 0:P], ALU.subtract))
                b = S.take()
                S.done(copy(osb[:, 1, :], b[:, 0:P]))
                S.settle()
                for n in range(2):
                    step(dve.tensor_tensor_reduce(qn[:, n, :], osb[:, n, :], osb[:, n, :], 1.0, 0.0,
                                                  ALU.mult, ALU.add, dss[:, 8 + n:9 + n]))
                ask.send(ts(dss[:, 8:10], dss[:, 8:10], 1.0 / P, EPS_RMS, ALU.mult, ALU.add))
                from_a.get()
                step(dve.reciprocal(dss[:, 14:16], dss[:, 12:14]))
                for n in range(2):
                    m = stt(osb[:, n, :], osb[:, n, :], dss[:, 14 + n:15 + n], dnw[:, :], ALU.mult, ALU.mult)
                step(m)
                step(tt(mix[:, :, bass.ds(i * P + AT_W, P)], osb[:, :, :], dz[:, :, :], ALU.mult))

            to_tensor.send(dve.memset(idle[:, 2:3], 0.0))
            dve.wait_ge(to_pe, to_tensor.c.at())
            add_bias(48, 144)
            from_features(XT, False)

            def gated_rows(c, t):
                cols = slice(512 * c, 512 * c + 512)
                b = G.take(t == XT - 1)
                G.done(tt(xn[:, t, cols], b[:, :], gateb[:, 0, cols], ALU.mult))
                G.settle()
                step(tt(tok[:, t, cols], tok[:, t, cols], xn[:, t, cols], ALU.add))

            for c in range(2):
                for t in range(XT):
                    gated_rows(c, t)

            scales(0, 3, {0: (parcol[:, 8:16], None)}, (0,))
            to_tensor.send(rms_rows())
            from_features(XT, True)
            b = S.take()
            S.done(tt(lg[:, :, :], b[:, 0:2 * EXPERTS].rearrange("p (t n) -> p t n", t=2),
                      brow[:, :].unsqueeze(1).to_broadcast([P, 2, EXPERTS]), ALU.add))
            S.settle()
            dve.memset(m8[:, :, :], 0.0)
            dve.memset(gate[:, :, EXPERTS:EXPERTS + 1], 0.0)
            step(dve.memset(pos[:, :, EXPERTS:EXPERTS + 1], -1.0))
            for t in range(XT):
                m = dve.max(m8[:, t, :], lg[:, t, :])
            step(m)
            ask.send(ts(rs[:, 0:2], m8[:, :, 0], -1.0, None, ALU.mult))
            fourth = lambda t: m8[:, t, TOP_K - 1:TOP_K]
            for t in range(XT):
                ts(eq[:, t, :], lg[:, t, :], fourth(t), None, ALU.is_equal)
                m = ts(sel[:, t, :], lg[:, t, :], fourth(t), None, ALU.is_gt)
            step(m)
            dve.tensor_reduce(rs[:, 2:4], sel[:, :, :], AX, ALU.add)
            step(copy(cum[:, 0, :, :], eq[:, :, :]))
            for l in range(5):
                s, d, w = cum[:, l % 2, :, :], cum[:, (l + 1) % 2, :, :], 1 << l
                copy(d[:, :, 0:w], s[:, :, 0:w])
                step(tt(d[:, :, w:EXPERTS], s[:, :, w:EXPERTS], s[:, :, 0:EXPERTS - w], ALU.add))
            step(ts(rs[:, 2:4], rs[:, 2:4], -1.0, float(TOP_K), ALU.mult, ALU.add))
            for t in range(XT):
                m = stt(eq[:, t, :], cum[:, 1, t, :], rs[:, 2 + t:3 + t], eq[:, t, :], ALU.is_le, ALU.mult)
            step(m)
            to_tensor.send(tt(sel[:, :, :], sel[:, :, :], eq[:, :, :], ALU.add))
            dve.wait_ge(to_pe, to_tensor.c.at())
            from_a.get()
            step(tt(eg[:, :, :], eg[:, :, :], sel[:, :, :], ALU.mult))
            step(dve.tensor_reduce(rs[:, 4:6], eg[:, :, :], AX, ALU.add))
            step(dve.reciprocal(rs[:, 6:8], rs[:, 4:6]))
            for t in range(XT):
                m = ts(gate[:, t, 0:EXPERTS], eg[:, t, :], rs[:, 6 + t:7 + t], None, ALU.mult)
            step(m)
            b = S.take()
            copy(cntf[:, :], b[:, 2 * EXPERTS:3 * EXPERTS])
            bp = b[:, 0:2 * EXPERTS].rearrange("p (t n) -> p t n", t=2)
            S.done(stt(pos[:, :, 0:EXPERTS], bp, 1.0, sel[:, :, :], ALU.add, ALU.mult))
            S.settle()
            step(ts(pos[:, :, 0:EXPERTS], pos[:, :, 0:EXPERTS], -1.0, None, ALU.add))
            to_tensor.send(ts(gate[:, 0, EXPERTS:EXPERTS + 1], gate[:, 0, EXPERTS:EXPERTS + 1], 0.0, None, ALU.mult))
            dve.memset(rs[:, 9:10], 0.0).then_inc(b2_go, 1)
            dve.memset(idle[:, 3:4], 0.0).then_inc(tiles_free, 1)
            b = S.take()
            S.done(copy(gT[0:EXPERTS, :], b[0:EXPERTS, 0:SEQ]))
            for t in range(XT):
                for c in range(2):
                    b = S.take()
                    S.done(copy(yacc[:, t, 512 * c:512 * c + 512], b[:, :]))
            S.settle()

            for r in range(3):
                m = ts(flags[:, r, :], cntf[:, :], float(CAP * (r + 1)), None, ALU.is_gt)
            step(m)
            flat = flags[:, :, :].rearrange("p a b -> p (a b)")
            step(copy(fcum[:, 0, :], flat))
            n = 3 * EXPERTS
            for l in range(7):
                s, d, w = fcum[:, l % 2, :], fcum[:, (l + 1) % 2, :], 1 << l
                copy(d[:, 0:w], s[:, 0:w])
                step(tt(d[:, w:n], s[:, w:n], s[:, 0:n - w], ALU.add))
            copy(more_i[:, :], fcum[:, 1, n - 1:n])
            over = lambda v: v.unsqueeze(1).to_broadcast([P, LIST, n])
            step(tt(match[:, :, :], over(fcum[:, 1, :]), tab_j.unsqueeze(2).to_broadcast([P, LIST, n]), ALU.is_equal))
            step(tt(match[:, :, :], match[:, :, :], over(flat), ALU.mult))
            step(tt(match2[:, :, :], match[:, :, :], over(tab_e), ALU.mult))
            step(dve.tensor_reduce(rs[:, 0:LIST], match2[:, :, :], AX, ALU.add))
            step(copy(list_e[:, :], rs[:, 0:LIST]))
            step(tt(match2[:, :, :], match[:, :, :], over(tab_s), ALU.mult))
            dve.tensor_reduce(list_s[:, :], match2[:, :, :], AX, ALU.add).then_inc(count_ready, 1)
            dve.wait_ge(count_ready, 1)

            def expert_reader(x, credit):
                return dict(G=GemmReader(dve, x["gemm"], x["done"], credit), S=Reader(dve, x["side"]),
                            A=Reader(dve, x["att"]), M=Reader(dve, x["mix"]), ask=Post(dve, x["to_act"]),
                            from_a=Post(dve, x["from_act"]), to_tensor=Post(dve, x["to_pe"]),
                            step=Chain(dve, x["step"]), freed=Post(dve, x["b1_used"]), uses=Count(),
                            arrived=x["b1"])

            def prepare(r, e, parity, base=None):
                e1 = pos[:, :, bass.ds(e, 1)].rearrange("p t a -> p (t a)")
                if base is None:
                    copy(pg[:, 0, parity, :], e1)
                else:
                    r["step"](copy(pg[:, 1, 1, 0:1], list_s[:, bass.ds(base, 1)]))
                    ts(pg[:, 0, parity, :], e1, pg[:, 1, 1, 0:1], None, ALU.subtract)
                r["step"](copy(pg[:, 1, parity, :], gate[:, :, bass.ds(e, 1)].rearrange("p t a -> p (t a)")))
                for t in range(XT):
                    ts(OH[:, t, :], iota[:, 0:CAP], pg[:, 0, parity, t:t + 1], None, ALU.is_equal)
                    m = ts(GD[:, parity, t, :], iota, pg[:, 0, parity, t:t + 1], pg[:, 1, parity, t:t + 1],
                           ALU.is_equal, ALU.mult)
                r["to_tensor"].send(m)

            def gathered(r):
                b = r["A"].take()
                for k in range(KT):
                    m = ts(xg[:, k, :], b[:, k * CAP:(k + 1) * CAP], scol[:, 0, k:k + 1], scol[:, 1, k:k + 1],
                           ALU.mult, ALU.add)
                r["A"].done(m)

            def expert(r, parity, ahead):
                G, S, A, M, step = r["G"], r["S"], r["A"], r["M"], r["step"]

                def biased(c, n):
                    b = G.take(True)
                    G.done(tt((act_h, up_h)[n][:, c, :], b[:, 0:256], b1b[:, parity, 2 * n + c, :], ALU.add))

                def swiglu(c):
                    G.settle()
                    r["ask"].send(ts(act_h[:, c, :], act_h[:, c, :], 7.0, None, ALU.min))
                    m = ts(up_h[:, c, :], up_h[:, c, :], 7.0, -7.0, ALU.min, ALU.max)
                    if c == 0:
                        step(m)
                    else:
                        r["freed"].send(m)
                        dve.wait_ge(r["freed"].sem, r["freed"].c.at(r.get("b1_credit", 0)))
                    dve.wait_ge(r["ask"].sem, r["ask"].c.at())
                    step(stt(up_h[:, c, :], up_h[:, c, :], 1.0, act_h[:, c, :], ALU.add, ALU.mult))
                    r["from_a"].get()
                    r["to_tensor"].send(tt(act_h[:, c, :], up_h[:, c, :], sig[:, c, :], ALU.mult))

                def turned(c):
                    b = S.take()
                    S.done(copy(aT[:, c, :, :].rearrange("p a b -> p (a b)"), b[:, 0:2 * P]))

                if not ahead:
                    gathered(r)
                buffers = 2 if ahead else 1
                dve.wait_ge(r["arrived"][parity], r["uses"].dma(buffers, 32))
                r["uses"].n += 1
                biased(0, 0)
                biased(0, 1)
                swiglu(0)
                if ahead:
                    prepare(r, ahead[0], 1 - parity)
                biased(1, 0)
                turned(0)
                biased(1, 1)
                swiglu(1)
                if ahead:
                    gathered(r)
                b = A.take()
                A.done(copy(comb[:, :, :].rearrange("p a b -> p (a b)"), b[:, 0:SEQ]))
                turned(1)
                for c in range(2):
                    b = G.take(True)
                    G.done(copy(ysb[:, c, :], b[:, 0:256]))
                for t in range(XT):
                    for s in range(2):
                        b = M.take()
                        y = yacc[:, t, :].rearrange("p (c s n) -> p c s n", c=2, s=2)[:, :, s, :]
                        M.done(tt(y, y, b[:, :].rearrange("p (c n) -> p c n", c=2), ALU.add))

            def counts(r, n, steps):
                return {r["G"].c: 6 * n, r["G"].panels: 6 * n, r["S"].c: 2 * n, r["A"].c: 2 * n, r["M"].c: 4 * n,
                        r["to_tensor"].c: 3 * n, r["ask"].c: 2 * n, r["from_a"].c: 2 * n, r["uses"]: n,
                        r["freed"].c: n, r["step"].c: steps * n}

            for x in ("gemm", "side", "att", "mix"):
                dve.sem_inc(E[x].free, 2)
            spread_gates(0, 5, (0,))
            r = expert_reader(E, 0)
            prepare(r, 0, 0)
            gathered(r)
            b = r["A"].take()
            r["A"].done(copy(comb[:, 0, :], b[:, 0:P]))
            with turns(dve, EXPERTS // 2, counts(r, 2, 4)) as i:
                for e in range(2):
                    expert(r, e, (i * 2 + (e + 1),))
            r["M"].settle()
            dve.wait_ge(count_ready, 1)
            more = dve.value_load(more_i[0:1, 0:1], min_val=0, max_val=LIST - 1)
            with dve.If(more > 0):
                for x in ("gemm", "side", "att", "mix"):
                    dve.sem_inc(O[x].free, 2)
                r = expert_reader(O, 2)
                r["b1_credit"] = 1
                with turns(dve, more, counts(r, 1, 5)) as i:
                    e = dve.value_load(list_e[0:1, bass.ds(i, 1)], min_val=0, max_val=EXPERTS - 1)
                    prepare(r, e, 0, i)
                    expert(r, 0, None)
                r["M"].settle()
                dve.sem_inc(further_done, 1)

            scales(1, 0, {0: (normcol[:, 8, :], None)}, (1, 2))
            for t in range(XT):
                m = tt(yacc[:, t, :], yacc[:, t, :], gateb[:, 0, :], ALU.mult)
            step(m)
            for t in range(XT):
                m = tt(tok[:, t, :], tok[:, t, :], yacc[:, t, :], ALU.add)
            step(m)
            variance(XT, lambda t: tok[:, t, :], False, EPS_RMS)
            for t in range(XT):
                m = ts(tok[:, t, :], tok[:, t, :], rstd[:, t:t + 1], None, ALU.mult)
            to_tensor.send(m)
            dve.wait_ge(to_pe, to_tensor.c.at())

            def gated_sum(b, t, c, n, done):
                s = slice(512 * c, 512 * c + 512)
                done(tt(gtmp[:, n % 2, :], b[:, :], gateb[:, t // 2, s], ALU.mult))
                G.settle()
                step(tt(tok[:, t, s], tok[:, t, s], gtmp[:, n % 2, :], ALU.add))

            def enter(layer, part, conds, number, tiles, split=False):
                if split:
                    split_features(tiles)
                else:
                    from_features(tiles, True)
                    spread_gates(layer, part + 2, conds)
                dve.wait_ge(rows_in, 16 + 32 * number)
                for t in range(tiles):
                    if number:
                        m = stt(tok[:, t, :], tok[:, t, :], ALPHA, lnrow[:, 0, :], ALU.mult, ALU.mult)
                    elif t < XT:
                        m = stt(tok[:, t, :], tok[:, t, :], ALPHA, lnrow[:, 0, :], ALU.mult, ALU.mult)
                    else:
                        m = ts(tok[:, t, :], tok[:, t, :], ALPHA, None, ALU.mult)
                if number:
                    step(m)
                    step(ts(lnrow[:, 1, :], lnrow[:, 1, :], ALPHA, None, ALU.mult))
                    for t in range(tiles):
                        m = tt(tok[:, t, :], tok[:, t, :], lnrow[:, 1, :], ALU.add)
                m.then_inc(rows_used, 1)
                dve.wait_ge(rows_used, number + 1)

            def layer_norm(tiles, layer, part, conds, norm):
                gate = lambda n: gmul[:, n, :]
                for n, c in enumerate(conds):
                    m = copy(gate(n), mod(layer, part + 2, c))
                step(m)
                diagonals(gate(0))
                scales(layer, part, norm, norm_conds(conds, tiles))
                variance(tiles, lambda t: tok[:, t, :], True, EPS_LN)
                spread(0)
                if len(conds) == 2:
                    diagonals(gate(1))
                for t in range(tiles):
                    m = ts(tok[:, t, :], tok[:, t, :], mv[:, t, 0:1], rstd[:, t:t + 1], ALU.subtract, ALU.mult)
                to_tensor.send(m)
                if len(conds) == 2:
                    spread(1)
                dve.wait_ge(to_pe, to_tensor.c.at())

            norm_conds = lambda conds, tiles: conds if tiles == 2 * len(conds) else (1, 2)
            norm_cols = lambda n: {k: (normcol[:, n, :], normcol[:, 4 + n, :]) for k in range(2)}

            enter(1, 0, (1, 2), 0, 4)
            ask.send(copy(lgam[:, :], lgam[:, :]))
            from_a.get()
            step(ts(lgam[:, :], lgam[:, :], -1.0, None, ALU.mult))
            ts(dpos[:, :, :], dist, 0.0, None, ALU.max)
            step(ts(dneg[:, :, :], dist, -1.0, 0.0, ALU.mult, ALU.max))
            with turns(dve, RET_HEADS, {**per_gemm(20, 4), S.c: 6, A.c: 6, M.c: 4, ask.c: 3, from_a.c: 3,
                                        to_tensor.c: 2, step.c: 19}) as i:
                copy(lgs[:, 0:1], lgam[:, bass.ds(i, 1)])
                step(copy(lgs[:, 1:2], lgam[:, bass.ds(i + RET_HEADS, 1)]))
                ts(lgx[:, 0:1], lgs[:, 1:2], -1.0, None, ALU.mult)
                ask.send(ts(lgs[:, 2:4], lgs[:, 0:2], float(SEQ), None, ALU.mult))
                for u in range(4):
                    b = G.take(u == 3)
                    G.done(copy(rqk[:, u, :], b[:, :]))
                G.settle()
                for n in range(2):
                    b = S.take()
                    S.done(tt(ro[:, n, :].rearrange("p (a b) -> p a b", a=2), b[:, :].rearrange("p (a b) -> p a b", a=2),
                              rope[:, :, 1, :], ALU.mult))
                    S.settle()
                    step(tt(rqk[:, 2 * n:2 * n + 2, 0:SEQ], rqk[:, 2 * n:2 * n + 2, 0:SEQ], rope[:, :, 0, :], ALU.mult))
                    m = tt(rqk[:, 2 * n:2 * n + 2, 0:SEQ], rqk[:, 2 * n:2 * n + 2, 0:SEQ],
                           ro[:, n, :].rearrange("p (a b) -> p a b", a=2), ALU.add)
                    step(m)
                from_a.get()
                stt(Wd[:, :, :], dist, 0.0, Wd[:, :, :], ALU.is_ge, ALU.mult)
                step(stt(We[:, :, :], dist, 0.0, We[:, :, :], ALU.is_le, ALU.mult))
                step(tt(Wd[:, :, :], Wd[:, :, :], We[:, :, :], ALU.add))
                to_tensor.send(tt(Wc[:, :, :], Wc[:, :, :], rtmp[:, :, :], ALU.add))
                dve.wait_ge(to_pe, to_tensor.c.at())
                for dst in (rv, rg):
                    for t in range(4):
                        b = G.take(t == 3)
                        m = copy(dst[:, t, :], b[:, :])
                        G.done(m)
                G.settle()
                ask.send(copy(lgs[:, 0:1], lgs[:, 0:1]))
                for n in range(6):
                    b = A.take()
                    w = Wc[:, n - 2, :] if n in (2, 3) else Wd[:, n % 2, :]
                    A.done(stt(rsT[:, n, :], b[:, 0:SEQ], 1.0 / 16, w, ALU.mult, ALU.mult))
                for t in range(4):
                    b = M.take()
                    M.done(copy(ro[:, t, :], b[:, :]))
                M.settle()
                from_a.get()
                variance(4, lambda t: ro[:, t, :], True, EPS_LN, width=512)
                for t in range(4):
                    m = ts(ro[:, t, :], ro[:, t, :], mv[:, t, 0:1], rstd[:, t:t + 1], ALU.subtract, ALU.mult)
                step(m)
                for t in range(4):
                    m = tt(ro[:, t, :], ro[:, t, :], rg[:, t, :], ALU.mult)
                to_tensor.send(m)
                for k in range(4):
                    b = S.take()
                    S.done(copy(roT[:, k, :], b[:, :]))
                for c in range(2):
                    for t in range(4):
                        gated_sum(G.take(c == 1 and t == 3), t, c, t, G.done)

            done_units = Count()

            def mlp(layer, conds, number):
                tiles = 2 * len(conds)
                width = tiles * P

                def take(ends_unit):
                    if ends_unit:
                        dve.wait_ge(unit_done, done_units.at(3))
                        done_units.n += 1
                    else:
                        dve.wait_ge(gemm.full, G.others.at(1))
                        G.others.n += 1
                    return G.pair.banks[G.c.n % 2]

                enter(layer, 3, conds, number, tiles, split=True)
                with turns(dve, 4, {G.c: 8 + 2 * tiles, G.others: 2 * tiles, done_units: 8, step.c: 16 + 2 * tiles,
                                    to_tensor.c: 1}) as i:
                    for u in range(8):
                        b = take(u % 2 == 1)
                        v = mtmp[:, u % 2, 0:width]
                        G.done(ts(v, b[:, 0:width], 0.0, None, ALU.max))
                        G.settle()
                        step(tt(v, v, v, ALU.mult))
                        step(copy(hid_hi[:, u, 0:width], v))
                        m = tt(hid_lo[:, u, 0:width], v, hid_hi[:, u, 0:width], ALU.subtract)
                    to_tensor.send(m)
                    for j in range(4):
                        cols = slice(256 * j, 256 * j + 256)
                        for t in range(0, tiles, 2):
                            b = take(t == tiles - 2)
                            g = gtmp[:, t // 2, :].rearrange("p (t n) -> p t n", t=2)
                            G.done(tt(g, b[:, :].rearrange("p (t n) -> p t n", t=2),
                                      gateb[:, t // 2, cols].unsqueeze(1).to_broadcast([P, 2, 256]), ALU.mult))
                            G.settle()
                            step(tt(tok[:, t:t + 2, cols], tok[:, t:t + 2, cols], g, ALU.add))

            dve.sem_inc(unit_done, 2)
            dve.memset(idle[:, 3:4], 0.0).then_inc(mlp_go, 1)
            layer_norm(4, 1, 3, (1, 2), norm_cols(0))
            mlp(1, (1, 2), 1)

            dve.memset(idle[:, 1:2], 0.0).then_inc(nat_go, 1)
            layer_norm(4, 2, 0, (1,), norm_cols(1))
            from_features(4, True)
            dve.wait_ge(rows_in, 16 + 32 * 2)
            for t in range(XT):
                m = stt(tok[:, t, :], tok[:, t, :], ALPHA, lnrow[:, 0, :], ALU.mult, ALU.mult)
            step(m)
            step(ts(lnrow[:, 1, :], lnrow[:, 1, :], ALPHA, None, ALU.mult))
            for t in range(XT):
                m = tt(tok[:, t, :], tok[:, t, :], lnrow[:, 1, :], ALU.add)
            m.then_inc(rows_used, 1)
            dve.wait_ge(rows_used, 3)
            freed = Post(dve, bias_used)

            def projected(part, p):
                b = G.take(part == 4)
                if part == 0:
                    m = ts(nq[:, p, :], b[:, 0:SEQ], NAT_HD ** -0.5, None, ALU.mult)
                elif part == 2:
                    m = copy(nk[:, p, :], b[:, :])
                else:
                    m = copy(nv[:, p, :, :].rearrange("p a b -> p (a b)"), b[:, :])
                G.done(m)

            def soften(n):
                p = n % 2
                b = A.take()
                A.c.n += 1
                m = dve.tensor_reduce(nmax[:, p:p + 1], b[:, :], AX, ALU.max)
                if n % 2:
                    freed.send(m)
                    dve.wait_ge(bias_used, freed.c.at())
                else:
                    step(m)
                ask.send(ts(nneg[:, p:p + 1], nmax[:, p:p + 1], -1.0, None, ALU.mult))

            def turned(n):
                b = M.take()
                M.done(copy(npT[:, n % 2, :, :].rearrange("p a b -> p (a b)"), b[:, :]))

            def group(i, p, last=False):
                for n in range(8):
                    if n in (1, 3, 5) and not last:
                        projected(n - 1, 1 - p)
                    step(dve.reciprocal(nrec[:, n % 2:n % 2 + 1], nden[:, n % 2:n % 2 + 1]))
                    if n < 6 or not last:
                        soften(n + 2)
                    if n < 7 or not last:
                        turned(n + 1)
                    b = S.take()
                    S.done(ts(no[:, n % 2, bass.ds(i * 256 + (p * P + NAT_HD * (n // 2)), NAT_HD)], b[:, 0:NAT_HD],
                              nrec[:, n % 2:n % 2 + 1], None, ALU.mult))

            for part in (0, 2, 4):
                projected(part, 0)
            soften(0)
            soften(1)
            turned(0)
            with turns(dve, NAT_GROUPS // 2 - 1, {**per_gemm(6, 2), S.c: 16, A.c: 16, M.c: 16, ask.c: 16,
                                                  freed.c: 8, step.c: 24}) as i:
                for p in range(2):
                    group(i, p)
            group(NAT_GROUPS // 2 - 1, 0)
            group(NAT_GROUPS // 2 - 1, 1, last=True)
            S.settle()
            to_tensor.send(dve.memset(idle[:, 2:3], 0.0))
            dve.wait_ge(to_pe, to_tensor.c.at())
            from_features(XT, False)
            for c in range(2):
                for t in range(XT):
                    gated_sum(G.take(t == XT - 1), t, c, t, G.done)
            dve.memset(idle[:, 3:4], 0.0).then_inc(mlp_go, 1)
            layer_norm(2, 2, 3, (1,), norm_cols(2))
            mlp(2, (1,), 3)
            variance(XT, lambda t: tok[:, t, :], True, EPS_LN)
            for t in range(XT):
                m = ts(tok[:, t, :], tok[:, t, :], mv[:, t, 0:1], rstd[:, t:t + 1], ALU.subtract, ALU.mult)
            step(m)
            dve.wait_ge(rows_in, 16 + 32 * 4)
            for n, op in enumerate((ALU.mult, ALU.add)):
                for t in range(XT):
                    m = tt(tok[:, t, :], tok[:, t, :], lnrow[:, n, :], op)
                if n == 0:
                    step(m)
            m.then_inc(out_ready, 1)


def kernel(**inputs):
    import concourse.bacc as _bacc
    from concourse.bass_utils import run_bass_kernel_spmd as _run

    x = {n: np.asarray(v) for n, v in inputs.items()}
    nc = _bacc.Bacc("TRN2", target_bir_lowering=False, num_devices=1)

    def cut(w, c0, width=512, r0=0):
        v = w[r0:r0 + D, c0:c0 + width]
        return v.reshape(KT, P, width).transpose(1, 0, 2).reshape(P, -1)

    def heads(w, firsts, i, width):
        return np.concatenate([w[:, f + i * width:f + (i + 1) * width] for f in firsts], axis=1)

    w_in = x["w_in"][0]
    pa = [cut(x["w_ada"][0], 512 * j) for j in range(12)]
    later = [cut(x["ada_w_2"][l], 512 * j) for l in range(2) for j in range(12)]
    for i in range(DN_HEADS):
        three = heads(w_in, (0, 512, 1024), i, P)
        pa.append(cut(np.concatenate([three, np.zeros_like(three[:, 0:P])], axis=1), 0))
        pa.append(cut(heads(w_in, (1536, 2048, 2560, 3072), i, P), 0))
        pa += later[6 * i:6 * i + 6]
    pa += [cut(x["w_out"][0], 512 * c) for c in range(2)]
    pe = np.empty((EXPERTS, 6, P, KT * 512), np.float32)
    for e in range(EXPERTS):
        for j, c0 in enumerate((0, 1024, 512, 1536)):
            pe[e, j] = cut(x["w1"][0, e], c0)
        for c in range(2):
            pe[e, 4 + c] = cut(x["w2"][0, e], 512 * c)
    pb = []
    rw, ro = x["ret_w_in_2"][0], x["ret_w_o_2"][0]
    for i in range(RET_HEADS):
        pb += [cut(heads(rw, (0, 1024), i, 256), 0), cut(rw, 2048 + 512 * i), cut(rw, 4096 + 512 * i)]
        v = ro[512 * i:512 * i + 512].reshape(4, P, 2, 512)
        pb.append(v.transpose(1, 2, 0, 3).reshape(P, -1))

    def mlp_panels(l):
        r = []
        for i in range(4):
            r += [cut(x["mlp_w1_2"][l], D * i + 256 * j, width=256) for j in range(4)]
            r += [cut(x["mlp_w2_2"][l], 256 * j, width=256, r0=D * i) for j in range(4)]
        return np.stack([np.concatenate(r[n:n + 2], axis=1) for n in range(0, len(r), 2)])

    pn = [cut(heads(x["nat_w_in_2"][0], (0, D, 2 * D), i, P), 0, width=3 * P) for i in range(NAT_GROUPS)]
    pc = [cut(x["nat_w_o_2"][0], 512 * c) for c in range(2)]
    rows = lambda v: v.reshape(-1, P)
    par = np.zeros((4, P, P), np.float32)
    one = np.concatenate([rows(x["c"]), rows(x["c_2"]), rows(x["c_ctx_2"])])
    par[0, 0:24] = one
    par[1, 0:96] = rows(x["ada_b_2"])
    taps = x["conv_w"][0].reshape(4, 3, DN_HEADS, P).transpose(2, 0, 1, 3)
    par[2, 0:112] = np.concatenate([rows(x["b_ada"]), rows(x["norm1_w"]), rows(x["norm2_w"]), rows(taps)])
    par[3, 0:72] = np.concatenate([rows(x["ln_g_2"]), rows(x["ln_b_2"]), rows(x["final_norm_w"])])
    small = np.concatenate([cut(w_in, 3584, width=8), cut(x["w_router"][0], 0, width=EXPERTS)], axis=1)
    rpb = np.zeros((NAT_HEADS, 15, RPB_W), np.float32)
    rpb[:, :, 48:79] = x["nat_rpb_2"][0]

    arrays = {
        "x": x["x"], "ctx_2": x["ctx_2"], "panels_a": np.stack(pa), "panels_e": pe.reshape(-1, P, KT * 512),
        "panels_b": np.stack(pb), "panels_n": np.stack(pn), "panels_c": np.stack(pc), "panels_m0": mlp_panels(0), "panels_m1": mlp_panels(1),
        "consts": constants(), "params": par.reshape(4 * P, P), "smallw": small, "rpb": rpb,
        "A_log": x["A_log"], "dt_bias": x["dt_bias"], "dn_norm_w": x["dn_norm_w"], "b_router": x["b_router"],
        "ret_decay": x["ret_decay_2"].reshape(8), "b1": x["b1"][0], "b2": x["b2"], "final_norm_w": x["final_norm_w"],
        "ln_g_2": x["ln_g_2"], "ln_b_2": x["ln_b_2"],
    }
    arrays = {n: np.ascontiguousarray(v) for n, v in arrays.items()}
    a = {n: nc.dram_tensor("in_" + n, v.shape, mybir.dt.from_np(v.dtype), kind="ExternalInput").ap()
         for n, v in arrays.items()}
    out = nc.dram_tensor("out_0", (1, SEQ, D), F32, kind="ExternalOutput").ap()
    program(nc, a, out)
    r = _run(nc, [{"in_" + n: v for n, v in arrays.items()}], core_ids=[0])
    return r.results[0]["out_0"]
```
